# Optimizing a Trainium2 kernel written in Bass

```python
import jax, jax.numpy as jnp
from jax import lax
import numpy as np
import math

D_MODEL = 1024
BATCH = 1
SEQ = 512
DEPTH = 1

CHUNK = 64
Q_BLOCK = 128
MLA_HEADS = 8
MLA_NOPE = 64
MLA_ROPE = 32
MLA_QK = MLA_NOPE + MLA_ROPE
MLA_V = 64
Q_LORA = 256
KV_LORA = 128
ROPE_BASE = 10000.0
CA_HEADS = 8
CA_HEAD_DIM = 64
LEFT_CHUNKS = 8
BAND = (LEFT_CHUNKS + 1) * CHUNK
MAX_REL = 256
MLA_WIDTH = MLA_HEADS * MLA_V
CA_WIDTH = CA_HEADS * CA_HEAD_DIM
IN_WIDTHS = (Q_LORA, KV_LORA, MLA_ROPE, CA_WIDTH, CA_WIDTH, CA_WIDTH, D_MODEL, D_MODEL)
IN_WIDTH = Q_LORA + KV_LORA + MLA_ROPE + 3 * CA_WIDTH + 2 * D_MODEL
N_GROUPS = 4
EXPERTS_PER_GROUP = 8
N_EXPERTS = N_GROUPS * EXPERTS_PER_GROUP
TOP_K = 2
EXPERT_FF = 256
NORM_EPS = 1e-6
NEG_INF = -1e30
N_MOD = 6


def rms_norm(x, g):
    xf = x.astype(jnp.float32)
    y = xf * lax.rsqrt(jnp.mean(xf * xf, axis=-1, keepdims=True) + NORM_EPS)
    return (y * g.astype(jnp.float32)).astype(x.dtype)

def modulate(x, shift, scale):
    return x * (1 + scale[:, None, :]) + shift[:, None, :]

def rope(x, positions):
    half = x.shape[-1] // 2
    inv = ROPE_BASE ** (-jnp.arange(half, dtype=jnp.float32) / half)
    ang = positions.astype(jnp.float32)[..., None] * inv
    ang = ang.reshape(ang.shape[:2] + (1,) * (x.ndim - 3) + (half,))
    cos = jnp.cos(ang).astype(x.dtype)
    sin = jnp.sin(ang).astype(x.dtype)
    x1, x2 = x[..., :half], x[..., half:]
    return jnp.concatenate([x1 * cos - x2 * sin, x2 * cos + x1 * sin], axis=-1)

def mla_attend(q, k, v):
    b, s, h, _ = q.shape
    n_blocks = s // Q_BLOCK
    scale = MLA_QK ** -0.5
    key_chunk = jnp.arange(s) // CHUNK

    def one_block(i):
        qb = lax.dynamic_slice_in_dim(q, i * Q_BLOCK, Q_BLOCK, axis=1)
        sc = jnp.einsum('bqhd,bkhd->bhqk', qb, k).astype(jnp.float32) * scale
        q_chunk = (i * Q_BLOCK + jnp.arange(Q_BLOCK)) // CHUNK
        mask = key_chunk[None, :] <= q_chunk[:, None]
        sc = jnp.where(mask[None, None], sc, NEG_INF)
        p = jax.nn.softmax(sc, axis=-1).astype(v.dtype)
        return jnp.einsum('bhqk,bkhd->bqhd', p, v)

    out = lax.map(one_block, jnp.arange(n_blocks))
    return out.transpose(1, 0, 2, 3, 4).reshape(b, s, h * v.shape[-1])

def chunk_band_attend(q, k, v, rel_table):
    b, s, h, d = q.shape
    n_chunks = s // CHUNK
    scale = d ** -0.5
    pad = ((0, 0), (LEFT_CHUNKS * CHUNK, 0), (0, 0), (0, 0))
    kp = jnp.pad(k, pad)
    vp = jnp.pad(v, pad)
    rel = (jnp.arange(CHUNK)[:, None] + LEFT_CHUNKS * CHUNK) - jnp.arange(BAND)[None, :]
    idx = jnp.clip(rel, -MAX_REL, MAX_REL) + MAX_REL
    bias = rel_table.astype(jnp.float32)[:, idx]

    def one_chunk(n):
        qc = lax.dynamic_slice_in_dim(q, n * CHUNK, CHUNK, axis=1)
        kb = lax.dynamic_slice_in_dim(kp, n * CHUNK, BAND, axis=1)
        vb = lax.dynamic_slice_in_dim(vp, n * CHUNK, BAND, axis=1)
        sc = jnp.einsum('bqhd,bkhd->bhqk', qc, kb).astype(jnp.float32) * scale + bias[None]
        valid = (n * CHUNK - LEFT_CHUNKS * CHUNK + jnp.arange(BAND)) >= 0
        sc = jnp.where(valid[None, None, None, :], sc, NEG_INF)
        p = jax.nn.softmax(sc, axis=-1).astype(vb.dtype)
        return jnp.einsum('bhqk,bkhd->bqhd', p, vb)

    out = lax.map(one_chunk, jnp.arange(n_chunks))
    return out.transpose(1, 0, 2, 3, 4).reshape(b, s, h * d)

def hybrid_mixer(h, positions, w_in, g_q, w_uq, g_kv, w_uk, w_uv, rel_table, w_oa, w_ob, w_out):
    b, s, _ = h.shape
    proj = h @ w_in
    cuts = [int(v) for v in np.cumsum(IN_WIDTHS)[:-1]]
    q_lat, kv_lat, k_rope, q_b, k_b, v_b, gate_a, gate_b = jnp.split(proj, cuts, axis=-1)
    q_a = (rms_norm(q_lat, g_q) @ w_uq).reshape(b, s, MLA_HEADS, MLA_QK)
    q_a = jnp.concatenate([q_a[..., :MLA_NOPE], rope(q_a[..., MLA_NOPE:], positions)], axis=-1)
    kv_n = rms_norm(kv_lat, g_kv)
    k_nope = (kv_n @ w_uk).reshape(b, s, MLA_HEADS, MLA_NOPE)
    v_a = (kv_n @ w_uv).reshape(b, s, MLA_HEADS, MLA_V)
    k_r = rope(k_rope, positions)
    k_a = jnp.concatenate(
        [k_nope, jnp.broadcast_to(k_r[:, :, None, :], (b, s, MLA_HEADS, MLA_ROPE))], axis=-1)
    o_a = mla_attend(q_a, k_a, v_a)
    o_b = chunk_band_attend(
        q_b.reshape(b, s, CA_HEADS, CA_HEAD_DIM),
        k_b.reshape(b, s, CA_HEADS, CA_HEAD_DIM),
        v_b.reshape(b, s, CA_HEADS, CA_HEAD_DIM), rel_table)
    merged = jax.nn.sigmoid(gate_a) * (o_a @ w_oa) + jax.nn.sigmoid(gate_b) * (o_b @ w_ob)
    return merged @ w_out

def hierarchical_moe(h, w_rg, b_rg, w_re, b_re, w_gate, w_up, w_down):
    b, s, d = h.shape
    t = h.reshape(b * s, d)
    n_tok = t.shape[0]
    g_prob = jax.nn.softmax((t @ w_rg + b_rg).astype(jnp.float32), axis=-1)
    g_w, g_idx = lax.top_k(g_prob, 1)
    g_w, g_idx = g_w[:, 0], g_idx[:, 0]
    e_logits = (t @ w_re + b_re).astype(jnp.float32).reshape(n_tok, N_GROUPS, EXPERTS_PER_GROUP)
    e_sel = jnp.take_along_axis(e_logits, g_idx[:, None, None], axis=1)[:, 0]
    e_prob = jax.nn.softmax(e_sel, axis=-1)
    top_w, top_i = lax.top_k(e_prob, TOP_K)
    top_w = top_w / jnp.sum(top_w, axis=-1, keepdims=True)
    in_group = jnp.sum(jax.nn.one_hot(top_i, EXPERTS_PER_GROUP, dtype=jnp.float32) * top_w[..., None], axis=1)
    combine = (jax.nn.one_hot(g_idx, N_GROUPS, dtype=jnp.float32)[:, :, None]
               * in_group[:, None, :] * g_w[:, None, None]).astype(h.dtype)
    y = jnp.zeros_like(t)
    for g in range(N_GROUPS):
        sl = slice(g * EXPERTS_PER_GROUP, (g + 1) * EXPERTS_PER_GROUP)
        a = jnp.einsum('td,edf->tef', t, w_gate[sl])
        u = jnp.einsum('td,edf->tef', t, w_up[sl])
        hid = jax.nn.silu(a) * u * combine[:, g, :, None]
        y = y + jnp.einsum('tef,efd->td', hid, w_down[sl])
    return y.reshape(b, s, d)

def first_inputs(seed: int = 0) -> dict:
    key = jax.random.key(seed)
    ks = iter(jax.random.split(key, 32))
    L, D = DEPTH, D_MODEL

    def w(shape, fan_in):
        return jax.random.normal(next(ks), shape, jnp.float32) * (fan_in ** -0.5)

    def gain(shape):
        return 1.0 + 0.02 * jax.random.normal(next(ks), shape, jnp.float32)

    def small(shape, s=0.01):
        return s * jax.random.normal(next(ks), shape, jnp.float32)

    x = jax.random.normal(next(ks), (BATCH, SEQ, D), jnp.float32)
    c = jax.random.normal(next(ks), (BATCH, D), jnp.float32)
    offsets = jax.random.randint(next(ks), (BATCH, 1), 0, 10000, dtype=jnp.int32)
    positions = offsets + jnp.arange(SEQ, dtype=jnp.int32)[None, :]
    return {
        'x': x,
        'c': c,
        'positions': positions,
        'w_ada': w((L, D, N_MOD * D), D),
        'b_ada': small((L, N_MOD * D), 0.02),
        'g_mix': gain((L, D)),
        'w_in': w((L, D, IN_WIDTH), D),
        'g_q': gain((L, Q_LORA)),
        'w_uq': w((L, Q_LORA, MLA_HEADS * MLA_QK), Q_LORA),
        'g_kv': gain((L, KV_LORA)),
        'w_uk': w((L, KV_LORA, MLA_HEADS * MLA_NOPE), KV_LORA),
        'w_uv': w((L, KV_LORA, MLA_WIDTH), KV_LORA),
        'rel_bias': small((L, CA_HEADS, 2 * MAX_REL + 1), 0.5),
        'w_oa': w((L, MLA_WIDTH, D), MLA_WIDTH),
        'w_ob': w((L, CA_WIDTH, D), CA_WIDTH),
        'w_out': w((L, D, D), D),
        'g_ffn': gain((L, D)),
        'w_rg': w((L, D, N_GROUPS), D),
        'b_rg': small((L, N_GROUPS)),
        'w_re': w((L, D, N_EXPERTS), D),
        'b_re': small((L, N_EXPERTS)),
        'w_gate': w((L, N_EXPERTS, D, EXPERT_FF), D),
        'w_up': w((L, N_EXPERTS, D, EXPERT_FF), D),
        'w_down': w((L, N_EXPERTS, EXPERT_FF, D), EXPERT_FF),
        'g_final': gain((D,)),
    }

def first_block(x, c, positions, w_ada, b_ada, g_mix, w_in, g_q, w_uq, g_kv, w_uk, w_uv,
              rel_bias, w_oa, w_ob, w_out, g_ffn, w_rg, b_rg, w_re, b_re,
              w_gate, w_up, w_down, g_final):
    c_act = jax.nn.silu(c)
    for l in range(DEPTH):
        mod = c_act @ w_ada[l] + b_ada[l]
        sh1, sc1, gt1, sh2, sc2, gt2 = jnp.split(mod, N_MOD, axis=-1)
        h = modulate(rms_norm(x, g_mix[l]), sh1, sc1)
        mix = hybrid_mixer(h, positions, w_in[l], g_q[l], w_uq[l], g_kv[l], w_uk[l], w_uv[l],
                           rel_bias[l], w_oa[l], w_ob[l], w_out[l])
        x = x + gt1[:, None, :] * mix
        h = modulate(rms_norm(x, g_ffn[l]), sh2, sc2)
        ffn = hierarchical_moe(h, w_rg[l], b_rg[l], w_re[l], b_re[l], w_gate[l], w_up[l], w_down[l])
        x = x + gt2[:, None, :] * ffn
    return rms_norm(x, g_final)


D_MIX = 2 * D_MODEL
D_ATT = D_MIX // 2
ATT_HEAD_DIM = 64
ATT_HEADS = D_ATT // ATT_HEAD_DIM
ATT_STEPS = 128
DILATIONS = (1, 4, 16)
D_SSM = D_MIX - D_ATT
SSM_HEAD_DIM = 64
SSM_HEADS = D_SSM // SSM_HEAD_DIM
SSM_GROUPS = 2
SSM_STATE = 128
CONV_WIDTH = 4
CHUNK_2 = 128
D_CONV = D_SSM + 2 * SSM_GROUPS * SSM_STATE
D_IN_PROJ = 4 * D_ATT + D_SSM + D_CONV + SSM_HEADS
SPLITS = (D_ATT, 2 * D_ATT, 3 * D_ATT, 4 * D_ATT, 4 * D_ATT + D_SSM, 4 * D_ATT + D_SSM + D_CONV)
NORM_EPS_2 = 1e-5


def rms_norm_2(u, g):
    uf = u.astype(jnp.float32)
    uf = uf * lax.rsqrt(jnp.mean(uf * uf, axis=-1, keepdims=True) + NORM_EPS_2)
    return (uf * g.astype(jnp.float32)).astype(u.dtype)

def layer_norm(u, g, b):
    uf = u.astype(jnp.float32)
    mu = jnp.mean(uf, axis=-1, keepdims=True)
    var = jnp.mean(jnp.square(uf - mu), axis=-1, keepdims=True)
    out = (uf - mu) * lax.rsqrt(var + NORM_EPS_2) * g.astype(jnp.float32) + b.astype(jnp.float32)
    return out.astype(u.dtype)

def alibi_slopes(n_heads):
    return jnp.asarray(2.0 ** (-8.0 * np.arange(1, n_heads + 1) / n_heads), dtype=jnp.float32)

def dilated_window_attention(q, k, v, slopes, dilation):
    B, S, H, E = q.shape
    unit = dilation * ATT_STEPS
    s_pad = -(-S // unit) * unit
    nb = s_pad // unit
    pad = ((0, 0), (0, s_pad - S), (0, 0), (0, 0))

    def to_blocks(t):
        return jnp.pad(t, pad).reshape(B, nb, ATT_STEPS, dilation, H, E)

    def with_prev(t):
        prev = jnp.pad(t, ((0, 0), (1, 0), (0, 0), (0, 0), (0, 0), (0, 0)))[:, :-1]
        return jnp.concatenate([prev, t], axis=2)

    qb = to_blocks(q)
    kk = with_prev(to_blocks(k))
    vv = with_prev(to_blocks(v))
    scores = jnp.einsum('bnqrhe,bnkrhe->bnrhqk', qb, kk).astype(jnp.float32)

    n_idx = jnp.arange(nb)[:, None, None]
    jq = n_idx * ATT_STEPS + jnp.arange(ATT_STEPS)[None, :, None]
    jk = (n_idx - 1) * ATT_STEPS + jnp.arange(2 * ATT_STEPS)[None, None, :]
    steps = jq - jk
    valid = (jk >= 0) & (steps >= 0) & (steps <= ATT_STEPS)
    dist = (steps * dilation).astype(jnp.float32)
    bias = -slopes[None, None, :, None, None] * dist[:, None, None, :, :]
    scores = jnp.where(valid[:, None, None], scores + bias, -jnp.inf)

    lse = jax.nn.logsumexp(scores, axis=-1)
    p = jnp.exp(scores - lse[..., None]).astype(vv.dtype)
    o = jnp.einsum('bnrhqk,bnkrhe->bnqrhe', p, vv)
    o = o.reshape(B, s_pad, H, E)[:, :S]
    lse = lse.transpose(0, 1, 4, 2, 3).reshape(B, s_pad, H)[:, :S]
    return o, lse

def causal_depthwise_conv(u, w, bias):
    out = lax.conv_general_dilated(
        u, w[:, None, :].astype(u.dtype), window_strides=(1,), padding=((CONV_WIDTH - 1, 0),),
        dimension_numbers=('NWC', 'WIO', 'NWC'), feature_group_count=u.shape[-1])
    return out + bias.astype(u.dtype)

def segsum(a):
    cs = jnp.cumsum(a, axis=-1)
    l = a.shape[-1]
    diff = cs[..., :, None] - cs[..., None, :]
    mask = jnp.tril(jnp.ones((l, l), dtype=bool))
    return jnp.where(mask, diff, -jnp.inf)

def ssd_chunked(x, dt, a, b, c):
    Bsz, S, H, P = x.shape
    G, N = b.shape[2], b.shape[3]
    J = H // G
    nc = S // CHUNK_2
    xg = (x * dt[..., None]).reshape(Bsz, nc, CHUNK_2, G, J, P)
    adt = (dt * a).reshape(Bsz, nc, CHUNK_2, G, J).transpose(0, 1, 3, 4, 2)
    bc = b.reshape(Bsz, nc, CHUNK_2, G, N)
    cc = c.reshape(Bsz, nc, CHUNK_2, G, N)
    a_cs = jnp.cumsum(adt, axis=-1)

    decay = jnp.exp(segsum(adt))
    cb = jnp.einsum('bclgn,bcsgn->bcgls', cc, bc)
    y_diag = jnp.einsum('bcgjls,bcsgjp->bclgjp', cb[:, :, :, None] * decay, xg)

    decay_to_end = jnp.exp(a_cs[..., -1:] - a_cs).transpose(0, 1, 4, 2, 3)[..., None]
    states = jnp.einsum('bcsgn,bcsgjp->bcgjpn', bc, xg * decay_to_end)

    chunk_decay = jnp.exp(a_cs[..., -1])

    def step(h, inp):
        st, dec = inp
        return h * dec[..., None, None] + st, h

    h0 = jnp.zeros((Bsz, G, J, P, N), dtype=jnp.float32)
    _, prev = lax.scan(step, h0, (jnp.moveaxis(states, 1, 0), jnp.moveaxis(chunk_decay, 1, 0)))
    prev = jnp.moveaxis(prev, 0, 1)

    state_decay = jnp.exp(a_cs).transpose(0, 1, 4, 2, 3)[..., None]
    y_off = jnp.einsum('bclgn,bcgjpn->bclgjp', cc, prev) * state_decay
    return (y_diag + y_off).reshape(Bsz, S, H, P)

def second_inputs(seed: int = 0) -> dict:
    key = jax.random.key(seed)
    ks = jax.random.split(key, 14)
    beta = (8.0 * DEPTH) ** -0.25
    f32 = jnp.float32
    x = jax.random.normal(ks[0], (BATCH, SEQ, D_MODEL), f32)
    col_scale = np.ones((D_IN_PROJ,), np.float32)
    col_scale[2 * D_ATT:3 * D_ATT] = beta
    col_scale[4 * D_ATT + D_SSM:4 * D_ATT + 2 * D_SSM] = beta
    w_in = jax.random.normal(ks[1], (DEPTH, D_MODEL, D_IN_PROJ), f32) * (D_MODEL ** -0.5) * jnp.asarray(col_scale)
    conv_w = jax.random.normal(ks[2], (DEPTH, CONV_WIDTH, D_CONV), f32) * (CONV_WIDTH ** -0.5)
    conv_b = 0.02 * jax.random.normal(ks[3], (DEPTH, D_CONV), f32)
    dt0 = jnp.exp(jax.random.uniform(ks[4], (DEPTH, SSM_HEADS), f32, math.log(1e-3), math.log(1e-1)))
    dt_bias = dt0 + jnp.log(-jnp.expm1(-dt0))
    a_log = jnp.log(jax.random.uniform(ks[5], (DEPTH, SSM_HEADS), f32, 1.0, 16.0))
    d_skip = 1.0 + 0.1 * jax.random.normal(ks[6], (DEPTH, SSM_HEADS), f32)
    att_norm_g = 1.0 + 0.1 * jax.random.normal(ks[7], (DEPTH, D_ATT), f32)
    ssm_norm_g = 1.0 + 0.1 * jax.random.normal(ks[8], (DEPTH, D_SSM), f32)
    w_out = jax.random.normal(ks[9], (DEPTH, D_MIX, D_MODEL), f32) * (D_MIX ** -0.5) * beta
    ln_g = 1.0 + 0.1 * jax.random.normal(ks[10], (DEPTH, D_MODEL), f32)
    ln_b = 0.02 * jax.random.normal(ks[11], (DEPTH, D_MODEL), f32)
    return {'x': x, 'w_in': w_in, 'conv_w': conv_w, 'conv_b': conv_b, 'dt_bias': dt_bias,
            'a_log': a_log, 'd_skip': d_skip, 'att_norm_g': att_norm_g, 'ssm_norm_g': ssm_norm_g,
            'w_out': w_out, 'ln_g': ln_g, 'ln_b': ln_b}

def second_block(x, w_in, conv_w, conv_b, dt_bias, a_log, d_skip, att_norm_g, ssm_norm_g, w_out, ln_g, ln_b):
    alpha = (2.0 * DEPTH) ** 0.25
    slopes = alibi_slopes(ATT_HEADS)
    Bsz, S, _ = x.shape
    for layer in range(DEPTH):
        proj = jnp.einsum('bsd,de->bse', x, w_in[layer])
        q, k, v, z_att, z_ssm, xbc, dt_raw = jnp.split(proj, list(SPLITS), axis=-1)

        q = q.reshape(Bsz, S, ATT_HEADS, ATT_HEAD_DIM) * (ATT_HEAD_DIM ** -0.5)
        k = k.reshape(Bsz, S, ATT_HEADS, ATT_HEAD_DIM)
        v = v.reshape(Bsz, S, ATT_HEADS, ATT_HEAD_DIM)
        o1, l1 = dilated_window_attention(q, k, v, slopes, DILATIONS[0])
        o2, l2 = dilated_window_attention(q, k, v, slopes, DILATIONS[1])
        o3, l3 = dilated_window_attention(q, k, v, slopes, DILATIONS[2])
        wts = jax.nn.softmax(jnp.stack([l1, l2, l3], axis=0), axis=0)
        y_att = (wts[0][..., None] * o1 + wts[1][..., None] * o2 + wts[2][..., None] * o3).astype(x.dtype)
        y_att = rms_norm_2(y_att.reshape(Bsz, S, D_ATT) * jax.nn.silu(z_att), att_norm_g[layer])

        xbc = jax.nn.silu(causal_depthwise_conv(xbc, conv_w[layer], conv_b[layer]))
        xs, bm, cm = jnp.split(xbc, [D_SSM, D_SSM + SSM_GROUPS * SSM_STATE], axis=-1)
        dt = jax.nn.softplus(dt_raw.astype(jnp.float32) + dt_bias[layer].astype(jnp.float32))
        a = -jnp.exp(a_log[layer].astype(jnp.float32))
        xs_h = xs.reshape(Bsz, S, SSM_HEADS, SSM_HEAD_DIM).astype(jnp.float32)
        y = ssd_chunked(xs_h, dt, a,
                        bm.reshape(Bsz, S, SSM_GROUPS, SSM_STATE).astype(jnp.float32),
                        cm.reshape(Bsz, S, SSM_GROUPS, SSM_STATE).astype(jnp.float32))
        y = y + d_skip[layer].astype(jnp.float32)[:, None] * xs_h
        y_ssm = rms_norm_2(y.reshape(Bsz, S, D_SSM).astype(x.dtype) * jax.nn.silu(z_ssm), ssm_norm_g[layer])

        mix = jnp.concatenate([y_att, y_ssm], axis=-1)
        out = jnp.einsum('bse,ed->bsd', mix, w_out[layer])
        x = layer_norm(alpha * x + out, ln_g[layer], ln_b[layer])
    return x


def setup_inputs(seed=0):
    out = dict(first_inputs(seed))
    for name, value in second_inputs(seed + 1).items():
        if name != "x":
            out[name + "_2"] = value
    return out


def reference(
    x, c, positions, w_ada, b_ada, g_mix, w_in, g_q, w_uq, g_kv, w_uk, w_uv, rel_bias, w_oa,
    w_ob, w_out, g_ffn, w_rg, b_rg, w_re, b_re, w_gate, w_up, w_down, g_final, w_in_2, conv_w_2,
    conv_b_2, dt_bias_2, a_log_2, d_skip_2, att_norm_g_2, ssm_norm_g_2, w_out_2, ln_g_2, ln_b_2,
):
    x = first_block(
        x, c, positions, w_ada, b_ada, g_mix, w_in, g_q, w_uq, g_kv, w_uk, w_uv, rel_bias, w_oa,
        w_ob, w_out, g_ffn, w_rg, b_rg, w_re, b_re, w_gate, w_up, w_down, g_final,
    )
    return second_block(
        x, w_in_2, conv_w_2, conv_b_2, dt_bias_2, a_log_2, d_skip_2, att_norm_g_2, ssm_norm_g_2,
        w_out_2, ln_g_2, ln_b_2,
    )


_drawn_inputs = setup_inputs


def setup_inputs(seed=0):
    import zlib

    import numpy as np

    out = dict(_drawn_inputs(seed))
    spreads = {}
    factors = {'g_mix': 3.245,
     'g_q': 8.0,
     'g_kv': 3.425,
     'b_re': 11.138,
     'conv_b_2': 3.549,
     'ln_b_2': 2.675,
     'b_rg': 5.2,
     'g_ffn': 2.872}
    for name, (base, spread) in spreads.items():
        noise = np.random.default_rng([zlib.crc32(name.encode()), seed]).standard_normal(out[name].shape)
        drawn = base * np.exp(spread * noise) if base else spread * noise
        out[name] = __import__('jax').numpy.asarray(drawn.astype(out[name].dtype))
    for name, factor in factors.items():
        out[name] = (out[name] * factor).astype(out[name].dtype)
    return out
```

```python
from contextlib import ExitStack

import numpy as np

import concourse.bass as bass
from concourse import mybir

F32 = mybir.dt.float32
I32 = mybir.dt.int32
ALU = mybir.AluOpType
ACT = mybir.ActivationFunctionType
AX_X = mybir.AxisListType.X

P = 128
T = 512
TT = T // P
D = 1024
KT = D // P
RING = 12
HG = 8
EPS1, EPS2 = 1e-6, 1e-5
NEG = -1e30
MLA_SCALE = 96 ** -0.5
N_EXP, QUAD, SLOTS = 32, 4, 64
MAXPASS = T // SLOTS
ALPHA = 2.0 ** 0.25
SSM_H, SSM_P = 16, 64

N_PRE = 16 + 48 + 3 + 24 + 8
QUAD_TILES = 24
N_QUADS = N_EXP // QUAD
N_POST = 8 * 3 + 12 + 8 + 8 + 16
GU_AT = [0, 4, 10, 16]
DN_AT = [8, 14, 20, 22]
GU_END = [a + 4 for a in GU_AT]
DN_END = [a + 2 for a in DN_AT]

V_NAMES = [("c", 8), ("b_ada", 48), ("g_mix", 8), ("g_ffn", 8), ("g_final", 8), ("g_q", 2), ("g_kv", 1),
           ("conv_w", 48), ("conv_b", 12), ("att_g", 8), ("ssm_g", 8), ("ln_g", 8), ("ln_b", 8),
           ("inv", 1), ("sign", 1)]
V_AT, _n = {}, 0
for _name, _k in V_NAMES:
    V_AT[_name] = _n
    _n += _k
NV = _n
R_BR, R_DTB, R_ALOG, R_DSKIP, NR = 0, 36, 52, 68, 84
TWO_PI = 2 * np.pi
C1 = 6.28125
C2 = float(np.float32(np.float32((TWO_PI - C1) * 2 ** 22).astype(np.int64) // 4096 * 4096) / 2 ** 22)
C3 = float(TWO_PI - C1 - C2)
ROUND = 12582912.0


def build(nc, xT_d, vec_d, rows_d, pos_d, rel_d, wr_d, wdt_d, pre_d, moe_d, post_d, out_d):
    ctx = ExitStack()
    with ctx:
        def sb(name, shape, dt=F32):
            return ctx.enter_context(nc.sbuf_tensor(name, shape, dt))

        def sem(name):
            return ctx.enter_context(nc.semaphore(name))

        ring = sb("ring", [P, RING, D])
        RA = sb("RA", [P, KT, T])
        RB = sb("RB", [P, KT, T])
        RC = sb("RC", [P, KT, T])
        RD = sb("RD", [P, KT, T])
        RE = sb("RE", [P, KT, T])
        RF = sb("RF", [P, KT, T])
        RG = sb("RG", [P, KT, T])
        RH = sb("RH", [P, KT, T])
        SB = sb("SB", [P, 2, T])
        PB = sb("PB", [P, 2, T])
        PTB = sb("PTB", [P, 2, T])
        OTK = sb("OTK", [P, 2, T])
        SQ = sb("SQ", [P, 2, T])
        RINV = sb("RINV", [P, T])
        MASK = sb("MASK", [P, T])
        ident = sb("ident", [P, P])
        ones = sb("ones", [P, P])
        upper = sb("upper", [P, P])
        flip = sb("flip", [P, P])
        vec = sb("vec", [P, NV])
        rows = sb("rows", [P, NR])
        small = sb("small", [P, 256])
        w_r = sb("w_r", [P, KT, 36])
        wdt = sb("wdt", [P, KT, 16])
        iota64 = sb("iota64", [P, SLOTS])
        npi = sb("npi", [1, 1], I32)
        ps = [ctx.enter_context(nc.psum_tensor(f"ps{i}", [P, T], F32)) for i in range(8)]
        ext_d = nc.dram_tensor("ext_scratch", [HG, 640], F32, kind="Internal").ap()

        cact = small[:, 0:8]
        mod = small[:, 8:56]
        A1 = small[:, 56:64]
        A2 = small[:, 64:72]
        gt1h = small[:, 72:80]
        rowsum = small[:, 80:96]
        rsinv = small[:, 96:112]
        eps1 = small[:, 112:113]
        eps2 = small[:, 113:114]
        cnt = small[:, 114:118]
        aneg = small[:, 120:136]


        def nmax(n):
            return small[:, 140 + n % 4:141 + n % 4]

        def zbuf(i):
            return (SB, PB)[i % 4 // 2][:, i % 2, :]

        ext_row = PTB[0:HG, :, :].rearrange("p a b -> p (a b)")[:, 0:640]
        cosT, sinT = PB[:, 0, :], PB[:, 1, :]
        qlT, kvT, krT = RH[:, 0:2, :], RH[:, 2, :], RH[:, 3, :]
        qnT, kvnT = RH[:, 4:6, :], RH[:, 6, :]
        qbT, kbT = RC[:, 0:4, :], RC[:, 4:8, :]
        vb, va = RF[:, 0:4, :], RF[:, 4:8, :]
        oaT, obT = RH[:, 0:4, :], RH[:, 4:8, :]
        RCf = RC[:, :, :].rearrange("p a b -> p (a b)")
        REf = RE[:, :, :].rearrange("p a b -> p (a b)")
        RFf = RF[:, :, :].rearrange("p a b -> p (a b)")
        RDf = RD[:, :, :].rearrange("p a b -> p (a b)")
        RHf = RH[:, :, :].rearrange("p a b -> p (a b)")
        RGf = RG[:, :, :].rearrange("p a b -> p (a b)")
        h2tok = RCf.rearrange("p (t d) -> p t d", t=TT)
        posm = RFf[:, 0:1024 + 2 * TT]
        combr = RFf[:, 1024:2048]
        Zs = RFf[:, 2048:4096].rearrange("p (a d) -> p a d", a=2)
        OH = REf[:, 0:512].rearrange("p (a t s) -> p a t s", a=2, t=TT)
        OHW = REf[:, 512:1536].rearrange("p (a t s) -> p a t s", a=2, t=TT)
        Xg = REf[:, 1536:2560].rearrange("p (a k s) -> p a k s", a=2, k=KT)
        hid = REf[:, 2560:2816].rearrange("p (a f s) -> p a f s", a=2, f=2)
        sg = REf[:, 2816:3072].rearrange("p (a x) -> p a x", a=2)
        St = REf[:, 3072:4096].rearrange("p (a x) -> p a x", a=2)
        chosen = OTK[:, 0, 0:TT * N_EXP].rearrange("p (t e) -> p t e", t=TT)
        xs_tok, xg_tok, y_tokT = (r.rearrange("p (t h c) -> p t h c", t=TT, h=SSM_H) for r in (RCf, RHf, RDf))
        decay = REf[:, 0:2048].rearrange("p (h l) -> p h l", h=SSM_H)
        xgd = REf[:, 2048:3072].rearrange("p (h c) -> p h c", h=SSM_H)
        y_off = REf[:, 3072:4096].rearrange("p (h c) -> p h c", h=SSM_H)
        convbuf = [REf[:, 0:T + 3], REf[:, 1024:1024 + T + 3]]
        b_tok = RFf[:, 2048:3072].rearrange("p (g t n) -> p g t n", g=2, t=TT)
        state = RFf[:, 3072:4096].rearrange("p (g x) -> p g x", g=2)
        dt_t, cs_t, tot_t, adt_t, sd_t, dte_t, dec_t, tmp_t = (
            MASK[:, i * 64:(i + 1) * 64].rearrange("p (t h) -> p t h", t=TT) for i in range(8))
        cbm = OTK[:, 0, 0:256].rearrange("p (g l) -> p g l", g=2)
        delta, lnm = RH[:, 0, :], RH[:, 1, :]
        v2 = REf.rearrange("p (t d) -> p t d", t=TT)

        w_in = [sem(f"w_in{n}") for n in range(RING)]
        w_in2 = [sem(f"w_in2_{n}") for n in range(RING)]
        ada_done = sem("ada_done")
        moe_used = sem("moe_used")
        x_in = sem("x_in")
        c_in = sem("c_in")
        wr_in = sem("wr_in")
        wdt_in = sem("wdt_in")
        rev_in = sem("rev_in")
        ext_out = sem("ext_out")
        bias_in = sem("bias_in")
        consts = sem("consts")
        cact_ok = sem("cact_ok")
        sq_ready = sem("sq_ready")
        sq_used = sem("sq_used")
        rinv_ok = sem("rinv_ok")
        rinv_used = sem("rinv_used")
        h_ok = sem("h_ok")
        acc = sem("acc")
        ev = [sem("ev0"), sem("ev1")]
        lat_n = sem("lat_n")
        lat_ok = sem("lat_ok")
        s_full = sem("s_full")
        biased = sem("biased")
        p_ready = sem("p_ready")
        pt_full = sem("pt_full")
        pt_ready = [sem("pt_ready0"), sem("pt_ready1")]
        pv_done = sem("pv_done")
        o_ready = sem("o_ready")
        bias_ok = sem("bias_ok")
        g_used = sem("g_used")
        g_tanh = sem("g_tanh")
        g_done = sem("g_done")
        x1_ok = sem("x1_ok")
        lg_full = sem("lg_full")
        mask_ok = sem("mask_ok")
        pos_full = sem("pos_full")
        route_ok = sem("route_ok")
        np_ok = sem("np_ok")
        oh_ready = sem("oh_ready")
        ohw_ready = sem("ohw_ready")
        got = sem("got")
        st_t = sem("st_t")
        x_ev = sem("x_ev")
        sg_done = sem("sg_done")
        hid_done = sem("hid_done")
        z_ev = sem("z_ev")
        st_ev = sem("st_ev")
        y_full = sem("y_full")
        y_ev = sem("y_ev")
        x2_ok = sem("x2_ok")
        lnm_ok = sem("lnm_ok")
        dt_full = sem("dt_full")
        mod_ok = sem("mod_ok")
        rope_ok = sem("rope_ok")
        ang_ok = sem("ang_ok")
        pos_in = sem("pos_in")
        mask_mem = sem("mask_mem")
        lat_raw = sem("lat_raw")
        ropeb = sem("ropeb")
        zero_ok = sem("zero_ok")
        y0_ok = sem("y0_ok")
        ext_ok = sem("ext_ok")
        h2t_ok = sem("h2t_ok")
        sp1 = sem("sp1")
        sp2 = sem("sp2")
        xg_ok = sem("xg_ok")
        yd_full = sem("yd_full")
        yo_full = sem("yo_full")
        st_full = sem("st_full")
        mixp = sem("mixp")
        ba_base = sem("ba_base")
        bias_used = sem("bias_used")
        adt_ok = sem("adt_ok")
        conv_in = sem("conv_in")
        conv_ok = sem("conv_ok")
        xbc_ok = sem("xbc_ok")
        cs_full = sem("cs_full")
        cs_ok = sem("cs_ok")
        cb_full = sem("cb_full")
        cb_ok = sem("cb_ok")
        csb_full = sem("csb_full")
        dd_ok = sem("dd_ok")
        ee_ok = sem("ee_ok")
        mm_ok = sem("mm_ok")
        xgd_ok = sem("xgd_ok")
        yst_full = sem("yst_full")
        state_ok = sem("state_ok")
        y_tok = sem("y_tok")
        zt_ok = sem("zt_ok")
        mixn = sem("mixn")
        r_ok = sem("r_ok")
        mod_h = sem("mod_h")
        flip_full = sem("flip_full")
        flip_ev = sem("flip_ev")
        delta_ok = sem("delta_ok")
        skip_ok = sem("skip_ok")
        cen_ok = sem("cen_ok")
        mu_full = sem("mu_full")
        fin_ok = sem("fin_ok")
        out_done = sem("out_done")
        dve_c, act_c, pool_c = sem("dve_chain"), sem("act_chain"), sem("pool_chain")

        def V(name, i=0, n=1):
            return vec[:, V_AT[name] + i:V_AT[name] + i + n]

        def slot(n):
            return ring[:, n % RING, :]

        def freed_pre(n):
            if n < 16:
                return ada_done, n + 1
            if n < 64:
                i, r = (n - 16) // 3, (n - 16) % 3
                return (acc, PE_S1 + i + 1) if r == 0 else (ada_done, 16 + 2 * i + r)
            if n < 67:
                return acc, PE_U + (4, 8, 16)[n - 64]
            if n < 91:
                return g_used, n - 66
            return acc, PE_O + n - 90

        def freed_post(n):
            for first, count, e in ((0, 24, PE_Q2), (24, 12, PE_XBC), (36, 16, PE_ZA)):
                if first <= n < first + count:
                    return acc, e + n - first + 1
            return acc, PE_OUT + (n - 52) // 2 + 1

        PE_S1 = 0
        PE_U = PE_S1 + 16
        PE_OT = PE_U + 16
        PE_O = PE_OT + 8
        PE_H = PE_O + 8
        PE_Q2 = PE_H + 8
        PE_OT2 = PE_Q2 + 24
        PE_XBC = PE_OT2 + 8
        PE_XT = PE_XBC + 12
        PE_BT = PE_XT + 8
        PE_YT = PE_BT + 2
        PE_ZA = PE_YT + 8
        PE_ZS = PE_ZA + 8
        PE_OUT = PE_ZS + 8
        assert all(e % 2 == 0 for e in (PE_U, PE_OT, PE_O, PE_H, PE_Q2, PE_OT2, PE_XBC, PE_XT, PE_BT, PE_YT, PE_ZA))

        def bank(e):
            return ps[6 + e % 2]

        def half(ap, h):
            return ap[(h % 2) * 64:(h % 2) * 64 + 64, h // 2, :]

        bias_hc = RG

        def group_ops(g):
            if g == 0:
                return (lambda h, t: half(qbT, h)[:, t * P:(t + 1) * P], lambda h, w: half(kbT, h)[:, 0:w],
                        lambda h, j: vb[:, j, h * 64:h * 64 + 64], lambda h: bias_hc[:, h, :])
            if g == 1:
                return (lambda h, t: RD[:, h, t * P:(t + 1) * P], lambda h, w: RE[:, h, 0:w],
                        lambda h, j: va[:, j, h * 64:h * 64 + 64], lambda h: MASK[:, :])
            o = (g - 2) * HG
            return (lambda h, t: half(RC, h + o)[:, t * P:(t + 1) * P], lambda h, w: half(RD, h + o)[:, 0:w],
                    lambda h, j: v2[:, j, (h + o) * 64:(h + o) * 64 + 64], lambda h: bias_hc[:, h, :])

        OT_DST = [obT, oaT, RB[:, 0:4, :], RB[:, 4:8, :]]
        UNITS = [(t, h) for t in range(TT) for h in range(HG)]
        NU = len(UNITS)

        def ot_event(g, t):
            return (PE_OT if g < 2 else PE_OT2) + (g % 2) * TT + t

        ST_H1, ST_Q, ST_KV, ST_H2 = 0, 8, 10, 11
        ST_F, ST_AT, ST_SS, ST_VAR = 19, 27, 35, 43

        block = ctx.enter_context(nc.Block())

        @block.sync
        def _(sp):
            sp.dma_start(vec[:, :], vec_d).then_inc(c_in, 16)
            sp.dma_start(rows[:, :], rows_d.partition_broadcast(P)).then_inc(c_in, 16)
            for n in range(N_PRE):
                if n >= RING:
                    sp.wait_ge(*freed_pre(n - RING))
                sp.dma_start(slot(n), pre_d[n]).then_inc(w_in[n % RING], 16)
            for j in range(QUAD_TILES):
                if j < RING:
                    sp.wait_ge(*freed_pre(N_PRE + j - RING))
                else:
                    sp.wait_ge(moe_used, QUAD_TILES + j - RING + 1)
                sp.dma_start(slot(N_PRE + j), moe_d[j]).then_inc(w_in[(N_PRE + j) % RING], 16)
            with sp.Fori(1, N_QUADS) as q:
                for j in range(QUAD_TILES):
                    sp.wait_ge(moe_used, QUAD_TILES + j - RING + 1 + q * QUAD_TILES)
                    sp.dma_start(slot(N_PRE + j), moe_d[bass.ds(q * QUAD_TILES + j, 1)].squeeze(0)).then_inc(
                        w_in[(N_PRE + j) % RING], 16)
            sp.wait_ge(np_ok, 1)
            npass = sp.value_load(npi[0:1, 0:1], min_val=1, max_val=MAXPASS)
            with sp.If(npass > 1):
                with sp.Fori(1, npass) as p:
                    with sp.Fori(0, N_QUADS) as q:
                        for j in range(QUAD_TILES):
                            sp.wait_ge(moe_used, QUAD_TILES + j - RING + 1 + q * QUAD_TILES
                                       + p * (QUAD_TILES * N_QUADS))
                            sp.dma_start(slot(N_PRE + j), moe_d[bass.ds(q * QUAD_TILES + j, 1)].squeeze(0)).then_inc(
                                w_in[(N_PRE + j) % RING], 16)
            for n in range(N_POST):
                if n < RING:
                    sp.wait_ge(moe_used, QUAD_TILES + n - RING + 1 + npass * (QUAD_TILES * N_QUADS))
                else:
                    sp.wait_ge(*freed_post(n - RING))
                sp.dma_start(slot(N_PRE + n), post_d[n]).then_inc(w_in2[(N_PRE + n) % RING], 16)
            for k in range(KT):
                sp.wait_ge(fin_ok, k + 1)
                sp.dma_start(out_d[k * P:(k + 1) * P, :], RC[:, k, :]).then_inc(out_done, 16)
            sp.wait_ge(out_done, 16 * KT)

        @block.tensor
        def _(pe):
            mm = nc.tensor.matmul
            e_state = [0]

            def free_bank(e):
                assert e == e_state[0], (e, e_state[0])
                e_state[0] += 1
                if e >= 2:
                    pe.wait_ge(ev[e % 2], e // 2)

            def arrive(n):
                pe.wait_ge(w_in[n % RING], 16 * (n // RING + 1))

            def arrive2(n):
                s = (N_PRE + n) % RING
                pe.wait_ge(w_in2[s], 16 * (n // RING + 1))

            def column(e, w, x, free=None):
                free_bank(e)
                k_n = free or KT
                for k in range(k_n):
                    last = mm(bank(e)[:, :], w[:, k * P:(k + 1) * P], x(k), start=(k == 0), stop=(k == k_n - 1))
                last.then_inc(acc, 1)

            def column_tok(e, w, x):
                free_bank(e)
                for t in range(TT):
                    for k in range(KT):
                        last = mm(bank(e)[:, t * P:(t + 1) * P], x(k)[:, t * P:(t + 1) * P],
                                  w[:, k * P:(k + 1) * P], start=(k == 0), stop=(k == KT - 1))
                last.then_inc(acc, 1)

            def stats(at, n, b):
                for k in range(n):
                    pe.wait_ge(sq_ready, at + k + 1)
                    mm(ps[b][:, :], ones[:, :], SQ[:, (at + k) % 2, :], start=(k == 0),
                       stop=(k == n - 1)).then_inc(sq_used, 1)

            def ada(n, col, b, base):
                arrive(n)
                for k in range(KT):
                    last = mm(ps[b][:, col - base:col - base + 1], slot(n)[:, k * P:(k + 1) * P], cact[:, k:k + 1],
                              start=(k == 0), stop=(k == KT - 1))
                last.then_inc(ada_done, 1)

            def hT(k):
                return RB[:, k, :]

            def attend(g):
                ql, kr, vv, _ = group_ops(g)

                def scores(u):
                    t, h = UNITS[u]
                    n = g * NU + u
                    if n >= 2:
                        pe.wait_ge(biased, n - 1)
                    w = (t + 1) * P
                    mm(ps[n % 2][:, 0:w], ql(h, t), kr(h, w), start=True, stop=True).then_inc(s_full, 1)

                def turn(u):
                    t, h = UNITS[u]
                    n = g * NU + u
                    pe.wait_ge(p_ready, n + 1)
                    if n >= 2:
                        pe.wait_ge(pt_ready[n % 2], n // 2)
                    for j in range(t + 1):
                        last = nc.tensor.transpose(ps[2 + n % 2][:, j * P:(j + 1) * P],
                                                   PB[:, n % 2, j * P:(j + 1) * P], ident[:, :])
                    last.then_inc(pt_full, 1)

                def values(u):
                    t, h = UNITS[u]
                    n = g * NU + u
                    i = g * TT + t
                    pe.wait_ge(pt_ready[n % 2], n // 2 + 1)
                    if h == 0 and i >= 2:
                        pe.wait_ge(o_ready, i - 1)
                    for j in range(t + 1):
                        last = mm(ps[4 + i % 2][:, h * 64:h * 64 + 64], PTB[:, n % 2, j * P:(j + 1) * P], vv(h, j),
                                  start=(j == 0), stop=(j == t))
                    last.then_inc(pv_done, 1)

                def outputs(t):
                    i = g * TT + t
                    e = ot_event(g, t)
                    free_bank(e)
                    pe.wait_ge(o_ready, i + 1)
                    for c in range(4):
                        last = nc.tensor.transpose(bank(e)[:, c * P:(c + 1) * P], OTK[:, i % 2, c * P:(c + 1) * P],
                                                   ident[:, :])
                    last.then_inc(acc, 1)

                scores(0)
                scores(1)
                for u in range(NU + 1):
                    if u < NU:
                        turn(u)
                    if u + 2 < NU:
                        scores(u + 2)
                    if u >= 1:
                        values(u - 1)
                    if u >= 4 and (u - 4) % HG == 0 and u >= HG:
                        outputs((u - 4) // HG - 1)
                outputs(TT - 1)

            pe.wait_ge(consts, 1)
            stats(ST_H1, KT, 2)
            pe.wait_ge(cact_ok, 1)
            for n in range(16):
                ada(n, n, 0, 0)
            pe.wait_ge(h_ok, KT)
            for i in range(16):
                n = 16 + 3 * i
                arrive(n)
                (column if i < 12 else column_tok)(PE_S1 + i, slot(n), hT)
                ada(n + 1, 16 + 2 * i, 1, 16)
                ada(n + 2, 17 + 2 * i, 1, 16)
                if i == 7:
                    stats(ST_Q, 2, 2)
                if i == 9:
                    stats(ST_KV, 1, 2)
            n = 64
            pe.wait_ge(lat_n, 3)
            for c in range(8):
                if c % 4 == 0:
                    arrive(n + c // 4)
                w = slot(n + c // 4)[:, (c % 4) * 256:(c % 4) * 256 + 256]
                column(PE_U + c, w, lambda k: qnT[:, k, :], free=2)
            arrive(n + 2)
            for c in range(4):
                column(PE_U + 8 + c, slot(n + 2)[:, c * P:(c + 1) * P], lambda k: kvnT, free=1)
            for t in range(TT):
                e = PE_U + 12 + t
                free_bank(e)
                mm(bank(e)[:, :], kvnT[:, t * P:(t + 1) * P], slot(n + 2)[:, 512:1024], start=True,
                   stop=True).then_inc(acc, 1)
            pe.wait_ge(ev[0], PE_OT // 2)
            pe.wait_ge(ev[1], PE_OT // 2)
            pe.wait_ge(bias_in, 16)
            for h in range(HG):
                if h >= 2:
                    pe.wait_ge(flip_ev, h)
                mm(ps[4 + h % 2][:, :], flip[:, :], RG[:, h, :], start=True, stop=True).then_inc(flip_full, 1)
            pe.wait_ge(flip_ev, HG + 1)
            pe.wait_ge(mod_ok, 2)
            attend(0)
            pe.wait_ge(lat_ok, 1)
            attend(1)
            pe.wait_ge(ev[0], (PE_O) // 2)
            pe.wait_ge(ev[1], (PE_O) // 2)
            pe.wait_ge(o_ready, 2 * TT)
            for i in range(KT):
                n = 67 + 3 * i
                b = 4 * (i % 2)
                if i >= 2:
                    pe.wait_ge(g_done, i - 1)
                for s in range(2):
                    arrive(n + s)
                    for k in range(KT):
                        last = mm(ps[b + s][:, :], slot(n + s)[:, k * P:(k + 1) * P], hT(k), start=(k == 0),
                                  stop=(k == KT - 1))
                    last.then_inc(g_used, 1)
                arrive(n + 2)
                for s, src in ((2, oaT), (3, obT)):
                    for k in range(4):
                        kk = (s - 2) * 4 + k
                        last = mm(ps[b + s][:, :], slot(n + 2)[:, kk * P:(kk + 1) * P], src[:, k, :], start=(k == 0),
                                  stop=(k == 3))
                last.then_inc(g_used, 1)
            pe.wait_ge(g_done, KT)
            for i in range(KT):
                n = 91 + i
                arrive(n)
                column(PE_O + i, slot(n), lambda k: RC[:, k, :])
            stats(ST_H2, KT, 2)
            pe.wait_ge(h_ok, 2 * KT)
            pe.wait_ge(wr_in, 16)
            for t in range(TT):
                for k in range(KT):
                    last = mm(ps[0][:, t * 36:t * 36 + 36], hT(k)[:, t * P:(t + 1) * P], w_r[:, k, :],
                              start=(k == 0), stop=(k == KT - 1))
            last.then_inc(lg_full, 1)
            for i in range(KT):
                e = PE_H + i
                free_bank(e)
                t, hf = i // 2, i % 2
                for c in range(4):
                    last = nc.tensor.transpose(bank(e)[:, c * P:(c + 1) * P], hT(hf * 4 + c)[:, t * P:(t + 1) * P],
                                               ident[:, :])
                last.then_inc(acc, 1)
            pe.wait_ge(mask_ok, 1)
            for t in range(TT):
                for s in range(t + 1):
                    last = mm(ps[3][:, t * 32:t * 32 + 32], ones[:, :] if s < t else upper[:, :],
                              chosen[:, s, :], start=(s == 0), stop=(s == t))
            last.then_inc(pos_full, 1)
            for s in range(TT):
                last = mm(ps[4][:, 0:32], ones[:, :], chosen[:, s, :], start=(s == 0), stop=(s == TT - 1))
            last.then_inc(pos_full, 1)
            pe.wait_ge(ev[0], PE_Q2 // 2)
            pe.wait_ge(ev[1], PE_Q2 // 2)
            pe.wait_ge(route_ok, 1)
            pe.wait_ge(np_ok, 1)
            npass = pe.value_load(npi[0:1, 0:1], min_val=1, max_val=MAXPASS)
            pe.sem_inc(got, 2)
            pe.sem_inc(st_t, 2)
            pe.sem_inc(y_full, 1)
            pe.sem_inc(moe_used, QUAD_TILES)
            with pe.Fori(0, npass * N_QUADS) as q:
                def warrive(j):
                    n = N_PRE + j
                    pe.wait_ge(w_in[n % RING], 16 * (n // RING + 1) + q * (16 * QUAD_TILES // RING))

                def gather(j):
                    pe.wait_ge(oh_ready, j + 1 + q * QUAD)
                    pe.wait_ge(x_ev, j + 1 + q * QUAD)
                    for k in range(KT):
                        for t in range(TT):
                            last = mm(ps[j % 2][:, k * SLOTS:(k + 1) * SLOTS], h2tok[:, t, k * P:(k + 1) * P],
                                      OH[:, j % 2, t, :], start=(t == 0), stop=(t == TT - 1))
                    last.then_inc(got, 1)

                def gate_up(j):
                    pe.wait_ge(x_ev, j + 3 + q * QUAD)
                    pe.wait_ge(hid_done, j + 1 + q * QUAD)
                    for s in range(4):
                        warrive(GU_AT[j] + s)
                        w = slot(N_PRE + GU_AT[j] + s)
                        for k in range(KT):
                            last = mm(ps[2 + j % 2][:, s * SLOTS:(s + 1) * SLOTS], w[:, k * P:(k + 1) * P],
                                      Xg[:, j % 2, k, :], start=(k == 0), stop=(k == KT - 1))
                        last.then_inc(moe_used, 1)

                def down(j):
                    pe.wait_ge(hid_done, j + 3 + q * QUAD)
                    pr, o = j // 2, (j % 2) * SLOTS
                    if j % 2 == 0:
                        pe.wait_ge(z_ev, pr + 1 + q * 2)
                    for s in range(2):
                        warrive(DN_AT[j] + s)
                    for hf in range(2):
                        for s in range(2):
                            w = slot(N_PRE + DN_AT[j] + s)
                            last = mm(ps[4 + hf][o:o + SLOTS, :], hid[:, j % 2, s, :], w[:, hf * T:(hf + 1) * T],
                                      start=(s == 0), stop=(s == 1))
                    last.then_inc(moe_used, 2)

                def turn_slots(pr):
                    pe.wait_ge(ohw_ready, 2 * pr + 2 + q * QUAD)
                    pe.wait_ge(y_ev, pr + 1 + q * KT)
                    for t in range(TT):
                        last = nc.tensor.transpose(ps[6 + pr][:, t * P:(t + 1) * P], OHW[:, pr, t, :], ident[:, :])
                    last.then_inc(st_t, 1)

                gather(0)
                gather(1)
                gate_up(0)
                gather(2)
                gate_up(1)
                down(0)
                gather(3)
                gate_up(2)
                down(1)
                turn_slots(0)
                gate_up(3)
                down(2)
                turn_slots(1)
                down(3)
                pe.wait_ge(z_ev, 3 + q * 2)
                pe.wait_ge(st_ev, 2 + q * 2)
                for n in range(KT):
                    if n >= 2:
                        pe.wait_ge(y_ev, n + 1 + q * KT)
                    for pr in range(2):
                        last = mm(ps[6 + n % 2][:, :], Zs[:, pr, n * P:(n + 1) * P], St[:, pr, :], start=(pr == 0),
                                  stop=(pr == 1))
                    last.then_inc(y_full, 1)
            stats(ST_F, KT, 2)
            pe.wait_ge(x2_ok, KT)
            xT = lambda k: RA[:, k, :]
            for i in range(24):
                e = PE_Q2 + i
                arrive2(i)
                (column if i < 16 else column_tok)(e, slot(N_PRE + i), xT)
            pe.wait_ge(ev[0], PE_OT2 // 2)
            pe.wait_ge(ev[1], PE_OT2 // 2)
            for g in (2, 3):
                attend(g)
            for i in range(12):
                arrive2(24 + i)
                column(PE_XBC + i, slot(N_PRE + 24 + i), xT)
            pe.wait_ge(wdt_in, 16)
            for t in range(TT):
                for k in range(KT):
                    last = mm(ps[0][:, t * 16:t * 16 + 16], xT(k)[:, t * P:(t + 1) * P], wdt[:, k, :],
                              start=(k == 0), stop=(k == KT - 1))
            last.then_inc(dt_full, 1)
            pe.wait_ge(xbc_ok, 8)
            for i in range(8):
                e = PE_XT + i
                free_bank(e)
                t, hf = i // 2, i % 2
                for c in range(4):
                    last = nc.tensor.transpose(bank(e)[:, c * P:(c + 1) * P],
                                               RG[:, hf * 4 + c, t * P:(t + 1) * P], ident[:, :])
                last.then_inc(acc, 1)
            pe.wait_ge(xbc_ok, 12)
            for g in range(2):
                e = PE_BT + g
                free_bank(e)
                for t in range(TT):
                    last = nc.tensor.transpose(bank(e)[:, t * P:(t + 1) * P], RF[:, g, t * P:(t + 1) * P], ident[:, :])
                last.then_inc(acc, 1)
            pe.wait_ge(adt_ok, 1)
            for c in range(TT):
                mm(ps[1][:, c * 16:c * 16 + 16], upper[:, :], adt_t[:, c, :], start=True, stop=True)
            for c in range(TT):
                last = mm(ps[1][:, 64 + c * 16:80 + c * 16], ones[:, :], adt_t[:, c, :], start=True, stop=True)
            last.then_inc(cs_full, 1)
            pe.wait_ge(ev[0], PE_YT // 2)
            pe.wait_ge(ev[1], PE_YT // 2)
            pe.wait_ge(cs_ok, 1)
            for c in range(TT):
                if c >= 1:
                    pe.wait_ge(y_tok, c)
                for g in range(2):
                    last = mm(ps[0][:, g * P:(g + 1) * P], RF[:, g, c * P:(c + 1) * P], RF[:, 2 + g, c * P:(c + 1) * P],
                              start=True, stop=True)
                last.then_inc(cb_full, 1)
                for q in range(4):
                    if 4 * c + q >= 2:
                        pe.wait_ge(dd_ok, 4 * c + q - 1)
                    for h in range(4):
                        last = mm(ps[2 + q % 2][:, h * P:(h + 1) * P],
                                  adt_t[:, c, 4 * q + h:4 * q + h + 1].to_broadcast([P, P]), upper[:, :],
                                  start=True, stop=True)
                    last.then_inc(csb_full, 1)
                if c == 0:
                    pe.wait_ge(xg_ok, TT)
                for h in range(SSM_H):
                    if h % 4 == 0:
                        pe.wait_ge(mm_ok, 4 * c + h // 4 + 1)
                    last = mm(ps[4 + h // 8][:, (h % 8) * 64:(h % 8) * 64 + 64], decay[:, h, :], xg_tok[:, c, h, :],
                              start=True, stop=True)
                last.then_inc(yd_full, 1)
                if c > 0:
                    pe.wait_ge(state_ok, c)
                    pe.wait_ge(cb_ok, c + 1)
                    for g in range(2):
                        last = mm(ps[g][:, :], RF[:, 2 + g, c * P:(c + 1) * P], state[:, g, :], start=True, stop=True)
                    last.then_inc(yo_full, 1)
                if c < TT - 1:
                    pe.wait_ge(xgd_ok, c + 1)
                    for g in range(2):
                        last = mm(ps[6 + g][:, :], b_tok[:, g, c, :], REf[:, 2048 + g * T:2048 + (g + 1) * T], start=True, stop=True)
                    last.then_inc(st_full, 1)
            for i in range(8):
                e = PE_YT + i
                t, hf = i // 2, i % 2
                free_bank(e)
                pe.wait_ge(y_tok, TT)
                for c in range(4):
                    last = nc.tensor.transpose(bank(e)[:, c * P:(c + 1) * P],
                                               RDf[:, t * D + (hf * 4 + c) * P:t * D + (hf * 4 + c + 1) * P], ident[:, :])
                last.then_inc(acc, 1)
            for i in range(16):
                arrive2(36 + i)
                column(PE_ZA + i, slot(N_PRE + 36 + i), xT)
            stats(ST_AT, KT, 2)
            stats(ST_SS, KT, 3)
            pe.wait_ge(mixn, 16)
            for i in range(KT):
                e = PE_OUT + i
                free_bank(e)
                for s in range(2):
                    n = 52 + 2 * i + s
                    arrive2(n)
                    for k in range(KT):
                        last = mm(bank(e)[:, :], slot(N_PRE + n)[:, k * P:(k + 1) * P],
                                  RB[:, k, :] if s == 0 else RG[:, k, :], start=(s == 0 and k == 0),
                                  stop=(s == 1 and k == KT - 1))
                last.then_inc(acc, 1)
            for k in range(KT):
                pe.wait_ge(r_ok, k + 1)
                last = mm(ps[4][:, :], ones[:, :], RA[:, k, :], start=(k == 0), stop=(k == KT - 1))
            last.then_inc(mu_full, 1)
            stats(ST_VAR, KT, 5)

        def tok_dst(view, t, hf):
            return view[:, t, hf * T:(hf + 1) * T]

        def quad(ap):
            return ap.rearrange("p (a b) -> p a b", a=4)

        def s1_dst(i):
            b = bank(PE_S1 + i)
            if i < 2:
                return [(qlT[:, i, :], b[:, :])], 1.0
            if i == 2:
                return [(kvT, b[:, :])], 1.0
            if i == 3:
                return [(krT, b[:, :])], 1.0
            if i < 8:
                return [(qbT[:, i - 4, :], b[:, :])], 0.125
            if i < 12:
                return [(kbT[:, i - 8, :], b[:, :])], 1.0
            return [(vb[:, :, (i - 12) * P:(i - 11) * P], quad(b[:, :]))], 1.0

        def u_dst(c):
            b = bank(PE_U + c)
            if c < 4:
                return [(RD[0:64, 2 * c, :], b[0:64, :]), (RD[64:128, 2 * c + 1, :], b[64:128, :])], MLA_SCALE
            if c < 8:
                return [((OTK if c % 2 == 0 else PTB)[:, (c - 4) // 2, :], b[:, :])], MLA_SCALE
            if c < 12:
                j = c - 8
                return [(RE[0:64, 2 * j, :], b[0:64, :]), (RE[64:128, 2 * j + 1, :], b[64:128, :])], 1.0
            return [(va[:, c - 12, :], b[:, :])], 1.0

        def q2_dst(i):
            b = bank(PE_Q2 + i)
            if i < 8:
                return [(RC[:, i, :], b[:, :])], 0.125
            if i < 16:
                return [(RD[:, i - 8, :], b[:, :])], 1.0
            return [(v2[:, :, (i - 16) * P:(i - 15) * P], quad(b[:, :]))], 1.0

        def ot_dst(g, t):
            return [(OT_DST[g][:, :, t * P:(t + 1) * P], quad(bank(ot_event(g, t))[:, :]))], 1.0

        @block.scalar
        def _(act):
            A = nc.scalar.activation
            links = [0]

            def link(ins):
                links[0] += 1
                ins.then_inc(act_c, 1)
                act.wait_ge(act_c, links[0])

            def evict(e, what):
                pairs, scale = what
                act.wait_ge(acc, e + 1)
                for dst, src in pairs:
                    ins = A(dst, src, ACT.Copy, scale=scale)
                ins.then_inc(ev[e % 2], 1)

            def norm(idx, at, n, b, src, ready, eps):
                for k in range(n):
                    ready(k)
                    if at + k >= 2:
                        act.wait_ge(sq_used, at + k - 1)
                    A(SQ[:, (at + k) % 2, :], src(k), ACT.Square).then_inc(sq_ready, 1)
                act.wait_ge(sq_used, at + n)
                if idx > 0:
                    act.wait_ge(rinv_used, idx)
                link(A(RINV[:, :], ps[b][:, :], ACT.Ln, scale=1.0 / (n * P), bias=eps))
                A(RINV[:, :], RINV[:, :], ACT.Exp, scale=-0.5).then_inc(rinv_ok, 1)

            def attend(g):
                def evict_pt(u):
                    n = g * NU + u
                    if n % 2 == 0:
                        return
                    w = (UNITS[u][0] + 1) * P
                    act.wait_ge(pt_full, n + 1)
                    if n >= 2:
                        act.wait_ge(pv_done, n - 1)
                    A(PTB[:, 1, 0:w], ps[3][:, 0:w], ACT.Copy).then_inc(pt_ready[1], 1)

                for u in range(NU):
                    t, h = UNITS[u]
                    n, i = g * NU + u, g * TT + t
                    w = (t + 1) * P
                    act.wait_ge(biased, n + 1)
                    if n >= 2:
                        act.wait_ge(pt_full, n - 1)
                    if h == 0 and i >= 2:
                        act.wait_ge(o_ready, i - 1)
                    A(PB[:, n % 2, 0:w], SB[:, n % 2, 0:w], ACT.Exp, scale=-1.0, bias=nmax(n),
                      accum_out=rowsum[:, (i % 2) * HG + h:(i % 2) * HG + h + 1]).then_inc(p_ready, 1)
                    if u >= 1:
                        evict_pt(u - 1)
                    if u % HG == 5 and u > HG:
                        t_o = u // HG - 1
                        if ot_event(g, t_o) % 2:
                            evict(ot_event(g, t_o), ot_dst(g, t_o))
                evict_pt(NU - 1)
                if ot_event(g, TT - 1) % 2:
                    evict(ot_event(g, TT - 1), ot_dst(g, TT - 1))

            act.dma_start(RA[:, 0:4, :], xT_d[0:T, :].rearrange("(k p) t -> p k t", p=P)).then_inc(x_in, 16)
            act.dma_start(RA[:, 4:8, :], xT_d[T:D, :].rearrange("(k p) t -> p k t", p=P)).then_inc(x_in, 16)
            act.dma_start(OTK[:, 0, :].bitcast(I32), pos_d.partition_broadcast(P)).then_inc(pos_in, 16)
            act.dma_start(ext_row[:, 255:640], rel_d[:, 0:385]).then_inc(rev_in, 16)
            act.dma_start(w_r[:, :, :], wr_d).then_inc(wr_in, 16)
            act.dma_start(wdt[:, :, :], wdt_d).then_inc(wdt_in, 16)
            act.wait_ge(x_in, 32)
            act.wait_ge(consts, 1)
            norm(0, ST_H1, KT, 2, lambda k: RA[:, k, :], lambda k: None, eps1)
            act.wait_ge(c_in, 32)
            A(cact, V("c", 0, 8), ACT.Silu).then_inc(cact_ok, 1)
            act.wait_ge(ext_ok, 1)
            act.dma_start(ext_d, ext_row[:, :]).then_inc(ext_out, 16)
            act.wait_ge(ext_out, 16)
            act.dma_start(RG[:, :, :], bass.AP(ext_d.tensor, 0, [[1, P], [640, HG], [1, T]])).then_inc(bias_in, 16)
            act.wait_ge(ang_ok, 2)
            A(sinT, RH[:, 4, :], ACT.Sin)
            A(cosT, RH[:, 5, :], ACT.Sin).then_inc(rope_ok, 1)
            for i in range(16):
                if i % 2:
                    evict(PE_S1 + i, s1_dst(i))
                if i == 7:
                    act.wait_ge(ev[0], 1)
                    norm(1, ST_Q, 2, 2, lambda k: qlT[:, k, :], lambda k: None, eps1)
                if i == 9:
                    act.wait_ge(ev[0], 2)
                    norm(2, ST_KV, 1, 2, lambda k: kvT, lambda k: None, eps1)
            for c in range(16):
                if c % 2:
                    evict(PE_U + c, u_dst(c))
            act.wait_ge(lat_ok, 1)
            attend(0)
            attend(1)
            act.wait_ge(pt_full, 2 * NU)
            for i in range(KT):
                if i >= 2:
                    act.wait_ge(g_done, i - 1)
                b = 4 * (i % 2)
                act.wait_ge(g_used, 3 * i + 1)
                A(SB[:, i % 2, :], ps[b][:, :], ACT.Tanh, scale=0.5)
                act.wait_ge(g_used, 3 * i + 2)
                A(PB[:, i % 2, :], ps[b + 1][:, :], ACT.Tanh, scale=0.5).then_inc(g_tanh, 1)
            norm(3, ST_H2, KT, 2, lambda k: RA[:, k, :], lambda k: act.wait_ge(x1_ok, k + 1), eps1)
            for i in range(8):
                if i % 2:
                    e = PE_H + i
                    evict(e, ([(tok_dst(h2tok, i // 2, 1), bank(e)[:, :])], 1.0))
            act.wait_ge(sp1, 1)
            A(SB[:, 0, 32:52], SB[:, 0, 0:20], ACT.Exp).then_inc(sp2, 1)
            act.wait_ge(np_ok, 1)
            npass = act.value_load(npi[0:1, 0:1], min_val=1, max_val=MAXPASS)
            act.sem_inc(x_ev, 2)
            act.sem_inc(z_ev, 1)
            with act.Fori(0, npass * N_QUADS) as q:
                def tiles(n):
                    return QUAD_TILES + n + q * QUAD_TILES

                def gathered(j):
                    act.wait_ge(got, j + 3 + q * QUAD)
                    act.wait_ge(moe_used, tiles(GU_END[j - 2] if j >= 2 else GU_END[j + 2] - QUAD_TILES))
                    A(Xg[:, j % 2, :, :], ps[j % 2][:, :].rearrange("p (k s) -> p k s", k=KT), ACT.Copy).then_inc(x_ev, 1)

                def gate(j):
                    act.wait_ge(moe_used, tiles(GU_END[j]))
                    act.wait_ge(hid_done, j + 1 + q * QUAD)
                    A(sg[:, j % 2, :], ps[2 + j % 2][:, 0:2 * SLOTS], ACT.Silu).then_inc(sg_done, 1)

                def downs(pr):
                    act.wait_ge(moe_used, tiles(DN_END[2 * pr + 1]))
                    act.wait_ge(y_full, 1 + q * KT)
                    A(Zs[:, pr, 0:T], ps[4][:, :], ACT.Copy)
                    A(Zs[:, pr, T:D], ps[5][:, :], ACT.Copy).then_inc(z_ev, 1)

                def turned(pr):
                    act.wait_ge(st_t, 3 + pr + q * 2)
                    act.wait_ge(y_full, 1 + q * KT)
                    A(St[:, pr, :], ps[6 + pr][:, :], ACT.Copy).then_inc(st_ev, 1)

                gathered(0)
                gathered(1)
                gate(0)
                gathered(2)
                gate(1)
                gathered(3)
                gate(2)
                downs(0)
                turned(0)
                gate(3)
                turned(1)
                downs(1)
            norm(4, ST_F, KT, 2, lambda k: RA[:, k, :], lambda k: act.wait_ge(x1_ok, KT + k + 1), eps1)
            for i in range(24):
                if i % 2:
                    evict(PE_Q2 + i, q2_dst(i))
            attend(2)
            attend(3)
            act.wait_ge(pv_done, 4 * NU)
            for i in range(13):
                if i < 12:
                    if i >= 2:
                        act.wait_ge(conv_ok, i - 1)
                    act.wait_ge(acc, PE_XBC + i + 1)
                    ins = A(convbuf[i % 2][:, 3:T + 3], bank(PE_XBC + i)[:, :], ACT.Copy)
                    ins.then_inc(ev[i % 2], 1)
                if i >= 1:
                    act.wait_ge(conv_ok, i)
                    tile = RG[:, i - 1, :] if i - 1 < 8 else RF[:, i - 9, :]
                    A(tile, tile, ACT.Silu).then_inc(xbc_ok, 1)
            act.wait_ge(sp1, 2)
            link(A(tmp_t[:, :, :], tmp_t[:, :, :], ACT.Exp))
            A(aneg, rows[:, R_ALOG:R_ALOG + 16], ACT.Exp)
            A(tmp_t[:, :, :], tmp_t[:, :, :], ACT.Ln, bias=ones[:, 0:1]).then_inc(sp2, 1)
            for i in range(8):
                if i % 2:
                    e = PE_XT + i
                    evict(e, ([(RCf[:, (i // 2) * D + T:(i // 2) * D + D], bank(e)[:, :])], 1.0))
            evict(PE_BT + 1, ([(b_tok[:, 1, :, :], quad(bank(PE_BT + 1)[:, :]))], 1.0))
            act.wait_ge(cs_ok, 1)
            A(sd_t[:, :, :], cs_t[:, :, :], ACT.Exp)
            A(dec_t[:, :, :], tot_t[:, :, :], ACT.Exp)
            A(dte_t[:, :, :], tmp_t[:, :, :], ACT.Exp).then_inc(sp2, 1)
            for c in range(TT):
                for q in range(4):
                    act.wait_ge(dd_ok, 4 * c + q + 1)
                    A(decay[:, 4 * q:4 * q + 4, :], decay[:, 4 * q:4 * q + 4, :], ACT.Exp).then_inc(ee_ok, 1)
            for i in range(8):
                if i % 2:
                    e = PE_YT + i
                    evict(e, ([(RG[:, 4:8, (i // 2) * P:(i // 2 + 1) * P], quad(bank(e)[:, :]))], 1.0))
            for i in range(16):
                e = PE_ZA + i
                if i >= 4:
                    act.wait_ge(mixp, i - 3)
                act.wait_ge(acc, e + 1)
                A(zbuf(i), bank(e)[:, :], ACT.Silu).then_inc(ev[e % 2], 1)
            norm(5, ST_AT, KT, 2, lambda k: RB[:, k, :], lambda k: act.wait_ge(mixp, k + 1), eps2)
            norm(6, ST_SS, KT, 3, lambda k: RG[:, k, :], lambda k: act.wait_ge(mixp, KT + k + 1), eps2)
            norm(7, ST_VAR, KT, 5, lambda k: RC[:, k, :], lambda k: act.wait_ge(cen_ok, k + 1), eps2)

        @block.vector
        def _(dve):
            v = nc.vector
            links = [0]

            def link(ins):
                links[0] += 1
                ins.then_inc(dve_c, 1)
                dve.wait_ge(dve_c, links[0])

            def evict(e, what):
                pairs, scale = what
                dve.wait_ge(acc, e + 1)
                for dst, src in pairs:
                    ins = v.tensor_scalar(dst, src, scale, None, ALU.mult) if scale != 1.0 else v.tensor_copy(dst, src)
                ins.then_inc(ev[e % 2], 1)

            def attend(g):
                def evict_pt(u):
                    n = g * NU + u
                    if n % 2:
                        return
                    w = (UNITS[u][0] + 1) * P
                    dve.wait_ge(pt_full, n + 1)
                    if n >= 2:
                        dve.wait_ge(pv_done, n - 1)
                    v.tensor_copy(PTB[:, 0, 0:w], ps[2][:, 0:w]).then_inc(pt_ready[0], 1)

                def normalise(t):
                    i = g * TT + t
                    dve.wait_ge(pv_done, HG * (i + 1))
                    r = rsinv[:, 0:HG]
                    link(v.reciprocal(r, rowsum[:, (i % 2) * HG:(i % 2) * HG + HG]))
                    if i >= 2:
                        gg, tt = (i - 2) // TT, (i - 2) % TT
                        dve.wait_ge(acc, ot_event(gg, tt) + 1)
                    v.tensor_tensor(OTK[:, i % 2, :].rearrange("p (h c) -> p h c", h=HG),
                                    ps[4 + i % 2][:, :].rearrange("p (h c) -> p h c", h=HG),
                                    r.unsqueeze(2).to_broadcast([P, HG, 64]), ALU.mult).then_inc(o_ready, 1)

                bias = group_ops(g)[3]
                for u in range(NU):
                    t, h = UNITS[u]
                    n = g * NU + u
                    w = (t + 1) * P
                    if g == 0 and u == 0:
                        dve.wait_ge(bias_ok, 1)
                    if g >= 2 and t == 0:
                        dve.wait_ge(bias_ok, 1 + (g - 2) * HG + h + 1)
                    dve.wait_ge(s_full, n + 1)
                    if n >= 2:
                        dve.wait_ge(p_ready, n - 1)
                    v.tensor_tensor_reduce(SB[:, n % 2, 0:w], ps[n % 2][:, 0:w], bias(h)[:, T - w:T], -1.0, 3e38,
                                           ALU.add, ALU.min, nmax(n)).then_inc(biased, 1)
                    if u >= 1:
                        evict_pt(u - 1)
                    if u % HG == 2 and u > HG:
                        normalise(u // HG - 1)
                    if u % HG == 5 and u > HG:
                        t_o = u // HG - 1
                        if ot_event(g, t_o) % 2 == 0:
                            evict(ot_event(g, t_o), ot_dst(g, t_o))
                evict_pt(NU - 1)
                normalise(TT - 1)
                if ot_event(g, TT - 1) % 2 == 0:
                    evict(ot_event(g, TT - 1), ot_dst(g, TT - 1))

            dve.wait_ge(c_in, 32)
            dve.wait_ge(pos_in, 16)
            posf, ang, turns, red = OTK[:, 1, :], SB[:, 0, :], SB[:, 1, :], PB[:, 0, :]
            link(v.tensor_copy(posf, OTK[:, 0, :].bitcast(I32)))
            link(v.tensor_scalar(ang, posf, V("inv"), None, ALU.mult))
            for quarter, dst in ((0.0, RH[:, 4, :]), (0.25, RH[:, 5, :])):
                link(v.tensor_scalar(turns, ang, float(1 / TWO_PI), quarter, ALU.mult, ALU.add))
                link(v.tensor_scalar(turns, turns, ROUND, None, ALU.add))
                link(v.tensor_scalar(turns, turns, ROUND, None, ALU.subtract))
                link(v.scalar_tensor_tensor(red, turns, -C1, ang, ALU.mult, ALU.add))
                link(v.scalar_tensor_tensor(red, turns, -C2, red, ALU.mult, ALU.add))
                link(v.scalar_tensor_tensor(red, turns, -C3, red, ALU.mult, ALU.add))
                link(v.tensor_scalar(red, red, quarter * TWO_PI, 3.1415925, ALU.add, ALU.min))
                v.tensor_scalar(dst, red, -3.1415925, None, ALU.max).then_inc(ang_ok, 1)
                dve.wait_ge(ang_ok, 1 if quarter == 0.0 else 2)
            dve.wait_ge(ada_done, 16)
            link(v.tensor_tensor(mod[:, 0:16], ps[0][:, 0:16], V("b_ada", 0, 16), ALU.add))
            link(v.scalar_tensor_tensor(A1, mod[:, 8:16], 1.0, V("g_mix", 0, 8), ALU.add, ALU.mult))
            dve.wait_ge(rinv_ok, 1)
            for k in range(KT):
                ins = v.scalar_tensor_tensor(RB[:, k, :], RA[:, k, :], A1[:, k:k + 1], RINV[:, :], ALU.mult, ALU.mult)
                ins.then_inc(mod_h, 1)
            dve.wait_ge(mod_h, KT)
            dve.sem_inc(rinv_used, 1)
            for i in range(16):
                if i % 2 == 0:
                    evict(PE_S1 + i, s1_dst(i))
                if i == 8:
                    dve.wait_ge(rinv_ok, 2)
                    dve.wait_ge(ev[1], 1)
                    for k in range(2):
                        v.scalar_tensor_tensor(qnT[:, k, :], qlT[:, k, :], V("g_q", k), RINV[:, :], ALU.mult,
                                               ALU.mult).then_inc(lat_n, 1)
                    dve.wait_ge(lat_n, 2)
                    dve.sem_inc(rinv_used, 1)
                if i == 10:
                    dve.wait_ge(rinv_ok, 3)
                    v.scalar_tensor_tensor(kvnT, kvT, V("g_kv"), RINV[:, :], ALU.mult, ALU.mult).then_inc(lat_n, 1)
                    dve.wait_ge(lat_n, 3)
                    dve.sem_inc(rinv_used, 1)
            dve.wait_ge(ada_done, 48)
            v.tensor_tensor(mod[:, 16:48], ps[1][:, 0:32], V("b_ada", 16, 32), ALU.add).then_inc(mod_ok, 2)
            dve.wait_ge(mod_ok, 2)
            link(v.scalar_tensor_tensor(A2, mod[:, 32:40], 1.0, V("g_ffn", 0, 8), ALU.add, ALU.mult))
            link(v.tensor_scalar(gt1h, mod[:, 16:24], 0.5, None, ALU.mult))
            dve.wait_ge(rope_ok, 1)
            dve.wait_ge(ev[1], 2)
            link(v.tensor_scalar(sinT, sinT, V("sign"), None, ALU.mult))
            dve.wait_ge(zero_ok, 1)
            link(v.tensor_tensor(SB[0:32, 0, :], krT[0:32, :], cosT[0:32, :], ALU.mult))
            link(v.tensor_tensor(SB[0:32, 1, :], krT[32:64, :], sinT[32:64, :], ALU.mult))
            for h in range(8):
                r = 64 if h % 2 == 0 else 32
                ins = v.tensor_tensor(RE[r:r + 32, h, :], SB[0:32, 0, :], SB[0:32, 1, :], ALU.add)
            link(ins)
            for c in range(16):
                if c % 2 == 0:
                    evict(PE_U + c, u_dst(c))
                if c in (6, 8):
                    r = (c - 6) // 2
                    dve.wait_ge(ev[0], (PE_U + 4 + 2 * r) // 2 + 1)
                    dve.wait_ge(ev[1], (PE_U + 5 + 2 * r) // 2 + 1)
                    link(v.tensor_tensor(SB[:, 0, :], OTK[:, r, :], cosT, ALU.mult))
                    link(v.tensor_tensor(SB[:, 1, :], PTB[:, r, :], sinT, ALU.mult))
                    for h in range(4):
                        hh, o = 4 * r + h, 64 if h % 2 == 0 else 32
                        ins = v.tensor_tensor(RD[o:o + 32, hh, :], SB[32 * h:32 * h + 32, 0, :],
                                              SB[32 * h:32 * h + 32, 1, :], ALU.add)
                    link(ins)
            for h in range(HG):
                dve.wait_ge(flip_full, h + 1)
                v.tensor_copy(RG[:, h, :], ps[4 + h % 2][:, :]).then_inc(flip_ev, 1)
            dve.sem_inc(lat_ok, 1)
            attend(0)
            attend(1)
            for i in range(KT):
                b = 4 * (i % 2)
                dve.wait_ge(g_tanh, i + 1)
                dve.wait_ge(g_used, 3 * i + 3)
                link(v.scalar_tensor_tensor(SB[:, i % 2, :], SB[:, i % 2, :], 1.0, ps[b + 2][:, :], ALU.add, ALU.mult))
                link(v.scalar_tensor_tensor(PB[:, i % 2, :], PB[:, i % 2, :], 1.0, ps[b + 3][:, :], ALU.add, ALU.mult))
                v.tensor_tensor(RC[:, i, :], SB[:, i % 2, :], PB[:, i % 2, :], ALU.add).then_inc(g_done, 1)
            for i in range(KT):
                e = PE_O + i
                dve.wait_ge(acc, e + 1)
                v.scalar_tensor_tensor(RA[:, i, :], bank(e)[:, :], gt1h[:, i:i + 1], RA[:, i, :], ALU.mult,
                                       ALU.add).then_inc(x1_ok, 1)
                dve.wait_ge(x1_ok, i + 1)
                dve.sem_inc(ev[e % 2], 1)
            dve.wait_ge(rinv_ok, 4)
            dve.wait_ge(g_used, 24)
            for k in range(KT):
                v.scalar_tensor_tensor(RB[:, k, :], RA[:, k, :], A2[:, k:k + 1], RINV[:, :], ALU.mult,
                                       ALU.mult).then_inc(mod_h, 1)
            dve.wait_ge(mod_h, 2 * KT)
            dve.sem_inc(rinv_used, 1)
            def lane(a, n):
                return SB[:, 0, a:a + n]

            L = OTK[:, 1, 0:144].rearrange("p (t n) -> p t n", t=TT)
            dve.wait_ge(lg_full, 1)
            dve.wait_ge(acc, PE_O)
            link(v.tensor_tensor(L, ps[0][:, 0:144].rearrange("p (t n) -> p t n", t=TT),
                                 rows[:, 0:36].unsqueeze(1).to_broadcast([P, TT, 36]), ALU.add))
            for i in range(8):
                if i % 2 == 0:
                    e = PE_H + i
                    evict(e, ([(tok_dst(h2tok, i // 2, 0), bank(e)[:, :])], 1.0))
            R = SB[:, 1, :]

            def r3(a, n):
                return R[:, a:a + TT * n].rearrange("p (t n) -> p t n", t=TT)

            def first_max(src, n, top, oh):
                link(v.tensor_reduce(top, src, AX_X, ALU.max))
                c = r3(256, n)
                link(v.tensor_tensor(c, src, top.unsqueeze(2).to_broadcast([P, TT, n]), ALU.is_equal))
                link(v.scalar_tensor_tensor(c, c, -64.0, iota64[:, 0:n].unsqueeze(1).to_broadcast([P, TT, n]),
                                            ALU.mult, ALU.add))
                link(v.tensor_reduce(R[:, 384:388], c, AX_X, ALU.min))
                link(v.tensor_tensor(oh, c, R[:, 384:388].unsqueeze(2).to_broadcast([P, TT, n]), ALU.is_equal))

            gmax, top1, top2 = lane(60, 4), lane(64, 4), lane(68, 4)
            goh = r3(400, 4)
            first_max(L[:, :, 0:4], 4, gmax, goh)
            link(v.tensor_scalar(goh, goh, 1e30, -1e30, ALU.mult, ALU.add))
            el = r3(0, 32)
            for t in range(TT):
                ins = v.tensor_tensor(el[:, t, :].rearrange("p (g e) -> p g e", g=4),
                                      L[:, t, 4:36].rearrange("p (g e) -> p g e", g=4),
                                      goh[:, t, :].unsqueeze(2).to_broadcast([P, 4, 8]), ALU.add)
            link(ins)
            oh1, oh2 = r3(128, 32), OTK[:, 1, 256:384].rearrange("p (t n) -> p t n", t=TT)
            first_max(el, 32, top1, oh1)
            link(v.scalar_tensor_tensor(el, oh1, -3e30, el, ALU.mult, ALU.add))
            first_max(el, 32, top2, oh2)
            link(v.tensor_tensor(lane(0, 16).rearrange("p (t n) -> p t n", t=TT), L[:, :, 0:4],
                                 gmax.unsqueeze(2).to_broadcast([P, TT, 4]), ALU.subtract))
            v.tensor_tensor(lane(16, 4), top2, top1, ALU.subtract).then_inc(sp1, 1)
            link(v.tensor_tensor(chosen, oh1, oh2, ALU.add))
            dve.sem_inc(mask_ok, 1)
            dve.wait_ge(sp2, 1)
            gsum, w1, w2 = lane(72, 4), lane(76, 4), lane(80, 4)
            link(v.tensor_reduce(gsum, lane(32, 16).rearrange("p (t n) -> p t n", t=TT), AX_X, ALU.add))
            link(v.tensor_scalar(w1, lane(48, 4), 1.0, None, ALU.add))
            link(v.tensor_tensor(w1, w1, gsum, ALU.mult))
            link(v.reciprocal(w1, w1))
            link(v.tensor_tensor(w2, w1, lane(48, 4), ALU.mult))
            link(v.tensor_tensor(oh1, oh1, w1.unsqueeze(2).to_broadcast([P, TT, 32]), ALU.mult))
            link(v.tensor_tensor(oh2, oh2, w2.unsqueeze(2).to_broadcast([P, TT, 32]), ALU.mult))
            dve.wait_ge(pv_done, 2 * NU)

            def et(ap, p=0):
                return ap[:, p * P:(p + 1) * P].rearrange("p (e t) -> p t e", t=TT)

            for p in range(MAXPASS):
                ins = v.tensor_tensor(et(combr, p), oh1, oh2, ALU.add)
            link(ins)
            dve.wait_ge(pos_full, 2)
            link(v.tensor_tensor(el, ps[3][:, 0:128].rearrange("p (t n) -> p t n", t=TT), chosen, ALU.mult))
            for p in range(MAXPASS):
                ins = v.tensor_scalar(et(posm, p), el, -1.0 - p * SLOTS, None, ALU.add)
            link(ins)
            dve.sem_inc(route_ok, 1)
            link(v.tensor_reduce(cnt[:, 0:1], ps[4][:, 0:32], AX_X, ALU.max))
            link(v.tensor_scalar(cnt[:, 1:2], cnt[:, 0:1], 1.0 / SLOTS, (SLOTS - 1) / SLOTS - 0.5 + 1 / 128, ALU.mult,
                                 ALU.add))
            v.tensor_copy(npi[0:1, 0:1], cnt[0:1, 1:2]).then_inc(np_ok, 1)
            dve.wait_ge(np_ok, 1)
            npass = dve.value_load(npi[0:1, 0:1], min_val=1, max_val=MAXPASS)
            dve.wait_ge(y0_ok, 1)
            dve.sem_inc(hid_done, 2)
            dve.sem_inc(y_ev, 2)

            def one_hot(q, j):
                dve.wait_ge(got, j + 1 + q * QUAD)
                if j >= 2:
                    dve.wait_ge(ohw_ready, j - 1 + q * QUAD)
                at = bass.ds(q * (QUAD * TT) + j * TT, TT) if not isinstance(q, int) else slice(j * TT, (j + 1) * TT)
                v.tensor_tensor(OH[:, j % 2, :, :], iota64[:, :].unsqueeze(1).to_broadcast([P, TT, SLOTS]),
                                posm[:, at].unsqueeze(2).to_broadcast([P, TT, SLOTS]),
                                ALU.is_equal).then_inc(oh_ready, 1)

            one_hot(0, 0)
            one_hot(0, 1)
            with dve.Fori(0, npass * N_QUADS) as q:
                for j in range(QUAD):
                    one_hot(q, j + 2)
                    dve.wait_ge(sg_done, j + 1 + q * QUAD)
                    dve.wait_ge(moe_used, QUAD_TILES + (DN_END[j - 2] if j >= 2 else DN_END[j + 2] - QUAD_TILES)
                                + q * QUAD_TILES)
                    v.tensor_tensor(hid[:, j % 2, :, :], sg[:, j % 2, :].rearrange("p (f s) -> p f s", f=2),
                                    ps[2 + j % 2][:, 2 * SLOTS:4 * SLOTS].rearrange("p (f s) -> p f s", f=2),
                                    ALU.mult).then_inc(hid_done, 1)
                for n in range(KT):
                    dve.wait_ge(y_full, n + 2 + q * KT)
                    v.tensor_tensor(RD[:, n, :], RD[:, n, :], ps[6 + n % 2][:, :], ALU.add).then_inc(y_ev, 1)
                dve.wait_ge(y_ev, KT + 2 + q * KT)
            for k in range(KT):
                v.scalar_tensor_tensor(RA[:, k, :], RD[:, k, :], mod[:, 40 + k:41 + k], RA[:, k, :], ALU.mult,
                                       ALU.add).then_inc(x1_ok, 1)
            dve.wait_ge(x1_ok, 2 * KT)
            dve.wait_ge(rinv_ok, 5)
            for k in range(KT):
                v.scalar_tensor_tensor(RA[:, k, :], RA[:, k, :], V("g_final", k), RINV[:, :], ALU.mult,
                                       ALU.mult).then_inc(x2_ok, 1)
            dve.wait_ge(x2_ok, KT)
            dve.sem_inc(rinv_used, 1)
            dve.wait_ge(delta_ok, 1)
            di = OTK[:, 0, :].bitcast(I32)
            dj = OTK[:, 1, :].bitcast(I32)
            df = RH[:, 2, :]
            for m, (mask, op) in enumerate(((3, 0), (15, 0))):
                link(v.tensor_scalar(dj, di, mask, None, ALU.bitwise_and))
                link(v.tensor_copy(df, dj))
                link(v.tensor_scalar(RH[:, 3 + m, :], df, 0.0, None, ALU.is_equal))
            link(v.tensor_scalar(lnm, delta, 128.0, None, ALU.is_le))
            link(v.tensor_tensor(lnm, lnm, RH[:, 3, :], ALU.add))
            link(v.tensor_tensor(lnm, lnm, RH[:, 4, :], ALU.add))
            link(v.tensor_scalar(df, delta, 0.0, None, ALU.is_ge))
            link(v.tensor_tensor(df, df, lnm, ALU.mult))
            link(v.tensor_scalar(lnm, df, 0.0, NEG, ALU.is_equal, ALU.mult))
            link(v.tensor_scalar(RH[:, 3, :], df, 2.0, float(np.log(2.0)), ALU.is_equal, ALU.mult))
            link(v.tensor_scalar(RH[:, 4, :], df, 3.0, float(np.log(3.0)), ALU.is_equal, ALU.mult))
            link(v.tensor_tensor(lnm, lnm, RH[:, 3, :], ALU.add))
            link(v.tensor_tensor(lnm, lnm, RH[:, 4, :], ALU.add))
            dve.sem_inc(lnm_ok, 1)
            for i in range(24):
                if i % 2 == 0:
                    evict(PE_Q2 + i, q2_dst(i))
            attend(2)
            attend(3)
            dve.wait_ge(pv_done, 4 * NU)
            link(v.memset(convbuf[0][:, 0:3], 0.0))
            link(v.memset(convbuf[1][:, 0:3], 0.0))
            for i in range(12):
                buf = convbuf[i % 2]
                tile = RG[:, i, :] if i < 8 else RF[:, i - 8, :]
                dve.wait_ge(ev[i % 2], PE_XBC // 2 + i // 2 + 1)
                link(v.tensor_scalar(tile, buf[:, 0:T], V("conv_w", 4 * i), V("conv_b", i), ALU.mult, ALU.add))
                for w in range(1, 4):
                    ins = v.scalar_tensor_tensor(tile, buf[:, w:w + T], V("conv_w", 4 * i + w), tile, ALU.mult, ALU.add)
                    if w < 3:
                        link(ins)
                ins.then_inc(conv_ok, 1)
            dve.wait_ge(dt_full, 1)
            link(v.tensor_tensor(dt_t, ps[0][:, 0:64].rearrange("p (t h) -> p t h", t=TT),
                                 rows[:, R_DTB:R_DTB + 16].unsqueeze(1).to_broadcast([P, TT, 16]), ALU.add))
            link(v.scalar_tensor_tensor(tmp_t, dt_t, -1.0, dt_t, ALU.mult, ALU.min))
            link(v.tensor_scalar(dt_t, dt_t, 0.0, None, ALU.max))
            dve.sem_inc(sp1, 1)
            dve.wait_ge(sp2, 2)
            link(v.tensor_tensor(dt_t, dt_t, tmp_t, ALU.add))
            link(v.scalar_tensor_tensor(adt_t, dt_t, -1.0, aneg.unsqueeze(1).to_broadcast([P, TT, 16]), ALU.mult,
                                        ALU.mult))
            dve.sem_inc(adt_ok, 1)
            for i in range(8):
                if i % 2 == 0:
                    e = PE_XT + i
                    evict(e, ([(RCf[:, (i // 2) * D:(i // 2) * D + T], bank(e)[:, :])], 1.0))
            evict(PE_BT, ([(b_tok[:, 0, :, :], quad(bank(PE_BT)[:, :]))], 1.0))
            dve.wait_ge(cs_full, 1)
            link(v.tensor_copy(cs_t, ps[1][:, 0:64].rearrange("p (t h) -> p t h", t=TT)))
            link(v.tensor_copy(tot_t, ps[1][:, 64:128].rearrange("p (t h) -> p t h", t=TT)))
            link(v.tensor_tensor(tmp_t, tot_t, cs_t, ALU.subtract))
            dve.sem_inc(cs_ok, 1)
            dve.wait_ge(sp2, 3)

            def heads(ap, o=0, n=8):
                return ap[:, o:o + n].unsqueeze(2).to_broadcast([P, n, 64])

            def h8(ap):
                return ap.rearrange("p (h c) -> p h c", h=8)

            for c in range(TT):
                dve.wait_ge(cb_full, c + 1)
                if c > 0:
                    dve.wait_ge(mm_ok, 4 * c)
                v.tensor_tensor(cbm, ps[0][:, 0:256].rearrange("p (g l) -> p g l", g=2),
                                upper[:, :].unsqueeze(1).to_broadcast([P, 2, P]), ALU.mult).then_inc(cb_ok, 1)
                if c > 0:
                    dve.wait_ge(yd_full, c)
                for q in range(4):
                    dve.wait_ge(csb_full, 4 * c + q + 1)
                    for h in range(4):
                        ins = v.tensor_scalar(decay[:, 4 * q + h, :], ps[2 + q % 2][:, h * P:(h + 1) * P],
                                              cs_t[:, c, 4 * q + h:4 * q + h + 1], 0.0, ALU.subtract, ALU.min)
                    ins.then_inc(dd_ok, 1)
                dve.wait_ge(skip_ok, c + 1)
                dve.wait_ge(yd_full, c + 1)
                for g in range(2):
                    yt = y_tokT[:, c, 8 * g:8 * g + 8, :]
                    ins = v.tensor_tensor(yt, yt, h8(ps[4 + g][:, :]), ALU.add)
                link(ins)
                if c > 0:
                    dve.wait_ge(yo_full, c)
                    for g in range(2):
                        ins = v.tensor_tensor(y_off[:, 8 * g:8 * g + 8, :], h8(ps[g][:, :]),
                                              heads(sd_t[:, c, :], 8 * g), ALU.mult)
                    link(ins)
                    link(v.tensor_tensor(y_tokT[:, c, :, :], y_tokT[:, c, :, :], y_off, ALU.add))
                dve.sem_inc(y_tok, 1)
                if c < TT - 1:
                    dve.wait_ge(st_full, c + 1)
                    for g in range(2):
                        sv = h8(state[:, g, :])
                        if c == 0:
                            ins = v.tensor_copy(sv, h8(ps[6 + g][:, :]))
                        else:
                            link(v.tensor_tensor(sv, sv, heads(dec_t[:, c, :], 8 * g), ALU.mult))
                            ins = v.tensor_tensor(sv, sv, h8(ps[6 + g][:, :]), ALU.add)
                    link(ins)
                    dve.sem_inc(state_ok, 1)
            for i in range(8):
                if i % 2 == 0:
                    e = PE_YT + i
                    evict(e, ([(RG[:, 0:4, (i // 2) * P:(i // 2 + 1) * P], quad(bank(e)[:, :]))], 1.0))
            for idx, reg, g in ((6, RB, "att_g"), (7, RG, "ssm_g")):
                dve.wait_ge(rinv_ok, idx)
                for k in range(KT):
                    v.scalar_tensor_tensor(reg[:, k, :], reg[:, k, :], V(g, k), RINV[:, :], ALU.mult,
                                           ALU.mult).then_inc(mixn, 1)
                dve.wait_ge(mixn, KT * (idx - 5))
                dve.sem_inc(rinv_used, 1)
            for i in range(KT):
                e = PE_OUT + i
                dve.wait_ge(acc, e + 1)
                v.scalar_tensor_tensor(RA[:, i, :], RA[:, i, :], ALPHA, bank(e)[:, :], ALU.mult,
                                       ALU.add).then_inc(r_ok, 1)
                dve.wait_ge(r_ok, i + 1)
                dve.sem_inc(ev[e % 2], 1)
            dve.wait_ge(mu_full, 1)
            for k in range(KT):
                v.scalar_tensor_tensor(RC[:, k, :], ps[4][:, :], -1.0 / D, RA[:, k, :], ALU.mult,
                                       ALU.add).then_inc(cen_ok, 1)
            dve.wait_ge(cen_ok, KT)
            dve.wait_ge(rinv_ok, 8)
            for k in range(KT):
                link(v.scalar_tensor_tensor(RC[:, k, :], RC[:, k, :], V("ln_g", k), RINV[:, :], ALU.mult, ALU.mult))
                v.tensor_scalar(RC[:, k, :], RC[:, k, :], V("ln_b", k), None, ALU.add).then_inc(fin_ok, 1)

        @block.gpsimd
        def _(pool):
            g = nc.gpsimd
            links = [0]

            def link(ins):
                links[0] += 1
                ins.then_inc(pool_c, 1)
                pool.wait_ge(pool_c, links[0])

            link(g.memset(ones[:, :], 1.0))
            link(g.memset(ident[:, :], 0.0))
            g.memset(eps1, EPS1)
            g.memset(eps2, EPS2)
            link(g.affine_select(out=ident[:, :], in_=ident[:, :], compare_op=ALU.not_equal, fill=1.0, base=0,
                                 pattern=[[-1, P]], channel_multiplier=1))
            link(g.affine_select(out=upper[:, :], in_=ones[:, :], compare_op=ALU.is_ge, fill=0.0, base=0,
                                 pattern=[[1, P]], channel_multiplier=-1))
            g.memset(flip[:, :], 0.0).then_inc(flip_ev, 1)
            pool.wait_ge(flip_ev, 1)
            link(g.affine_select(out=flip[:, :], in_=flip[:, :], compare_op=ALU.not_equal, fill=1.0, base=1 - P,
                                 pattern=[[1, P]], channel_multiplier=1))
            pool.sem_inc(consts, 1)
            g.iota(iota64[:, :], [[1, SLOTS]], base=0, channel_multiplier=0, allow_small_or_imprecise_dtypes=True)
            pool.wait_ge(rev_in, 16)
            g.tensor_copy(ext_row[:, 0:255], ext_row[:, 255:256].to_broadcast([HG, 255])).then_inc(ext_ok, 1)
            link(g.memset(MASK[:, :], 0.0))
            g.memset(MASK[0:64, 448:512], NEG)
            g.memset(RD[96:128, 0:8:2, :], 0.0)
            g.memset(RD[0:32, 1:8:2, :], 0.0)
            g.memset(RE[96:128, 0:8:2, :], 0.0)
            link(g.memset(RE[0:32, 1:8:2, :], 0.0))
            pool.sem_inc(zero_ok, 1)
            for k in range(KT):
                pool.wait_ge(mod_h, k + 1)
                g.tensor_scalar(RB[:, k, :], RB[:, k, :], mod[:, k:k + 1], None, ALU.add).then_inc(h_ok, 1)
            pool.wait_ge(flip_ev, HG + 1)
            g.memset(RG[0:64, :, 448:512], NEG).then_inc(bias_ok, 1)
            for k in range(KT):
                pool.wait_ge(mod_h, KT + k + 1)
                g.tensor_scalar(RB[:, k, :], RB[:, k, :], mod[:, 24 + k:25 + k], None, ALU.add).then_inc(h_ok, 1)
            pool.wait_ge(pv_done, 2 * NU)
            link(g.memset(RD[:, :, :], 0.0))
            pool.sem_inc(y0_ok, 1)
            pool.wait_ge(route_ok, 1)
            pool.wait_ge(np_ok, 1)
            npass = pool.value_load(npi[0:1, 0:1], min_val=1, max_val=MAXPASS)
            with pool.Fori(0, npass * N_QUADS) as q:
                for j in range(QUAD):
                    at = bass.ds(q * (QUAD * TT) + j * TT, TT)
                    if j % 2 == 0:
                        pool.wait_ge(st_t, j // 2 + 1 + q * 2)
                    pool.wait_ge(oh_ready, j + 1 + q * QUAD)
                    o = (j % 2) * SLOTS
                    g.tensor_tensor(OHW[:, j // 2, :, o:o + SLOTS], OH[:, j % 2, :, :],
                                    combr[:, at].unsqueeze(2).to_broadcast([P, TT, SLOTS]),
                                    ALU.mult).then_inc(ohw_ready, 1)
            pool.wait_ge(x2_ok, KT)
            g.iota(delta, [[-1, T]], base=T - P, channel_multiplier=1, allow_small_or_imprecise_dtypes=True)
            g.iota(OTK[:, 0, :].bitcast(I32), [[-1, T]], base=2 * T - P, channel_multiplier=1).then_inc(delta_ok, 1)
            pool.wait_ge(lnm_ok, 1)
            for h in range(2 * HG):
                if h >= HG:
                    pool.wait_ge(biased, 2 * NU + 24 + h - HG + 1)
                link(g.tensor_scalar(RG[:, h % HG, :], delta, -float(2.0 ** (-8.0 * (h + 1) / 16)), None, ALU.mult))
                g.tensor_tensor(RG[:, h % HG, :], RG[:, h % HG, :], lnm, ALU.add).then_inc(bias_ok, 1)
            for t in range(TT):
                pool.wait_ge(ev[0], (PE_XT + 2 * t) // 2 + 1)
                pool.wait_ge(ev[1], (PE_XT + 2 * t) // 2 + 1)
                pool.wait_ge(adt_ok, 1)
                g.tensor_tensor(xg_tok[:, t, :, :], xs_tok[:, t, :, :],
                                dt_t[:, t, :].unsqueeze(2).to_broadcast([P, SSM_H, SSM_P]), ALU.mult).then_inc(xg_ok, 1)
                g.tensor_tensor(y_tokT[:, t, :, :], xs_tok[:, t, :, :],
                                rows[:, R_DSKIP:R_DSKIP + 16].unsqueeze(2).to_broadcast([P, SSM_H, SSM_P]),
                                ALU.mult).then_inc(skip_ok, 1)
            pool.wait_ge(xg_ok, TT)
            pool.wait_ge(sp2, 3)
            for c in range(TT):
                if c < TT - 1:
                    if c > 0:
                        pool.wait_ge(st_full, c)
                    g.tensor_tensor(xgd, xg_tok[:, c, :, :],
                                    dte_t[:, c, :].unsqueeze(2).to_broadcast([P, SSM_H, SSM_P]),
                                    ALU.mult).then_inc(xgd_ok, 1)
                pool.wait_ge(cb_ok, c + 1)
                for q in range(4):
                    pool.wait_ge(ee_ok, 4 * c + q + 1)
                    g.tensor_tensor(decay[:, 4 * q:4 * q + 4, :], decay[:, 4 * q:4 * q + 4, :],
                                    cbm[:, q // 2, :].unsqueeze(1).to_broadcast([P, 4, P]), ALU.mult).then_inc(mm_ok, 1)
            pool.wait_ge(ev[0], PE_ZA // 2)
            pool.wait_ge(ev[1], PE_ZA // 2)
            for i in range(16):
                e = PE_ZA + i
                tile = RB[:, i, :] if i < KT else RG[:, i - KT, :]
                pool.wait_ge(ev[e % 2], e // 2 + 1)
                g.tensor_tensor(tile, tile, zbuf(i), ALU.mult).then_inc(mixp, 1)


def _tiles(w):
    m = w.shape[1] // P
    return w.reshape(KT, P, m, P).transpose(2, 1, 0, 3).reshape(m, P, D)


def _cols(v):
    return v.reshape(-1, P).T


def kernel(**inputs):
    import concourse.bacc as bacc
    from concourse.bass_utils import run_bass_kernel_spmd as run

    a = {k: np.ascontiguousarray(v) for k, v in inputs.items()}
    w_in = a["w_in"][0]
    swap = np.r_[16:32, 0:16]
    kr = 384 + np.arange(32)
    kr_cols = np.r_[kr, kr[swap], kr, kr[swap]]
    s1 = _tiles(np.concatenate([w_in[:, 0:384], w_in[:, kr_cols], w_in[:, 416:1952]], 1))
    ada = _tiles(a["w_ada"][0])
    uq = a["w_uq"][0]
    head = np.arange(8)[:, None] * 96
    nope = (head + np.arange(64)).reshape(4, P)
    rope_a = (head + 64 + np.arange(32)).reshape(2, P)
    rope_b = (head + 64 + swap).reshape(2, P)
    uq_cols = np.concatenate([nope, rope_a[0:1], rope_b[0:1], rope_a[1:2], rope_b[1:2]]).reshape(-1)
    uq_t = uq[:, uq_cols].reshape(2, P, 2, 4, P).transpose(2, 1, 3, 0, 4).reshape(2, P, D)
    ukv = np.concatenate([a["w_uk"][0], a["w_uv"][0]], 1)[None]
    ga, gb = _tiles(w_in[:, 1952:2976]), _tiles(w_in[:, 2976:4000])
    oab = _tiles(np.concatenate([a["w_oa"][0], a["w_ob"][0]], 0))
    first = [ada[0:16]]
    for i in range(16):
        first += [s1[i:i + 1], ada[16 + 2 * i:18 + 2 * i]]
    first += [uq_t, ukv]
    for i in range(KT):
        first += [ga[i:i + 1], gb[i:i + 1], oab[i:i + 1]]
    first += [_tiles(a["w_out"][0])]
    pre = np.concatenate(first, 0)
    moe = np.empty((N_QUADS, QUAD_TILES, P, D), np.float32)
    for j in range(QUAD):
        gate = a["w_gate"][0][j::QUAD].reshape(N_QUADS, KT, P, 2, P).transpose(0, 3, 2, 1, 4).reshape(N_QUADS, 2, P, D)
        up = a["w_up"][0][j::QUAD].reshape(N_QUADS, KT, P, 2, P).transpose(0, 3, 2, 1, 4).reshape(N_QUADS, 2, P, D)
        moe[:, GU_AT[j]:GU_AT[j] + 2] = gate
        moe[:, GU_AT[j] + 2:GU_AT[j] + 4] = up
        moe[:, DN_AT[j]:DN_AT[j] + 2] = a["w_down"][0][j::QUAD].reshape(N_QUADS, 2, P, D)
    moe = moe.reshape(-1, P, D)
    w2 = a["w_in_2"][0]
    out2 = a["w_out_2"][0]
    pair = np.stack([_tiles(out2[0:D]), _tiles(out2[D:2 * D])], 1).reshape(-1, P, D)
    post = np.concatenate([_tiles(w2[:, 0:3072]), _tiles(w2[:, 5120:6656]), _tiles(w2[:, 3072:5120]), pair], 0)
    w_rt = np.concatenate([a["w_rg"][0], a["w_re"][0]], 1).reshape(KT, P, 36).transpose(1, 0, 2)
    w_dt = w2[:, 6656:6672].reshape(KT, P, 16).transpose(1, 0, 2)
    inv = (10000.0 ** (-np.arange(16, dtype=np.float32) / np.float32(16))).astype(np.float32)
    parts = {"c": _cols(a["c"][0]), "b_ada": _cols(a["b_ada"][0]), "g_mix": _cols(a["g_mix"][0]),
             "g_ffn": _cols(a["g_ffn"][0]), "g_final": _cols(a["g_final"]), "g_q": _cols(a["g_q"][0]),
             "g_kv": _cols(a["g_kv"][0]),
             "conv_w": a["conv_w_2"][0].reshape(4, 12, P).transpose(2, 1, 0).reshape(P, 48),
             "conv_b": _cols(a["conv_b_2"][0]), "att_g": _cols(a["att_norm_g_2"][0]),
             "ssm_g": _cols(a["ssm_norm_g_2"][0]), "ln_g": _cols(a["ln_g_2"][0]), "ln_b": _cols(a["ln_b_2"][0]),
             "inv": np.tile(inv, 8)[:, None], "sign": np.tile(np.repeat(np.float32([-1, 1]), 16), 4)[:, None]}
    vec = np.concatenate([parts[n] for n, _ in V_NAMES], 1)
    rows = np.concatenate([a["b_rg"][0], a["b_re"][0], a["dt_bias_2"][0], a["a_log_2"][0], a["d_skip_2"][0]])
    rel = a["rel_bias"][0][:, ::-1]
    arrays = {"xT": a["x"][0].T, "vec": vec, "rows": rows, "pos": a["positions"][0], "rel": rel, "w_rt": w_rt,
              "w_dt": w_dt, "w_pre": pre, "w_moe": moe, "w_post": post}
    nc = bacc.Bacc("TRN2", target_bir_lowering=False, num_devices=1)
    args = []
    for name in arrays:
        arrays[name] = np.ascontiguousarray(arrays[name])
        args.append(nc.dram_tensor(f"in_{name}", arrays[name].shape, mybir.dt.from_np(arrays[name].dtype),
                                   kind="ExternalInput").ap())
    args.append(nc.dram_tensor("outT", (D, T), F32, kind="ExternalOutput").ap())
    build(nc, *args)
    r = run(nc, [{f"in_{n}": v for n, v in arrays.items()}], core_ids=[0])
    return np.ascontiguousarray(r.results[0]["outT"].T)[None]
```

```python
from contextlib import ExitStack

import numpy as np

import concourse.bass as bass
from concourse import mybir

F32 = mybir.dt.float32
I32 = mybir.dt.int32
ALU = mybir.AluOpType
ACT = mybir.ActivationFunctionType
AX_X = mybir.AxisListType.X

P = 128
T = 512
TT = T // P
D = 1024
KT = D // P
RING = 12
HG = 8
EPS1, EPS2 = 1e-6, 1e-5
NEG = -1e30
MLA_SCALE = 96 ** -0.5
N_EXP, SLOTS = 32, 64
MAXPASS = T // SLOTS
MAX_QUADS = 12
ALPHA = 2.0 ** 0.25
SSM_H, SSM_P = 16, 64

N_PRE = 16 + 48 + 3 + 24 + 8
PAIR_TILES = 12
N_POST = 8 * 3 + 12 + 8 + 8 + 16

V_NAMES = [("c", 8), ("b_ada", 48), ("g_mix", 8), ("g_ffn", 8), ("g_final", 8), ("g_q", 2), ("g_kv", 1),
           ("conv_w", 48), ("conv_b", 12), ("att_g", 8), ("ssm_g", 8), ("ln_g", 8), ("ln_b", 8),
           ("inv", 1), ("sign", 1)]
V_AT, _n = {}, 0
for _name, _k in V_NAMES:
    V_AT[_name] = _n
    _n += _k
NV = _n
R_BR, R_DTB, R_ALOG, R_DSKIP, NR = 0, 36, 52, 68, 84
TWO_PI = 2 * np.pi
C1 = 6.28125
C2 = float(np.float32(np.float32((TWO_PI - C1) * 2 ** 22).astype(np.int64) // 4096 * 4096) / 2 ** 22)
C3 = float(TWO_PI - C1 - C2)
ROUND = 12582912.0


def build(nc, xT_d, vec_d, rows_d, pos_d, rel_d, wr_d, wdt_d, pre_d, moe_d, post_d, out_d):
    ctx = ExitStack()
    with ctx:
        def sb(name, shape, dt=F32):
            return ctx.enter_context(nc.sbuf_tensor(name, shape, dt))

        def sem(name):
            return ctx.enter_context(nc.semaphore(name))

        ring = sb("ring", [P, RING, D])
        RA = sb("RA", [P, KT, T])
        RB = sb("RB", [P, KT, T])
        RC = sb("RC", [P, KT, T])
        RD = sb("RD", [P, KT, T])
        RE = sb("RE", [P, KT, T])
        RF = sb("RF", [P, KT, T])
        RG = sb("RG", [P, KT, T])
        RH = sb("RH", [P, KT, T])
        SB = sb("SB", [P, 2, T])
        PB = sb("PB", [P, 2, T])
        PTB = sb("PTB", [P, 2, T])
        OTK = sb("OTK", [P, 2, T])
        SQ = sb("SQ", [P, 2, T])
        RINV = sb("RINV", [P, T])
        MASK = sb("MASK", [P, T])
        ident = sb("ident", [P, P])
        ones = sb("ones", [P, P])
        upper = sb("upper", [P, P])
        flip = sb("flip", [P, P])
        vec = sb("vec", [P, NV])
        rows = sb("rows", [P, NR])
        small = sb("small", [P, 256])
        w_r = sb("w_r", [P, KT, 36])
        wdt = sb("wdt", [P, KT, 16])
        iota64 = sb("iota64", [P, SLOTS])
        nqi = sb("nqi", [1, 1], I32)
        units = sb("units", [1, 2, SLOTS], I32)
        sel = sb("sel", [P, 8])
        ps = [ctx.enter_context(nc.psum_tensor(f"ps{i}", [P, T], F32)) for i in range(8)]
        ext_d = nc.dram_tensor("ext_scratch", [HG, 640], F32, kind="Internal").ap()

        cact = small[:, 0:8]
        mod = small[:, 8:56]
        A1 = small[:, 56:64]
        A2 = small[:, 64:72]
        gt1h = small[:, 72:80]
        rowsum = small[:, 80:96]
        rsinv = small[:, 96:112]
        eps1 = small[:, 112:113]
        eps2 = small[:, 113:114]
        cnt = small[:, 114:118]
        aneg = small[:, 120:136]


        def nmax(n):
            return small[:, 140 + n % 4:141 + n % 4]

        def zbuf(i):
            return (SB, PB)[i % 4 // 2][:, i % 2, :]

        ext_row = PTB[0:HG, :, :].rearrange("p a b -> p (a b)")[:, 0:640]
        cosT, sinT = PB[:, 0, :], PB[:, 1, :]
        qlT, kvT, krT = RH[:, 0:2, :], RH[:, 2, :], RH[:, 3, :]
        qnT, kvnT = RH[:, 4:6, :], RH[:, 6, :]
        qbT, kbT = RC[:, 0:4, :], RC[:, 4:8, :]
        vb, va = RF[:, 0:4, :], RF[:, 4:8, :]
        oaT, obT = RH[:, 0:4, :], RH[:, 4:8, :]
        RCf = RC[:, :, :].rearrange("p a b -> p (a b)")
        REf = RE[:, :, :].rearrange("p a b -> p (a b)")
        RFf = RF[:, :, :].rearrange("p a b -> p (a b)")
        RDf = RD[:, :, :].rearrange("p a b -> p (a b)")
        RHf = RH[:, :, :].rearrange("p a b -> p (a b)")
        RGf = RG[:, :, :].rearrange("p a b -> p (a b)")
        h2tok = RCf.rearrange("p (t d) -> p t d", t=TT)
        posm = RFf[:, 0:(MAXPASS * N_EXP + 1) * TT]
        combr = RFf[:, 1040:1040 + N_EXP * TT]
        Zs = RFf[:, 2048:4096].rearrange("p (a d) -> p a d", a=2)
        OH = REf[:, 0:1024].rearrange("p (a t s) -> p a t s", a=2, t=TT)
        OHW = REf[:, 1024:2048].rearrange("p (a t s) -> p a t s", a=2, t=TT)
        St = REf[:, 2048:3072].rearrange("p (a x) -> p a x", a=2)
        hid = REf[:, 3072:3584].rearrange("p (a f) -> p a f", a=2)
        hidT = REf[:, 3584:4096].rearrange("p (a f s) -> p a f s", a=2, f=2)
        Xg = RHf[:, 0:2048].rearrange("p (a k s) -> p a k s", a=2, k=KT)
        sg = RHf[:, 2048:2560].rearrange("p (a x) -> p a x", a=2)
        ranked = OTK[:, 1, 384:512].rearrange("p (a u) -> p a u", a=2)
        chosen = OTK[:, 0, 0:TT * N_EXP].rearrange("p (t e) -> p t e", t=TT)
        xs_tok, xg_tok, y_tokT = (r.rearrange("p (t h c) -> p t h c", t=TT, h=SSM_H) for r in (RCf, RHf, RDf))
        decay = REf[:, 0:2048].rearrange("p (h l) -> p h l", h=SSM_H)
        xgd = REf[:, 2048:3072].rearrange("p (h c) -> p h c", h=SSM_H)
        y_off = REf[:, 3072:4096].rearrange("p (h c) -> p h c", h=SSM_H)
        convbuf = [REf[:, 0:T + 3], REf[:, 1024:1024 + T + 3]]
        b_tok = RFf[:, 2048:3072].rearrange("p (g t n) -> p g t n", g=2, t=TT)
        state = RFf[:, 3072:4096].rearrange("p (g x) -> p g x", g=2)
        dt_t, cs_t, tot_t, adt_t, sd_t, dte_t, dec_t, tmp_t = (
            MASK[:, i * 64:(i + 1) * 64].rearrange("p (t h) -> p t h", t=TT) for i in range(8))
        cbm = OTK[:, 0, 0:256].rearrange("p (g l) -> p g l", g=2)
        delta, lnm = RH[:, 0, :], RH[:, 1, :]
        v2 = REf.rearrange("p (t d) -> p t d", t=TT)

        w_in = [sem(f"w_in{n}") for n in range(RING)]
        w_in2 = [sem(f"w_in2_{n}") for n in range(RING)]
        ada_done = sem("ada_done")
        moe_used = sem("moe_used")
        dn_half = sem("dn_half")
        ht_done = sem("ht_done")
        ht_ev = sem("ht_ev")
        cnt_full = sem("cnt_full")
        flag_ok = sem("flag_ok")
        rank_full = sem("rank_full")
        rank_ok = sem("rank_ok")
        list_full = sem("list_full")
        x_in = sem("x_in")
        c_in = sem("c_in")
        wr_in = sem("wr_in")
        wdt_in = sem("wdt_in")
        rev_in = sem("rev_in")
        ext_out = sem("ext_out")
        bias_in = sem("bias_in")
        consts = sem("consts")
        cact_ok = sem("cact_ok")
        sq_ready = sem("sq_ready")
        sq_used = sem("sq_used")
        rinv_ok = sem("rinv_ok")
        rinv_used = sem("rinv_used")
        h_ok = sem("h_ok")
        acc = sem("acc")
        ev = [sem("ev0"), sem("ev1")]
        lat_n = sem("lat_n")
        lat_ok = sem("lat_ok")
        s_full = sem("s_full")
        biased = sem("biased")
        p_ready = sem("p_ready")
        pt_full = sem("pt_full")
        pt_ready = [sem("pt_ready0"), sem("pt_ready1")]
        pv_done = sem("pv_done")
        o_ready = sem("o_ready")
        bias_ok = sem("bias_ok")
        g_used = sem("g_used")
        g_tanh = sem("g_tanh")
        g_done = sem("g_done")
        x1_ok = sem("x1_ok")
        lg_full = sem("lg_full")
        mask_ok = sem("mask_ok")
        pos_full = sem("pos_full")
        route_ok = sem("route_ok")
        list_ok = sem("list_ok")
        oh_ready = sem("oh_ready")
        ohw_ready = sem("ohw_ready")
        got = sem("got")
        st_t = sem("st_t")
        x_ev = sem("x_ev")
        sg_done = sem("sg_done")
        hid_done = sem("hid_done")
        z_ev = sem("z_ev")
        st_ev = sem("st_ev")
        y_full = sem("y_full")
        y_ev = sem("y_ev")
        x2_ok = sem("x2_ok")
        lnm_ok = sem("lnm_ok")
        dt_full = sem("dt_full")
        mod_ok = sem("mod_ok")
        rope_ok = sem("rope_ok")
        ang_ok = sem("ang_ok")
        pos_in = sem("pos_in")
        mask_mem = sem("mask_mem")
        lat_raw = sem("lat_raw")
        ropeb = sem("ropeb")
        zero_ok = sem("zero_ok")
        y0_ok = sem("y0_ok")
        ext_ok = sem("ext_ok")
        h2t_ok = sem("h2t_ok")
        sp1 = sem("sp1")
        sp2 = sem("sp2")
        xg_ok = sem("xg_ok")
        yd_full = sem("yd_full")
        yo_full = sem("yo_full")
        st_full = sem("st_full")
        mixp = sem("mixp")
        ba_base = sem("ba_base")
        bias_used = sem("bias_used")
        adt_ok = sem("adt_ok")
        conv_in = sem("conv_in")
        conv_ok = sem("conv_ok")
        xbc_ok = sem("xbc_ok")
        cs_full = sem("cs_full")
        cs_ok = sem("cs_ok")
        cb_full = sem("cb_full")
        cb_ok = sem("cb_ok")
        csb_full = sem("csb_full")
        dd_ok = sem("dd_ok")
        ee_ok = sem("ee_ok")
        mm_ok = sem("mm_ok")
        xgd_ok = sem("xgd_ok")
        yst_full = sem("yst_full")
        state_ok = sem("state_ok")
        y_tok = sem("y_tok")
        zt_ok = sem("zt_ok")
        mixn = sem("mixn")
        r_ok = sem("r_ok")
        mod_h = sem("mod_h")
        sel_ok = sem("sel_ok")
        flip_full = sem("flip_full")
        flip_ev = sem("flip_ev")
        delta_ok = sem("delta_ok")
        skip_ok = sem("skip_ok")
        cen_ok = sem("cen_ok")
        mu_full = sem("mu_full")
        fin_ok = sem("fin_ok")
        out_done = sem("out_done")
        dve_c, act_c, pool_c = sem("dve_chain"), sem("act_chain"), sem("pool_chain")

        def V(name, i=0, n=1):
            return vec[:, V_AT[name] + i:V_AT[name] + i + n]

        def slot(n):
            return ring[:, n % RING, :]

        def freed_pre(n):
            if n < 16:
                return ada_done, n + 1
            if n < 64:
                i, r = (n - 16) // 3, (n - 16) % 3
                return (acc, PE_S1 + i + 1) if r == 0 else (ada_done, 16 + 2 * i + r)
            if n < 67:
                return acc, PE_U + (4, 8, 16)[n - 64]
            if n < 91:
                return g_used, n - 66
            return acc, PE_O + n - 90

        def freed_post(n):
            for first, count, e in ((0, 24, PE_Q2), (24, 12, PE_XBC), (36, 16, PE_ZA)):
                if first <= n < first + count:
                    return acc, e + n - first + 1
            return acc, PE_OUT + (n - 52) // 2 + 1

        PE_S1 = 0
        PE_U = PE_S1 + 16
        PE_OT = PE_U + 16
        PE_O = PE_OT + 8
        PE_H = PE_O + 8
        PE_Q2 = PE_H + 8
        PE_OT2 = PE_Q2 + 24
        PE_XBC = PE_OT2 + 8
        PE_XT = PE_XBC + 12
        PE_BT = PE_XT + 8
        PE_YT = PE_BT + 2
        PE_ZA = PE_YT + 8
        PE_ZS = PE_ZA + 8
        PE_OUT = PE_ZS + 8
        assert all(e % 2 == 0 for e in (PE_U, PE_OT, PE_O, PE_H, PE_Q2, PE_OT2, PE_XBC, PE_XT, PE_BT, PE_YT, PE_ZA))

        def bank(e):
            return ps[6 + e % 2]

        def half(ap, h):
            return ap[(h % 2) * 64:(h % 2) * 64 + 64, h // 2, :]

        bias_hc = RG

        def group_ops(g):
            if g == 0:
                return (lambda h, t: half(qbT, h)[:, t * P:(t + 1) * P], lambda h, w: half(kbT, h)[:, 0:w],
                        lambda h, j: vb[:, j, h * 64:h * 64 + 64], lambda h: bias_hc[:, h, :])
            if g == 1:
                return (lambda h, t: RD[:, h, t * P:(t + 1) * P], lambda h, w: RE[:, h, 0:w],
                        lambda h, j: va[:, j, h * 64:h * 64 + 64], lambda h: MASK[:, :])
            o = (g - 2) * HG
            return (lambda h, t: half(RC, h + o)[:, t * P:(t + 1) * P], lambda h, w: half(RD, h + o)[:, 0:w],
                    lambda h, j: v2[:, j, (h + o) * 64:(h + o) * 64 + 64], lambda h: bias_hc[:, h, :])

        OT_DST = [obT, oaT, RB[:, 0:4, :], RB[:, 4:8, :]]
        UNITS = [(t, h) for t in range(TT) for h in range(HG)]
        NU = len(UNITS)

        def ot_event(g, t):
            return (PE_OT if g < 2 else PE_OT2) + (g % 2) * TT + t

        ST_H1, ST_Q, ST_KV, ST_H2 = 0, 8, 10, 11
        ST_F, ST_AT, ST_SS, ST_VAR = 19, 27, 35, 43

        block = ctx.enter_context(nc.Block())

        @block.sync
        def _(sp):
            sp.dma_start(vec[:, :], vec_d).then_inc(c_in, 16)
            sp.dma_start(rows[:, :], rows_d.partition_broadcast(P)).then_inc(c_in, 16)
            for n in range(N_PRE):
                if n >= RING:
                    sp.wait_ge(*freed_pre(n - RING))
                sp.dma_start(slot(n), pre_d[n]).then_inc(w_in[n % RING], 16)
            sp.wait_ge(list_ok, 1)
            n_quads = sp.value_load(nqi[0:1, 0:1], min_val=1, max_val=MAX_QUADS)
            at = [sp.value_load(units[0:1, 1, u:u + 1], min_val=0, max_val=N_EXP - 1) for u in range(2)]
            for j in range(PAIR_TILES):
                sp.wait_ge(*freed_pre(N_PRE + j - RING))
                sp.dma_start(slot(N_PRE + j), moe_d[bass.ds(at[j % 2] * 6 + j // 2, 1)].squeeze(0)).then_inc(
                    w_in[(N_PRE + j) % RING], 16)
            with sp.Fori(1, n_quads * 2) as p:
                at = [sp.value_load(units[0:1, 1, bass.ds(p * 2 + u, 1)], min_val=0, max_val=N_EXP - 1)
                      for u in range(2)]
                for j in range(PAIR_TILES):
                    sp.wait_ge(moe_used, PAIR_TILES + 1 + j + p * PAIR_TILES)
                    sp.dma_start(slot(N_PRE + j), moe_d[bass.ds(at[j % 2] * 6 + j // 2, 1)].squeeze(0)).then_inc(
                        w_in[(N_PRE + j) % RING], 16)
            for n in range(N_POST):
                if n < RING:
                    sp.wait_ge(moe_used, PAIR_TILES + 1 + n + n_quads * (2 * PAIR_TILES))
                else:
                    sp.wait_ge(*freed_post(n - RING))
                sp.dma_start(slot(N_PRE + n), post_d[n]).then_inc(w_in2[(N_PRE + n) % RING], 16)
            for k in range(KT):
                sp.wait_ge(fin_ok, k + 1)
                sp.dma_start(out_d[k * P:(k + 1) * P, :], RC[:, k, :]).then_inc(out_done, 16)
            sp.wait_ge(out_done, 16 * KT)

        @block.tensor
        def _(pe):
            mm = nc.tensor.matmul
            e_state = [0]

            def free_bank(e):
                assert e == e_state[0], (e, e_state[0])
                e_state[0] += 1
                if e >= 2:
                    pe.wait_ge(ev[e % 2], e // 2)

            def arrive(n):
                pe.wait_ge(w_in[n % RING], 16 * (n // RING + 1))

            def arrive2(n):
                s = (N_PRE + n) % RING
                pe.wait_ge(w_in2[s], 16 * (n // RING + 1))

            def column(e, w, x, free=None):
                free_bank(e)
                k_n = free or KT
                for k in range(k_n):
                    last = mm(bank(e)[:, :], w[:, k * P:(k + 1) * P], x(k), start=(k == 0), stop=(k == k_n - 1))
                last.then_inc(acc, 1)

            def column_tok(e, w, x):
                free_bank(e)
                for t in range(TT):
                    for k in range(KT):
                        last = mm(bank(e)[:, t * P:(t + 1) * P], x(k)[:, t * P:(t + 1) * P],
                                  w[:, k * P:(k + 1) * P], start=(k == 0), stop=(k == KT - 1))
                last.then_inc(acc, 1)

            def stats(at, n, b):
                for k in range(n):
                    pe.wait_ge(sq_ready, at + k + 1)
                    mm(ps[b][:, :], ones[:, :], SQ[:, (at + k) % 2, :], start=(k == 0),
                       stop=(k == n - 1)).then_inc(sq_used, 1)

            def ada(n, col, b, base):
                arrive(n)
                for k in range(KT):
                    last = mm(ps[b][:, col - base:col - base + 1], slot(n)[:, k * P:(k + 1) * P], cact[:, k:k + 1],
                              start=(k == 0), stop=(k == KT - 1))
                last.then_inc(ada_done, 1)

            def hT(k):
                return RB[:, k, :]

            def attend(g):
                ql, kr, vv, _ = group_ops(g)

                def scores(u):
                    t, h = UNITS[u]
                    n = g * NU + u
                    if n >= 2:
                        pe.wait_ge(biased, n - 1)
                    w = (t + 1) * P
                    mm(ps[n % 2][:, 0:w], ql(h, t), kr(h, w), start=True, stop=True).then_inc(s_full, 1)

                def turn(u):
                    t, h = UNITS[u]
                    n = g * NU + u
                    pe.wait_ge(p_ready, n + 1)
                    if n >= 2:
                        pe.wait_ge(pt_ready[n % 2], n // 2)
                    for j in range(t + 1):
                        last = nc.tensor.transpose(ps[2 + n % 2][:, j * P:(j + 1) * P],
                                                   PB[:, n % 2, j * P:(j + 1) * P], ident[:, :])
                    last.then_inc(pt_full, 1)

                def values(u):
                    t, h = UNITS[u]
                    n = g * NU + u
                    i = g * TT + t
                    pe.wait_ge(pt_ready[n % 2], n // 2 + 1)
                    if h == 0 and i >= 2:
                        pe.wait_ge(o_ready, i - 1)
                    for j in range(t + 1):
                        last = mm(ps[4 + i % 2][:, h * 64:h * 64 + 64], PTB[:, n % 2, j * P:(j + 1) * P], vv(h, j),
                                  start=(j == 0), stop=(j == t))
                    last.then_inc(pv_done, 1)

                def outputs(t):
                    i = g * TT + t
                    e = ot_event(g, t)
                    free_bank(e)
                    pe.wait_ge(o_ready, i + 1)
                    for c in range(4):
                        last = nc.tensor.transpose(bank(e)[:, c * P:(c + 1) * P], OTK[:, i % 2, c * P:(c + 1) * P],
                                                   ident[:, :])
                    last.then_inc(acc, 1)

                scores(0)
                scores(1)
                for u in range(NU + 1):
                    if u < NU:
                        turn(u)
                    if u + 2 < NU:
                        scores(u + 2)
                    if u >= 1:
                        values(u - 1)
                    if u >= 4 and (u - 4) % HG == 0 and u >= HG:
                        outputs((u - 4) // HG - 1)
                outputs(TT - 1)

            pe.wait_ge(consts, 1)
            stats(ST_H1, KT, 2)
            pe.wait_ge(cact_ok, 1)
            for n in range(16):
                ada(n, n, 0, 0)
            pe.wait_ge(h_ok, KT)
            for i in range(16):
                n = 16 + 3 * i
                arrive(n)
                (column if i < 12 else column_tok)(PE_S1 + i, slot(n), hT)
                ada(n + 1, 16 + 2 * i, 1, 16)
                ada(n + 2, 17 + 2 * i, 1, 16)
                if i == 7:
                    stats(ST_Q, 2, 2)
                if i == 9:
                    stats(ST_KV, 1, 2)
            n = 64
            pe.wait_ge(lat_n, 3)
            for c in range(8):
                if c % 4 == 0:
                    arrive(n + c // 4)
                w = slot(n + c // 4)[:, (c % 4) * 256:(c % 4) * 256 + 256]
                column(PE_U + c, w, lambda k: qnT[:, k, :], free=2)
            arrive(n + 2)
            for c in range(4):
                column(PE_U + 8 + c, slot(n + 2)[:, c * P:(c + 1) * P], lambda k: kvnT, free=1)
            for t in range(TT):
                e = PE_U + 12 + t
                free_bank(e)
                mm(bank(e)[:, :], kvnT[:, t * P:(t + 1) * P], slot(n + 2)[:, 512:1024], start=True,
                   stop=True).then_inc(acc, 1)
            pe.wait_ge(ev[0], PE_OT // 2)
            pe.wait_ge(ev[1], PE_OT // 2)
            pe.wait_ge(bias_in, 16)
            for h in range(HG):
                if h >= 2:
                    pe.wait_ge(flip_ev, h)
                mm(ps[4 + h % 2][:, :], flip[:, :], RG[:, h, :], start=True, stop=True).then_inc(flip_full, 1)
            pe.wait_ge(flip_ev, HG + 1)
            pe.wait_ge(mod_ok, 2)
            attend(0)
            pe.wait_ge(lat_ok, 1)
            attend(1)
            pe.wait_ge(ev[0], (PE_O) // 2)
            pe.wait_ge(ev[1], (PE_O) // 2)
            pe.wait_ge(o_ready, 2 * TT)
            for i in range(KT):
                n = 67 + 3 * i
                b = 4 * (i % 2)
                if i >= 2:
                    pe.wait_ge(g_done, i - 1)
                for s in range(2):
                    arrive(n + s)
                    for k in range(KT):
                        last = mm(ps[b + s][:, :], slot(n + s)[:, k * P:(k + 1) * P], hT(k), start=(k == 0),
                                  stop=(k == KT - 1))
                    last.then_inc(g_used, 1)
                arrive(n + 2)
                for s, src in ((2, oaT), (3, obT)):
                    for k in range(4):
                        kk = (s - 2) * 4 + k
                        last = mm(ps[b + s][:, :], slot(n + 2)[:, kk * P:(kk + 1) * P], src[:, k, :], start=(k == 0),
                                  stop=(k == 3))
                last.then_inc(g_used, 1)
            pe.wait_ge(g_done, KT)
            for i in range(KT):
                n = 91 + i
                arrive(n)
                column(PE_O + i, slot(n), lambda k: RC[:, k, :])
            stats(ST_H2, KT, 2)
            pe.wait_ge(h_ok, 2 * KT)
            pe.wait_ge(wr_in, 16)
            for t in range(TT):
                for k in range(KT):
                    last = mm(ps[0][:, t * 36:t * 36 + 36], hT(k)[:, t * P:(t + 1) * P], w_r[:, k, :],
                              start=(k == 0), stop=(k == KT - 1))
            last.then_inc(lg_full, 1)
            for i in range(KT):
                e = PE_H + i
                free_bank(e)
                t, hf = i // 2, i % 2
                for c in range(4):
                    last = nc.tensor.transpose(bank(e)[:, c * P:(c + 1) * P], hT(hf * 4 + c)[:, t * P:(t + 1) * P],
                                               ident[:, :])
                last.then_inc(acc, 1)
            pe.wait_ge(mask_ok, 1)
            for t in range(TT):
                for s in range(t + 1):
                    last = mm(ps[3][:, t * 32:t * 32 + 32], ones[:, :] if s < t else upper[:, :],
                              chosen[:, s, :], start=(s == 0), stop=(s == t))
            last.then_inc(pos_full, 1)
            for r in range(4):
                for s in range(TT):
                    last = mm(ps[4][32 * r:32 * r + 32, 0:1], chosen[:, s, :], ones[:, 0:1], start=(s == 0),
                              stop=(s == TT - 1))
            last.then_inc(cnt_full, 1)
            pe.wait_ge(flag_ok, 1)
            mm(ps[5][:, 0:1], upper[:, :], sel[:, 6:7], start=True, stop=True)
            mm(ps[5][:, 1:2], ones[:, :], sel[:, 6:7], start=True, stop=False)
            mm(ps[5][:, 1:2], upper[:, :], sel[:, 7:8], start=False, stop=True)
            mm(ps[5][:, 2:3], ones[:, :], sel[:, 6:7], start=True, stop=False)
            mm(ps[5][:, 2:3], ones[:, :], sel[:, 7:8], start=False, stop=True).then_inc(rank_full, 1)
            pe.wait_ge(rank_ok, 1)
            for i in range(2):
                for hf in range(2):
                    last = mm(ps[5][0:1, 64 + i * SLOTS:64 + (i + 1) * SLOTS], sel[:, 2 * i + hf:2 * i + hf + 1],
                              ranked[:, hf, :], start=(hf == 0), stop=(hf == 1))
            last.then_inc(list_full, 1)
            pe.wait_ge(ev[0], PE_Q2 // 2)
            pe.wait_ge(ev[1], PE_Q2 // 2)
            pe.wait_ge(route_ok, 1)
            pe.wait_ge(list_ok, 1)
            n_quads = pe.value_load(nqi[0:1, 0:1], min_val=1, max_val=MAX_QUADS)
            pe.sem_inc(got, 2)
            pe.sem_inc(st_t, 2)
            pe.sem_inc(y_full, 1)
            pe.sem_inc(ht_done, 2)
            pe.sem_inc(moe_used, 2 * PAIR_TILES)

            def gather(b, q2):
                pe.wait_ge(oh_ready, b + 1 + q2)
                pe.wait_ge(x_ev, b + 1 + q2)
                for k in range(KT):
                    for t in range(TT):
                        last = mm(ps[k // 4][:, (k % 4) * P:(k % 4 + 1) * P], h2tok[:, t, k * P:(k + 1) * P],
                                  OH[:, b % 2, t, :], start=(t == 0), stop=(t == TT - 1))
                last.then_inc(got, 1)

            gather(0, 0)
            with pe.Fori(0, n_quads) as q:
                def arrive_pair(b, j):
                    n = N_PRE + j
                    pe.wait_ge(w_in[n % RING], 16 * (n // RING + 1 + b) + q * 32)

                def gate_up(b):
                    pe.wait_ge(x_ev, b + 2 + q * 2)
                    pe.wait_ge(ht_ev, b + 1 + q * 2)
                    for s in range(4):
                        for u in range(2):
                            arrive_pair(b, 2 * s + u)
                        for k in range(2):
                            kk = 2 * s + k
                            for u in range(2):
                                last = mm(ps[2 + b][u * SLOTS:(u + 1) * SLOTS, :],
                                          Xg[:, b, kk, u * SLOTS:(u + 1) * SLOTS],
                                          slot(N_PRE + 2 * s + u)[:, k * T:(k + 1) * T],
                                          start=(kk == 0), stop=(kk == KT - 1))
                        last.then_inc(moe_used, 2)

                def down(b):
                    pe.wait_ge(hid_done, b + 1 + q * 2)
                    for f in range(2):
                        last = nc.tensor.transpose(ps[2 + b][:, f * P:(f + 1) * P], hid[:, b, f * P:(f + 1) * P],
                                                   ident[:, :])
                    last.then_inc(ht_done, 1)
                    pe.wait_ge(ht_ev, b + 3 + q * 2)
                    for j in range(8, 12):
                        arrive_pair(b, j)
                    for hf in range(2):
                        pe.wait_ge(z_ev, 2 * b + hf + 1 + q * 4)
                        for f in range(2):
                            for u in range(2):
                                last = mm(ps[4 + hf][u * SLOTS:(u + 1) * SLOTS, :],
                                          hidT[:, b, f, u * SLOTS:(u + 1) * SLOTS],
                                          slot(N_PRE + 8 + 2 * f + u)[:, hf * T:(hf + 1) * T],
                                          start=(f == 0), stop=(f == 1))
                        if hf == 0:
                            last.then_inc(dn_half, 1)
                    last.then_inc(moe_used, 4)

                def turn_slots(b):
                    pe.wait_ge(ohw_ready, b + 2 + q * 2)
                    pe.wait_ge(y_ev, b + 1 + q * KT)
                    for t in range(TT):
                        last = nc.tensor.transpose(ps[6 + b][:, t * P:(t + 1) * P], OHW[:, b, t, :], ident[:, :])
                    last.then_inc(st_t, 1)

                gate_up(0)
                gather(1, q * 2)
                down(0)
                gate_up(1)
                turn_slots(0)
                turn_slots(1)
                gather(2, q * 2)
                down(1)
                pe.wait_ge(st_ev, 2 + q * 2)
                for n in range(KT):
                    if n % 4 == 0:
                        pe.wait_ge(z_ev, 5 + n // 4 + q * 4)
                    if n >= 2:
                        pe.wait_ge(y_ev, n + 1 + q * KT)
                    for b in range(2):
                        last = mm(ps[6 + n % 2][:, :], Zs[:, b, n * P:(n + 1) * P], St[:, b, :], start=(b == 0),
                                  stop=(b == 1))
                    last.then_inc(y_full, 1)
            stats(ST_F, KT, 2)
            pe.wait_ge(x2_ok, KT)
            xT = lambda k: RA[:, k, :]
            for i in range(24):
                e = PE_Q2 + i
                arrive2(i)
                (column if i < 16 else column_tok)(e, slot(N_PRE + i), xT)
            pe.wait_ge(ev[0], PE_OT2 // 2)
            pe.wait_ge(ev[1], PE_OT2 // 2)
            for g in (2, 3):
                attend(g)
            for i in range(12):
                arrive2(24 + i)
                column(PE_XBC + i, slot(N_PRE + 24 + i), xT)
            pe.wait_ge(wdt_in, 16)
            for t in range(TT):
                for k in range(KT):
                    last = mm(ps[0][:, t * 16:t * 16 + 16], xT(k)[:, t * P:(t + 1) * P], wdt[:, k, :],
                              start=(k == 0), stop=(k == KT - 1))
            last.then_inc(dt_full, 1)
            pe.wait_ge(xbc_ok, 8)
            for i in range(8):
                e = PE_XT + i
                free_bank(e)
                t, hf = i // 2, i % 2
                for c in range(4):
                    last = nc.tensor.transpose(bank(e)[:, c * P:(c + 1) * P],
                                               RG[:, hf * 4 + c, t * P:(t + 1) * P], ident[:, :])
                last.then_inc(acc, 1)
            pe.wait_ge(xbc_ok, 12)
            for g in range(2):
                e = PE_BT + g
                free_bank(e)
                for t in range(TT):
                    last = nc.tensor.transpose(bank(e)[:, t * P:(t + 1) * P], RF[:, g, t * P:(t + 1) * P], ident[:, :])
                last.then_inc(acc, 1)
            pe.wait_ge(adt_ok, 1)
            for c in range(TT):
                mm(ps[1][:, c * 16:c * 16 + 16], upper[:, :], adt_t[:, c, :], start=True, stop=True)
            for c in range(TT):
                last = mm(ps[1][:, 64 + c * 16:80 + c * 16], ones[:, :], adt_t[:, c, :], start=True, stop=True)
            last.then_inc(cs_full, 1)
            pe.wait_ge(ev[0], PE_YT // 2)
            pe.wait_ge(ev[1], PE_YT // 2)
            pe.wait_ge(cs_ok, 1)
            for c in range(TT):
                if c >= 1:
                    pe.wait_ge(y_tok, c)
                for g in range(2):
                    last = mm(ps[0][:, g * P:(g + 1) * P], RF[:, g, c * P:(c + 1) * P], RF[:, 2 + g, c * P:(c + 1) * P],
                              start=True, stop=True)
                last.then_inc(cb_full, 1)
                for q in range(4):
                    if 4 * c + q >= 2:
                        pe.wait_ge(dd_ok, 4 * c + q - 1)
                    for h in range(4):
                        last = mm(ps[2 + q % 2][:, h * P:(h + 1) * P],
                                  adt_t[:, c, 4 * q + h:4 * q + h + 1].to_broadcast([P, P]), upper[:, :],
                                  start=True, stop=True)
                    last.then_inc(csb_full, 1)
                if c == 0:
                    pe.wait_ge(xg_ok, TT)
                for h in range(SSM_H):
                    if h % 4 == 0:
                        pe.wait_ge(mm_ok, 4 * c + h // 4 + 1)
                    last = mm(ps[4 + h // 8][:, (h % 8) * 64:(h % 8) * 64 + 64], decay[:, h, :], xg_tok[:, c, h, :],
                              start=True, stop=True)
                last.then_inc(yd_full, 1)
                if c > 0:
                    pe.wait_ge(state_ok, c)
                    pe.wait_ge(cb_ok, c + 1)
                    for g in range(2):
                        last = mm(ps[g][:, :], RF[:, 2 + g, c * P:(c + 1) * P], state[:, g, :], start=True, stop=True)
                    last.then_inc(yo_full, 1)
                if c < TT - 1:
                    pe.wait_ge(xgd_ok, c + 1)
                    for g in range(2):
                        last = mm(ps[6 + g][:, :], b_tok[:, g, c, :], REf[:, 2048 + g * T:2048 + (g + 1) * T], start=True, stop=True)
                    last.then_inc(st_full, 1)
            for i in range(8):
                e = PE_YT + i
                t, hf = i // 2, i % 2
                free_bank(e)
                pe.wait_ge(y_tok, TT)
                for c in range(4):
                    last = nc.tensor.transpose(bank(e)[:, c * P:(c + 1) * P],
                                               RDf[:, t * D + (hf * 4 + c) * P:t * D + (hf * 4 + c + 1) * P], ident[:, :])
                last.then_inc(acc, 1)
            for i in range(16):
                arrive2(36 + i)
                column(PE_ZA + i, slot(N_PRE + 36 + i), xT)
            stats(ST_AT, KT, 2)
            stats(ST_SS, KT, 3)
            pe.wait_ge(mixn, 16)
            for i in range(KT):
                e = PE_OUT + i
                free_bank(e)
                for s in range(2):
                    n = 52 + 2 * i + s
                    arrive2(n)
                    for k in range(KT):
                        last = mm(bank(e)[:, :], slot(N_PRE + n)[:, k * P:(k + 1) * P],
                                  RB[:, k, :] if s == 0 else RG[:, k, :], start=(s == 0 and k == 0),
                                  stop=(s == 1 and k == KT - 1))
                last.then_inc(acc, 1)
            for k in range(KT):
                pe.wait_ge(r_ok, k + 1)
                last = mm(ps[4][:, :], ones[:, :], RA[:, k, :], start=(k == 0), stop=(k == KT - 1))
            last.then_inc(mu_full, 1)
            stats(ST_VAR, KT, 5)

        def tok_dst(view, t, hf):
            return view[:, t, hf * T:(hf + 1) * T]

        def quad(ap):
            return ap.rearrange("p (a b) -> p a b", a=4)

        def s1_dst(i):
            b = bank(PE_S1 + i)
            if i < 2:
                return [(qlT[:, i, :], b[:, :])], 1.0
            if i == 2:
                return [(kvT, b[:, :])], 1.0
            if i == 3:
                return [(krT, b[:, :])], 1.0
            if i < 8:
                return [(qbT[:, i - 4, :], b[:, :])], 0.125
            if i < 12:
                return [(kbT[:, i - 8, :], b[:, :])], 1.0
            return [(vb[:, :, (i - 12) * P:(i - 11) * P], quad(b[:, :]))], 1.0

        def u_dst(c):
            b = bank(PE_U + c)
            if c < 4:
                return [(RD[0:64, 2 * c, :], b[0:64, :]), (RD[64:128, 2 * c + 1, :], b[64:128, :])], MLA_SCALE
            if c < 8:
                return [((OTK if c % 2 == 0 else PTB)[:, (c - 4) // 2, :], b[:, :])], MLA_SCALE
            if c < 12:
                j = c - 8
                return [(RE[0:64, 2 * j, :], b[0:64, :]), (RE[64:128, 2 * j + 1, :], b[64:128, :])], 1.0
            return [(va[:, c - 12, :], b[:, :])], 1.0

        def q2_dst(i):
            b = bank(PE_Q2 + i)
            if i < 8:
                return [(RC[:, i, :], b[:, :])], 0.125
            if i < 16:
                return [(RD[:, i - 8, :], b[:, :])], 1.0
            return [(v2[:, :, (i - 16) * P:(i - 15) * P], quad(b[:, :]))], 1.0

        def ot_dst(g, t):
            return [(OT_DST[g][:, :, t * P:(t + 1) * P], quad(bank(ot_event(g, t))[:, :]))], 1.0

        @block.scalar
        def _(act):
            A = nc.scalar.activation
            links = [0]

            def link(ins):
                links[0] += 1
                ins.then_inc(act_c, 1)
                act.wait_ge(act_c, links[0])

            def evict(e, what):
                pairs, scale = what
                act.wait_ge(acc, e + 1)
                for dst, src in pairs:
                    ins = A(dst, src, ACT.Copy, scale=scale)
                ins.then_inc(ev[e % 2], 1)

            def norm(idx, at, n, b, src, ready, eps):
                for k in range(n):
                    ready(k)
                    if at + k >= 2:
                        act.wait_ge(sq_used, at + k - 1)
                    A(SQ[:, (at + k) % 2, :], src(k), ACT.Square).then_inc(sq_ready, 1)
                act.wait_ge(sq_used, at + n)
                if idx > 0:
                    act.wait_ge(rinv_used, idx)
                link(A(RINV[:, :], ps[b][:, :], ACT.Ln, scale=1.0 / (n * P), bias=eps))
                A(RINV[:, :], RINV[:, :], ACT.Exp, scale=-0.5).then_inc(rinv_ok, 1)

            def attend(g):
                def evict_pt(u):
                    n = g * NU + u
                    if n % 2 == 0:
                        return
                    w = (UNITS[u][0] + 1) * P
                    act.wait_ge(pt_full, n + 1)
                    if n >= 2:
                        act.wait_ge(pv_done, n - 1)
                    A(PTB[:, 1, 0:w], ps[3][:, 0:w], ACT.Copy).then_inc(pt_ready[1], 1)

                for u in range(NU):
                    t, h = UNITS[u]
                    n, i = g * NU + u, g * TT + t
                    w = (t + 1) * P
                    act.wait_ge(biased, n + 1)
                    if n >= 2:
                        act.wait_ge(pt_full, n - 1)
                    if h == 0 and i >= 2:
                        act.wait_ge(o_ready, i - 1)
                    A(PB[:, n % 2, 0:w], SB[:, n % 2, 0:w], ACT.Exp, scale=-1.0, bias=nmax(n),
                      accum_out=rowsum[:, (i % 2) * HG + h:(i % 2) * HG + h + 1]).then_inc(p_ready, 1)
                    if u >= 1:
                        evict_pt(u - 1)
                    if u % HG == 5 and u > HG:
                        t_o = u // HG - 1
                        if ot_event(g, t_o) % 2:
                            evict(ot_event(g, t_o), ot_dst(g, t_o))
                evict_pt(NU - 1)
                if ot_event(g, TT - 1) % 2:
                    evict(ot_event(g, TT - 1), ot_dst(g, TT - 1))

            act.dma_start(RA[:, 0:4, :], xT_d[0:T, :].rearrange("(k p) t -> p k t", p=P)).then_inc(x_in, 16)
            act.dma_start(RA[:, 4:8, :], xT_d[T:D, :].rearrange("(k p) t -> p k t", p=P)).then_inc(x_in, 16)
            act.dma_start(OTK[:, 0, :].bitcast(I32), pos_d.partition_broadcast(P)).then_inc(pos_in, 16)
            act.dma_start(ext_row[:, 255:640], rel_d[:, 0:385]).then_inc(rev_in, 16)
            act.dma_start(w_r[:, :, :], wr_d).then_inc(wr_in, 16)
            act.dma_start(wdt[:, :, :], wdt_d).then_inc(wdt_in, 16)
            act.wait_ge(x_in, 32)
            act.wait_ge(consts, 1)
            norm(0, ST_H1, KT, 2, lambda k: RA[:, k, :], lambda k: None, eps1)
            act.wait_ge(c_in, 32)
            A(cact, V("c", 0, 8), ACT.Silu).then_inc(cact_ok, 1)
            act.wait_ge(ext_ok, 1)
            act.dma_start(ext_d, ext_row[:, :]).then_inc(ext_out, 16)
            act.wait_ge(ext_out, 16)
            act.dma_start(RG[:, :, :], bass.AP(ext_d.tensor, 0, [[1, P], [640, HG], [1, T]])).then_inc(bias_in, 16)
            act.wait_ge(ang_ok, 2)
            A(sinT, RH[:, 4, :], ACT.Sin)
            A(cosT, RH[:, 5, :], ACT.Sin).then_inc(rope_ok, 1)
            for i in range(16):
                if i % 2:
                    evict(PE_S1 + i, s1_dst(i))
                if i == 7:
                    act.wait_ge(ev[0], 1)
                    norm(1, ST_Q, 2, 2, lambda k: qlT[:, k, :], lambda k: None, eps1)
                if i == 9:
                    act.wait_ge(ev[0], 2)
                    norm(2, ST_KV, 1, 2, lambda k: kvT, lambda k: None, eps1)
            for c in range(16):
                if c % 2:
                    evict(PE_U + c, u_dst(c))
            act.wait_ge(lat_ok, 1)
            attend(0)
            attend(1)
            act.wait_ge(pt_full, 2 * NU)
            for i in range(KT):
                if i >= 2:
                    act.wait_ge(g_done, i - 1)
                b = 4 * (i % 2)
                act.wait_ge(g_used, 3 * i + 1)
                A(SB[:, i % 2, :], ps[b][:, :], ACT.Tanh, scale=0.5)
                act.wait_ge(g_used, 3 * i + 2)
                A(PB[:, i % 2, :], ps[b + 1][:, :], ACT.Tanh, scale=0.5).then_inc(g_tanh, 1)
            norm(3, ST_H2, KT, 2, lambda k: RA[:, k, :], lambda k: act.wait_ge(x1_ok, k + 1), eps1)
            for i in range(8):
                if i % 2:
                    e = PE_H + i
                    evict(e, ([(tok_dst(h2tok, i // 2, 1), bank(e)[:, :])], 1.0))
            act.wait_ge(sp1, 1)
            A(SB[:, 0, 32:52], SB[:, 0, 0:20], ACT.Exp).then_inc(sp2, 1)
            act.wait_ge(list_ok, 1)
            n_quads = act.value_load(nqi[0:1, 0:1], min_val=1, max_val=MAX_QUADS)
            act.sem_inc(x_ev, 1)
            act.sem_inc(z_ev, 2)
            act.sem_inc(ht_ev, 2)

            def gathered(b, q2, q24):
                act.wait_ge(got, b + 3 + q2)
                act.wait_ge(moe_used, PAIR_TILES * b + 8 + q24)
                A(Xg[:, b % 2, 0:4, :], quad(ps[0][:, :]), ACT.Copy)
                A(Xg[:, b % 2, 4:8, :], quad(ps[1][:, :]), ACT.Copy).then_inc(x_ev, 1)

            gathered(0, 0, 0)
            with act.Fori(0, n_quads) as q:
                def gate(b):
                    act.wait_ge(moe_used, PAIR_TILES * (b + 2) + 8 + q * (2 * PAIR_TILES))
                    A(sg[:, b, :], ps[2 + b][:, 0:256], ACT.Silu).then_inc(sg_done, 1)

                def turned_hidden(b):
                    act.wait_ge(ht_done, b + 3 + q * 2)
                    act.wait_ge(moe_used, PAIR_TILES * b + 12 + q * (2 * PAIR_TILES))
                    A(hidT[:, b, :, :], ps[2 + b][:, 0:256].rearrange("p (f s) -> p f s", f=2),
                      ACT.Copy).then_inc(ht_ev, 1)

                def downs(b):
                    act.wait_ge(y_full, 1 + q * KT)
                    act.wait_ge(dn_half, b + 1 + q * 2)
                    A(Zs[:, b, 0:T], ps[4][:, :], ACT.Copy).then_inc(z_ev, 1)
                    act.wait_ge(moe_used, PAIR_TILES * (b + 3) + q * (2 * PAIR_TILES))
                    A(Zs[:, b, T:D], ps[5][:, :], ACT.Copy).then_inc(z_ev, 1)

                def turned(b):
                    act.wait_ge(st_t, 3 + b + q * 2)
                    A(St[:, b, :], ps[6 + b][:, :], ACT.Copy).then_inc(st_ev, 1)

                gate(0)
                gathered(1, q * 2, q * (2 * PAIR_TILES))
                turned_hidden(0)
                downs(0)
                gate(1)
                turned(0)
                turned(1)
                gathered(2, q * 2, q * (2 * PAIR_TILES))
                turned_hidden(1)
                downs(1)
            norm(4, ST_F, KT, 2, lambda k: RA[:, k, :], lambda k: act.wait_ge(x1_ok, KT + k + 1), eps1)
            for i in range(24):
                if i % 2:
                    evict(PE_Q2 + i, q2_dst(i))
            attend(2)
            attend(3)
            act.wait_ge(pv_done, 4 * NU)
            for i in range(13):
                if i < 12:
                    if i >= 2:
                        act.wait_ge(conv_ok, i - 1)
                    act.wait_ge(acc, PE_XBC + i + 1)
                    ins = A(convbuf[i % 2][:, 3:T + 3], bank(PE_XBC + i)[:, :], ACT.Copy)
                    ins.then_inc(ev[i % 2], 1)
                if i >= 1:
                    act.wait_ge(conv_ok, i)
                    tile = RG[:, i - 1, :] if i - 1 < 8 else RF[:, i - 9, :]
                    A(tile, tile, ACT.Silu).then_inc(xbc_ok, 1)
            act.wait_ge(sp1, 2)
            link(A(tmp_t[:, :, :], tmp_t[:, :, :], ACT.Exp))
            A(aneg, rows[:, R_ALOG:R_ALOG + 16], ACT.Exp)
            A(tmp_t[:, :, :], tmp_t[:, :, :], ACT.Ln, bias=ones[:, 0:1]).then_inc(sp2, 1)
            for i in range(8):
                if i % 2:
                    e = PE_XT + i
                    evict(e, ([(RCf[:, (i // 2) * D + T:(i // 2) * D + D], bank(e)[:, :])], 1.0))
            evict(PE_BT + 1, ([(b_tok[:, 1, :, :], quad(bank(PE_BT + 1)[:, :]))], 1.0))
            act.wait_ge(cs_ok, 1)
            A(sd_t[:, :, :], cs_t[:, :, :], ACT.Exp)
            A(dec_t[:, :, :], tot_t[:, :, :], ACT.Exp)
            A(dte_t[:, :, :], tmp_t[:, :, :], ACT.Exp).then_inc(sp2, 1)
            for c in range(TT):
                for q in range(4):
                    act.wait_ge(dd_ok, 4 * c + q + 1)
                    A(decay[:, 4 * q:4 * q + 4, :], decay[:, 4 * q:4 * q + 4, :], ACT.Exp).then_inc(ee_ok, 1)
            for i in range(8):
                if i % 2:
                    e = PE_YT + i
                    evict(e, ([(RG[:, 4:8, (i // 2) * P:(i // 2 + 1) * P], quad(bank(e)[:, :]))], 1.0))
            for i in range(16):
                e = PE_ZA + i
                if i >= 4:
                    act.wait_ge(mixp, i - 3)
                act.wait_ge(acc, e + 1)
                A(zbuf(i), bank(e)[:, :], ACT.Silu).then_inc(ev[e % 2], 1)
            norm(5, ST_AT, KT, 2, lambda k: RB[:, k, :], lambda k: act.wait_ge(mixp, k + 1), eps2)
            norm(6, ST_SS, KT, 3, lambda k: RG[:, k, :], lambda k: act.wait_ge(mixp, KT + k + 1), eps2)
            norm(7, ST_VAR, KT, 5, lambda k: RC[:, k, :], lambda k: act.wait_ge(cen_ok, k + 1), eps2)

        @block.vector
        def _(dve):
            v = nc.vector
            links = [0]

            def link(ins):
                links[0] += 1
                ins.then_inc(dve_c, 1)
                dve.wait_ge(dve_c, links[0])

            def evict(e, what):
                pairs, scale = what
                dve.wait_ge(acc, e + 1)
                for dst, src in pairs:
                    ins = v.tensor_scalar(dst, src, scale, None, ALU.mult) if scale != 1.0 else v.tensor_copy(dst, src)
                ins.then_inc(ev[e % 2], 1)

            def attend(g):
                def evict_pt(u):
                    n = g * NU + u
                    if n % 2:
                        return
                    w = (UNITS[u][0] + 1) * P
                    dve.wait_ge(pt_full, n + 1)
                    if n >= 2:
                        dve.wait_ge(pv_done, n - 1)
                    v.tensor_copy(PTB[:, 0, 0:w], ps[2][:, 0:w]).then_inc(pt_ready[0], 1)

                def normalise(t):
                    i = g * TT + t
                    dve.wait_ge(pv_done, HG * (i + 1))
                    r = rsinv[:, 0:HG]
                    link(v.reciprocal(r, rowsum[:, (i % 2) * HG:(i % 2) * HG + HG]))
                    if i >= 2:
                        gg, tt = (i - 2) // TT, (i - 2) % TT
                        dve.wait_ge(acc, ot_event(gg, tt) + 1)
                    v.tensor_tensor(OTK[:, i % 2, :].rearrange("p (h c) -> p h c", h=HG),
                                    ps[4 + i % 2][:, :].rearrange("p (h c) -> p h c", h=HG),
                                    r.unsqueeze(2).to_broadcast([P, HG, 64]), ALU.mult).then_inc(o_ready, 1)

                bias = group_ops(g)[3]
                for u in range(NU):
                    t, h = UNITS[u]
                    n = g * NU + u
                    w = (t + 1) * P
                    if g == 0 and u == 0:
                        dve.wait_ge(bias_ok, 1)
                    if g >= 2 and t == 0:
                        dve.wait_ge(bias_ok, 1 + (g - 2) * HG + h + 1)
                    dve.wait_ge(s_full, n + 1)
                    if n >= 2:
                        dve.wait_ge(p_ready, n - 1)
                    v.tensor_tensor_reduce(SB[:, n % 2, 0:w], ps[n % 2][:, 0:w], bias(h)[:, T - w:T], -1.0, 3e38,
                                           ALU.add, ALU.min, nmax(n)).then_inc(biased, 1)
                    if u >= 1:
                        evict_pt(u - 1)
                    if u % HG == 2 and u > HG:
                        normalise(u // HG - 1)
                    if u % HG == 5 and u > HG:
                        t_o = u // HG - 1
                        if ot_event(g, t_o) % 2 == 0:
                            evict(ot_event(g, t_o), ot_dst(g, t_o))
                evict_pt(NU - 1)
                normalise(TT - 1)
                if ot_event(g, TT - 1) % 2 == 0:
                    evict(ot_event(g, TT - 1), ot_dst(g, TT - 1))

            dve.wait_ge(c_in, 32)
            dve.wait_ge(pos_in, 16)
            posf, ang, turns, red = OTK[:, 1, :], SB[:, 0, :], SB[:, 1, :], PB[:, 0, :]
            link(v.tensor_copy(posf, OTK[:, 0, :].bitcast(I32)))
            link(v.tensor_scalar(ang, posf, V("inv"), None, ALU.mult))
            for quarter, dst in ((0.0, RH[:, 4, :]), (0.25, RH[:, 5, :])):
                link(v.tensor_scalar(turns, ang, float(1 / TWO_PI), quarter, ALU.mult, ALU.add))
                link(v.tensor_scalar(turns, turns, ROUND, None, ALU.add))
                link(v.tensor_scalar(turns, turns, ROUND, None, ALU.subtract))
                link(v.scalar_tensor_tensor(red, turns, -C1, ang, ALU.mult, ALU.add))
                link(v.scalar_tensor_tensor(red, turns, -C2, red, ALU.mult, ALU.add))
                link(v.scalar_tensor_tensor(red, turns, -C3, red, ALU.mult, ALU.add))
                link(v.tensor_scalar(red, red, quarter * TWO_PI, 3.1415925, ALU.add, ALU.min))
                v.tensor_scalar(dst, red, -3.1415925, None, ALU.max).then_inc(ang_ok, 1)
                dve.wait_ge(ang_ok, 1 if quarter == 0.0 else 2)
            dve.wait_ge(ada_done, 16)
            link(v.tensor_tensor(mod[:, 0:16], ps[0][:, 0:16], V("b_ada", 0, 16), ALU.add))
            link(v.scalar_tensor_tensor(A1, mod[:, 8:16], 1.0, V("g_mix", 0, 8), ALU.add, ALU.mult))
            dve.wait_ge(rinv_ok, 1)
            for k in range(KT):
                ins = v.scalar_tensor_tensor(RB[:, k, :], RA[:, k, :], A1[:, k:k + 1], RINV[:, :], ALU.mult, ALU.mult)
                ins.then_inc(mod_h, 1)
            dve.wait_ge(mod_h, KT)
            dve.sem_inc(rinv_used, 1)
            for i in range(16):
                if i % 2 == 0:
                    evict(PE_S1 + i, s1_dst(i))
                if i == 8:
                    dve.wait_ge(rinv_ok, 2)
                    dve.wait_ge(ev[1], 1)
                    for k in range(2):
                        v.scalar_tensor_tensor(qnT[:, k, :], qlT[:, k, :], V("g_q", k), RINV[:, :], ALU.mult,
                                               ALU.mult).then_inc(lat_n, 1)
                    dve.wait_ge(lat_n, 2)
                    dve.sem_inc(rinv_used, 1)
                if i == 10:
                    dve.wait_ge(rinv_ok, 3)
                    v.scalar_tensor_tensor(kvnT, kvT, V("g_kv"), RINV[:, :], ALU.mult, ALU.mult).then_inc(lat_n, 1)
                    dve.wait_ge(lat_n, 3)
                    dve.sem_inc(rinv_used, 1)
            dve.wait_ge(ada_done, 48)
            v.tensor_tensor(mod[:, 16:48], ps[1][:, 0:32], V("b_ada", 16, 32), ALU.add).then_inc(mod_ok, 2)
            dve.wait_ge(mod_ok, 2)
            link(v.scalar_tensor_tensor(A2, mod[:, 32:40], 1.0, V("g_ffn", 0, 8), ALU.add, ALU.mult))
            link(v.tensor_scalar(gt1h, mod[:, 16:24], 0.5, None, ALU.mult))
            dve.wait_ge(rope_ok, 1)
            dve.wait_ge(ev[1], 2)
            link(v.tensor_scalar(sinT, sinT, V("sign"), None, ALU.mult))
            dve.wait_ge(zero_ok, 1)
            link(v.tensor_tensor(SB[0:32, 0, :], krT[0:32, :], cosT[0:32, :], ALU.mult))
            link(v.tensor_tensor(SB[0:32, 1, :], krT[32:64, :], sinT[32:64, :], ALU.mult))
            for h in range(8):
                r = 64 if h % 2 == 0 else 32
                ins = v.tensor_tensor(RE[r:r + 32, h, :], SB[0:32, 0, :], SB[0:32, 1, :], ALU.add)
            link(ins)
            for c in range(16):
                if c % 2 == 0:
                    evict(PE_U + c, u_dst(c))
                if c in (6, 8):
                    r = (c - 6) // 2
                    dve.wait_ge(ev[0], (PE_U + 4 + 2 * r) // 2 + 1)
                    dve.wait_ge(ev[1], (PE_U + 5 + 2 * r) // 2 + 1)
                    link(v.tensor_tensor(SB[:, 0, :], OTK[:, r, :], cosT, ALU.mult))
                    link(v.tensor_tensor(SB[:, 1, :], PTB[:, r, :], sinT, ALU.mult))
                    for h in range(4):
                        hh, o = 4 * r + h, 64 if h % 2 == 0 else 32
                        ins = v.tensor_tensor(RD[o:o + 32, hh, :], SB[32 * h:32 * h + 32, 0, :],
                                              SB[32 * h:32 * h + 32, 1, :], ALU.add)
                    link(ins)
            for h in range(HG):
                dve.wait_ge(flip_full, h + 1)
                v.tensor_copy(RG[:, h, :], ps[4 + h % 2][:, :]).then_inc(flip_ev, 1)
            dve.sem_inc(lat_ok, 1)
            attend(0)
            attend(1)
            for i in range(KT):
                b = 4 * (i % 2)
                dve.wait_ge(g_tanh, i + 1)
                dve.wait_ge(g_used, 3 * i + 3)
                link(v.scalar_tensor_tensor(SB[:, i % 2, :], SB[:, i % 2, :], 1.0, ps[b + 2][:, :], ALU.add, ALU.mult))
                link(v.scalar_tensor_tensor(PB[:, i % 2, :], PB[:, i % 2, :], 1.0, ps[b + 3][:, :], ALU.add, ALU.mult))
                v.tensor_tensor(RC[:, i, :], SB[:, i % 2, :], PB[:, i % 2, :], ALU.add).then_inc(g_done, 1)
            for i in range(KT):
                e = PE_O + i
                dve.wait_ge(acc, e + 1)
                v.scalar_tensor_tensor(RA[:, i, :], bank(e)[:, :], gt1h[:, i:i + 1], RA[:, i, :], ALU.mult,
                                       ALU.add).then_inc(x1_ok, 1)
                dve.wait_ge(x1_ok, i + 1)
                dve.sem_inc(ev[e % 2], 1)
            dve.wait_ge(rinv_ok, 4)
            dve.wait_ge(g_used, 24)
            for k in range(KT):
                v.scalar_tensor_tensor(RB[:, k, :], RA[:, k, :], A2[:, k:k + 1], RINV[:, :], ALU.mult,
                                       ALU.mult).then_inc(mod_h, 1)
            dve.wait_ge(mod_h, 2 * KT)
            dve.sem_inc(rinv_used, 1)
            def lane(a, n):
                return SB[:, 0, a:a + n]

            L = OTK[:, 1, 0:144].rearrange("p (t n) -> p t n", t=TT)
            dve.wait_ge(lg_full, 1)
            dve.wait_ge(acc, PE_O)
            link(v.tensor_tensor(L, ps[0][:, 0:144].rearrange("p (t n) -> p t n", t=TT),
                                 rows[:, 0:36].unsqueeze(1).to_broadcast([P, TT, 36]), ALU.add))
            for i in range(8):
                if i % 2 == 0:
                    e = PE_H + i
                    evict(e, ([(tok_dst(h2tok, i // 2, 0), bank(e)[:, :])], 1.0))
            R = SB[:, 1, :]

            def r3(a, n):
                return R[:, a:a + TT * n].rearrange("p (t n) -> p t n", t=TT)

            def first_max(src, n, top, oh):
                link(v.tensor_reduce(top, src, AX_X, ALU.max))
                c = r3(256, n)
                link(v.tensor_tensor(c, src, top.unsqueeze(2).to_broadcast([P, TT, n]), ALU.is_equal))
                link(v.scalar_tensor_tensor(c, c, -64.0, iota64[:, 0:n].unsqueeze(1).to_broadcast([P, TT, n]),
                                            ALU.mult, ALU.add))
                link(v.tensor_reduce(R[:, 384:388], c, AX_X, ALU.min))
                link(v.tensor_tensor(oh, c, R[:, 384:388].unsqueeze(2).to_broadcast([P, TT, n]), ALU.is_equal))

            gmax, top1, top2 = lane(60, 4), lane(64, 4), lane(68, 4)
            goh = r3(400, 4)
            first_max(L[:, :, 0:4], 4, gmax, goh)
            link(v.tensor_scalar(goh, goh, 1e30, -1e30, ALU.mult, ALU.add))
            el = r3(0, 32)
            for t in range(TT):
                ins = v.tensor_tensor(el[:, t, :].rearrange("p (g e) -> p g e", g=4),
                                      L[:, t, 4:36].rearrange("p (g e) -> p g e", g=4),
                                      goh[:, t, :].unsqueeze(2).to_broadcast([P, 4, 8]), ALU.add)
            link(ins)
            oh1, oh2 = r3(128, 32), OTK[:, 1, 256:384].rearrange("p (t n) -> p t n", t=TT)
            first_max(el, 32, top1, oh1)
            link(v.scalar_tensor_tensor(el, oh1, -3e30, el, ALU.mult, ALU.add))
            first_max(el, 32, top2, oh2)
            link(v.tensor_tensor(lane(0, 16).rearrange("p (t n) -> p t n", t=TT), L[:, :, 0:4],
                                 gmax.unsqueeze(2).to_broadcast([P, TT, 4]), ALU.subtract))
            v.tensor_tensor(lane(16, 4), top2, top1, ALU.subtract).then_inc(sp1, 1)
            link(v.tensor_tensor(chosen, oh1, oh2, ALU.add))
            dve.sem_inc(mask_ok, 1)
            dve.wait_ge(sp2, 1)
            gsum, w1, w2 = lane(72, 4), lane(76, 4), lane(80, 4)
            link(v.tensor_reduce(gsum, lane(32, 16).rearrange("p (t n) -> p t n", t=TT), AX_X, ALU.add))
            link(v.tensor_scalar(w1, lane(48, 4), 1.0, None, ALU.add))
            link(v.tensor_tensor(w1, w1, gsum, ALU.mult))
            link(v.reciprocal(w1, w1))
            link(v.tensor_tensor(w2, w1, lane(48, 4), ALU.mult))
            link(v.tensor_tensor(oh1, oh1, w1.unsqueeze(2).to_broadcast([P, TT, 32]), ALU.mult))
            link(v.tensor_tensor(oh2, oh2, w2.unsqueeze(2).to_broadcast([P, TT, 32]), ALU.mult))
            dve.wait_ge(pv_done, 2 * NU)

            def et(ap, p=0):
                return ap[:, p * P:(p + 1) * P].rearrange("p (e t) -> p t e", t=TT)

            link(v.tensor_tensor(et(combr), oh1, oh2, ALU.add))
            dve.wait_ge(pos_full, 1)
            link(v.tensor_tensor(el, ps[3][:, 0:128].rearrange("p (t n) -> p t n", t=TT), chosen, ALU.mult))
            for p in range(MAXPASS):
                ins = v.tensor_scalar(et(posm, p), el, -1.0 - p * SLOTS, None, ALU.add)
            v.memset(posm[:, MAXPASS * P:(MAXPASS * N_EXP + 1) * TT], -1.0)
            link(ins)
            dve.sem_inc(route_ok, 1)
            dve.wait_ge(cnt_full, 1)
            dve.wait_ge(sel_ok, 1)
            link(v.tensor_scalar(sel[:, 6:8], sel[:, 4:6], ps[4][:, 0:1], None, ALU.is_lt))
            dve.sem_inc(flag_ok, 1)
            dve.wait_ge(rank_full, 1)
            link(v.tensor_tensor(cnt[:, 0:2], ps[5][:, 0:2], sel[:, 6:8], ALU.mult))
            link(v.tensor_scalar(cnt[:, 0:2], cnt[:, 0:2], 1.0, None, ALU.subtract))
            for hf in range(2):
                ins = v.tensor_scalar(ranked[:, hf, :], iota64[:, :], cnt[:, hf:hf + 1], None, ALU.is_equal)
            link(ins)
            link(v.tensor_scalar(cnt[:, 2:3], ps[5][:, 2:3], 0.25, 0.75 - 0.5 + 0.125, ALU.mult, ALU.add))
            dve.sem_inc(rank_ok, 1)
            link(v.tensor_copy(nqi[0:1, 0:1], cnt[0:1, 2:3]))
            dve.wait_ge(list_full, 1)
            link(v.tensor_scalar(units[0:1, 0, :], ps[5][0:1, 64:128], float(MAXPASS * N_EXP), None, ALU.add))
            link(v.tensor_copy(units[0:1, 1, :], ps[5][0:1, 128:192]))
            dve.sem_inc(list_ok, 1)
            n_quads = dve.value_load(nqi[0:1, 0:1], min_val=1, max_val=MAX_QUADS)
            dve.wait_ge(y0_ok, 1)
            dve.sem_inc(y_ev, 2)

            def one_hot(b, q2):
                dve.wait_ge(got, b + 1 + q2)
                if b:
                    dve.wait_ge(ohw_ready, b + q2)
                for u in range(2):
                    at = units[0:1, 0, bass.ds(q2 * 2 + 2 * b + u, 1)] if b else units[0:1, 0, u:u + 1]
                    block_no = dve.value_load(at, min_val=0, max_val=MAXPASS * N_EXP)
                    ins = v.tensor_tensor(OH[:, b % 2, :, u * SLOTS:(u + 1) * SLOTS],
                                          iota64[:, :].unsqueeze(1).to_broadcast([P, TT, SLOTS]),
                                          posm[:, bass.ds(block_no * TT, TT)].unsqueeze(2).to_broadcast([P, TT, SLOTS]),
                                          ALU.is_equal)
                ins.then_inc(oh_ready, 1)

            one_hot(0, 0)
            with dve.Fori(0, n_quads) as q:
                def hidden(b):
                    dve.wait_ge(sg_done, b + 1 + q * 2)
                    dve.wait_ge(ht_done, b + 1 + q * 2)
                    v.tensor_tensor(hid[:, b, :], sg[:, b, :], ps[2 + b][:, 256:512], ALU.mult).then_inc(hid_done, 1)

                one_hot(1, q * 2)
                hidden(0)
                one_hot(2, q * 2)
                hidden(1)
                for n in range(KT):
                    dve.wait_ge(y_full, n + 2 + q * KT)
                    v.tensor_tensor(RD[:, n, :], RD[:, n, :], ps[6 + n % 2][:, :], ALU.add).then_inc(y_ev, 1)
                dve.wait_ge(y_ev, KT + 2 + q * KT)
            for k in range(KT):
                v.scalar_tensor_tensor(RA[:, k, :], RD[:, k, :], mod[:, 40 + k:41 + k], RA[:, k, :], ALU.mult,
                                       ALU.add).then_inc(x1_ok, 1)
            dve.wait_ge(x1_ok, 2 * KT)
            dve.wait_ge(rinv_ok, 5)
            for k in range(KT):
                v.scalar_tensor_tensor(RA[:, k, :], RA[:, k, :], V("g_final", k), RINV[:, :], ALU.mult,
                                       ALU.mult).then_inc(x2_ok, 1)
            dve.wait_ge(x2_ok, KT)
            dve.sem_inc(rinv_used, 1)
            dve.wait_ge(delta_ok, 1)
            di = OTK[:, 0, :].bitcast(I32)
            dj = OTK[:, 1, :].bitcast(I32)
            df = RH[:, 2, :]
            for m, (mask, op) in enumerate(((3, 0), (15, 0))):
                link(v.tensor_scalar(dj, di, mask, None, ALU.bitwise_and))
                link(v.tensor_copy(df, dj))
                link(v.tensor_scalar(RH[:, 3 + m, :], df, 0.0, None, ALU.is_equal))
            link(v.tensor_scalar(lnm, delta, 128.0, None, ALU.is_le))
            link(v.tensor_tensor(lnm, lnm, RH[:, 3, :], ALU.add))
            link(v.tensor_tensor(lnm, lnm, RH[:, 4, :], ALU.add))
            link(v.tensor_scalar(df, delta, 0.0, None, ALU.is_ge))
            link(v.tensor_tensor(df, df, lnm, ALU.mult))
            link(v.tensor_scalar(lnm, df, 0.0, NEG, ALU.is_equal, ALU.mult))
            link(v.tensor_scalar(RH[:, 3, :], df, 2.0, float(np.log(2.0)), ALU.is_equal, ALU.mult))
            link(v.tensor_scalar(RH[:, 4, :], df, 3.0, float(np.log(3.0)), ALU.is_equal, ALU.mult))
            link(v.tensor_tensor(lnm, lnm, RH[:, 3, :], ALU.add))
            link(v.tensor_tensor(lnm, lnm, RH[:, 4, :], ALU.add))
            dve.sem_inc(lnm_ok, 1)
            for i in range(24):
                if i % 2 == 0:
                    evict(PE_Q2 + i, q2_dst(i))
            attend(2)
            attend(3)
            dve.wait_ge(pv_done, 4 * NU)
            link(v.memset(convbuf[0][:, 0:3], 0.0))
            link(v.memset(convbuf[1][:, 0:3], 0.0))
            for i in range(12):
                buf = convbuf[i % 2]
                tile = RG[:, i, :] if i < 8 else RF[:, i - 8, :]
                dve.wait_ge(ev[i % 2], PE_XBC // 2 + i // 2 + 1)
                link(v.tensor_scalar(tile, buf[:, 0:T], V("conv_w", 4 * i), V("conv_b", i), ALU.mult, ALU.add))
                for w in range(1, 4):
                    ins = v.scalar_tensor_tensor(tile, buf[:, w:w + T], V("conv_w", 4 * i + w), tile, ALU.mult, ALU.add)
                    if w < 3:
                        link(ins)
                ins.then_inc(conv_ok, 1)
            dve.wait_ge(dt_full, 1)
            link(v.tensor_tensor(dt_t, ps[0][:, 0:64].rearrange("p (t h) -> p t h", t=TT),
                                 rows[:, R_DTB:R_DTB + 16].unsqueeze(1).to_broadcast([P, TT, 16]), ALU.add))
            link(v.scalar_tensor_tensor(tmp_t, dt_t, -1.0, dt_t, ALU.mult, ALU.min))
            link(v.tensor_scalar(dt_t, dt_t, 0.0, None, ALU.max))
            dve.sem_inc(sp1, 1)
            dve.wait_ge(sp2, 2)
            link(v.tensor_tensor(dt_t, dt_t, tmp_t, ALU.add))
            link(v.scalar_tensor_tensor(adt_t, dt_t, -1.0, aneg.unsqueeze(1).to_broadcast([P, TT, 16]), ALU.mult,
                                        ALU.mult))
            dve.sem_inc(adt_ok, 1)
            for i in range(8):
                if i % 2 == 0:
                    e = PE_XT + i
                    evict(e, ([(RCf[:, (i // 2) * D:(i // 2) * D + T], bank(e)[:, :])], 1.0))
            evict(PE_BT, ([(b_tok[:, 0, :, :], quad(bank(PE_BT)[:, :]))], 1.0))
            dve.wait_ge(cs_full, 1)
            link(v.tensor_copy(cs_t, ps[1][:, 0:64].rearrange("p (t h) -> p t h", t=TT)))
            link(v.tensor_copy(tot_t, ps[1][:, 64:128].rearrange("p (t h) -> p t h", t=TT)))
            link(v.tensor_tensor(tmp_t, tot_t, cs_t, ALU.subtract))
            dve.sem_inc(cs_ok, 1)
            dve.wait_ge(sp2, 3)

            def heads(ap, o=0, n=8):
                return ap[:, o:o + n].unsqueeze(2).to_broadcast([P, n, 64])

            def h8(ap):
                return ap.rearrange("p (h c) -> p h c", h=8)

            for c in range(TT):
                dve.wait_ge(cb_full, c + 1)
                if c > 0:
                    dve.wait_ge(mm_ok, 4 * c)
                v.tensor_tensor(cbm, ps[0][:, 0:256].rearrange("p (g l) -> p g l", g=2),
                                upper[:, :].unsqueeze(1).to_broadcast([P, 2, P]), ALU.mult).then_inc(cb_ok, 1)
                if c > 0:
                    dve.wait_ge(yd_full, c)
                for q in range(4):
                    dve.wait_ge(csb_full, 4 * c + q + 1)
                    for h in range(4):
                        ins = v.tensor_scalar(decay[:, 4 * q + h, :], ps[2 + q % 2][:, h * P:(h + 1) * P],
                                              cs_t[:, c, 4 * q + h:4 * q + h + 1], 0.0, ALU.subtract, ALU.min)
                    ins.then_inc(dd_ok, 1)
                dve.wait_ge(skip_ok, c + 1)
                dve.wait_ge(yd_full, c + 1)
                for g in range(2):
                    yt = y_tokT[:, c, 8 * g:8 * g + 8, :]
                    ins = v.tensor_tensor(yt, yt, h8(ps[4 + g][:, :]), ALU.add)
                link(ins)
                if c > 0:
                    dve.wait_ge(yo_full, c)
                    for g in range(2):
                        ins = v.tensor_tensor(y_off[:, 8 * g:8 * g + 8, :], h8(ps[g][:, :]),
                                              heads(sd_t[:, c, :], 8 * g), ALU.mult)
                    link(ins)
                    link(v.tensor_tensor(y_tokT[:, c, :, :], y_tokT[:, c, :, :], y_off, ALU.add))
                dve.sem_inc(y_tok, 1)
                if c < TT - 1:
                    dve.wait_ge(st_full, c + 1)
                    for g in range(2):
                        sv = h8(state[:, g, :])
                        if c == 0:
                            ins = v.tensor_copy(sv, h8(ps[6 + g][:, :]))
                        else:
                            link(v.tensor_tensor(sv, sv, heads(dec_t[:, c, :], 8 * g), ALU.mult))
                            ins = v.tensor_tensor(sv, sv, h8(ps[6 + g][:, :]), ALU.add)
                    link(ins)
                    dve.sem_inc(state_ok, 1)
            for i in range(8):
                if i % 2 == 0:
                    e = PE_YT + i
                    evict(e, ([(RG[:, 0:4, (i // 2) * P:(i // 2 + 1) * P], quad(bank(e)[:, :]))], 1.0))
            for idx, reg, g in ((6, RB, "att_g"), (7, RG, "ssm_g")):
                dve.wait_ge(rinv_ok, idx)
                for k in range(KT):
                    v.scalar_tensor_tensor(reg[:, k, :], reg[:, k, :], V(g, k), RINV[:, :], ALU.mult,
                                           ALU.mult).then_inc(mixn, 1)
                dve.wait_ge(mixn, KT * (idx - 5))
                dve.sem_inc(rinv_used, 1)
            for i in range(KT):
                e = PE_OUT + i
                dve.wait_ge(acc, e + 1)
                v.scalar_tensor_tensor(RA[:, i, :], RA[:, i, :], ALPHA, bank(e)[:, :], ALU.mult,
                                       ALU.add).then_inc(r_ok, 1)
                dve.wait_ge(r_ok, i + 1)
                dve.sem_inc(ev[e % 2], 1)
            dve.wait_ge(mu_full, 1)
            for k in range(KT):
                v.scalar_tensor_tensor(RC[:, k, :], ps[4][:, :], -1.0 / D, RA[:, k, :], ALU.mult,
                                       ALU.add).then_inc(cen_ok, 1)
            dve.wait_ge(cen_ok, KT)
            dve.wait_ge(rinv_ok, 8)
            for k in range(KT):
                link(v.scalar_tensor_tensor(RC[:, k, :], RC[:, k, :], V("ln_g", k), RINV[:, :], ALU.mult, ALU.mult))
                v.tensor_scalar(RC[:, k, :], RC[:, k, :], V("ln_b", k), None, ALU.add).then_inc(fin_ok, 1)

        @block.gpsimd
        def _(pool):
            g = nc.gpsimd
            links = [0]

            def link(ins):
                links[0] += 1
                ins.then_inc(pool_c, 1)
                pool.wait_ge(pool_c, links[0])

            link(g.memset(ones[:, :], 1.0))
            link(g.memset(ident[:, :], 0.0))
            g.memset(eps1, EPS1)
            g.memset(eps2, EPS2)
            link(g.affine_select(out=ident[:, :], in_=ident[:, :], compare_op=ALU.not_equal, fill=1.0, base=0,
                                 pattern=[[-1, P]], channel_multiplier=1))
            link(g.affine_select(out=upper[:, :], in_=ones[:, :], compare_op=ALU.is_ge, fill=0.0, base=0,
                                 pattern=[[1, P]], channel_multiplier=-1))
            g.memset(flip[:, :], 0.0).then_inc(flip_ev, 1)
            pool.wait_ge(flip_ev, 1)
            link(g.affine_select(out=flip[:, :], in_=flip[:, :], compare_op=ALU.not_equal, fill=1.0, base=1 - P,
                                 pattern=[[1, P]], channel_multiplier=1))
            pool.sem_inc(consts, 1)
            g.iota(iota64[:, :], [[1, SLOTS]], base=0, channel_multiplier=0, allow_small_or_imprecise_dtypes=True)
            for hf in range(2):
                link(g.iota(sel[:, hf:hf + 1], [[0, 1]], base=hf * P - MAXPASS * N_EXP, channel_multiplier=1,
                            allow_small_or_imprecise_dtypes=True))
                for r in range(4):
                    link(g.iota(sel[32 * r:32 * r + 32, 2 + hf:3 + hf], [[0, 1]], base=0, channel_multiplier=1,
                                allow_small_or_imprecise_dtypes=True))
                    link(g.memset(sel[32 * r:32 * r + 32, 4 + hf:5 + hf], float((4 * hf + r) * SLOTS)))
            pool.sem_inc(sel_ok, 1)
            pool.wait_ge(rev_in, 16)
            g.tensor_copy(ext_row[:, 0:255], ext_row[:, 255:256].to_broadcast([HG, 255])).then_inc(ext_ok, 1)
            link(g.memset(MASK[:, :], 0.0))
            g.memset(MASK[0:64, 448:512], NEG)
            g.memset(RD[96:128, 0:8:2, :], 0.0)
            g.memset(RD[0:32, 1:8:2, :], 0.0)
            g.memset(RE[96:128, 0:8:2, :], 0.0)
            link(g.memset(RE[0:32, 1:8:2, :], 0.0))
            pool.sem_inc(zero_ok, 1)
            for k in range(KT):
                pool.wait_ge(mod_h, k + 1)
                g.tensor_scalar(RB[:, k, :], RB[:, k, :], mod[:, k:k + 1], None, ALU.add).then_inc(h_ok, 1)
            pool.wait_ge(flip_ev, HG + 1)
            g.memset(RG[0:64, :, 448:512], NEG).then_inc(bias_ok, 1)
            for k in range(KT):
                pool.wait_ge(mod_h, KT + k + 1)
                g.tensor_scalar(RB[:, k, :], RB[:, k, :], mod[:, 24 + k:25 + k], None, ALU.add).then_inc(h_ok, 1)
            pool.wait_ge(pv_done, 2 * NU)
            link(g.memset(RD[:, :, :], 0.0))
            pool.sem_inc(y0_ok, 1)
            pool.wait_ge(route_ok, 1)
            pool.wait_ge(list_ok, 1)
            n_quads = pool.value_load(nqi[0:1, 0:1], min_val=1, max_val=MAX_QUADS)
            pool.sem_inc(ohw_ready, 1)
            with pool.Fori(0, n_quads) as q:
                for b in range(2):
                    pool.wait_ge(st_t, b + 1 + q * 2)
                    pool.wait_ge(oh_ready, b + 1 + q * 2)
                    for u in range(2):
                        e = pool.value_load(units[0:1, 1, bass.ds(q * 4 + 2 * b + u, 1)], min_val=0, max_val=N_EXP - 1)
                        ins = g.tensor_tensor(OHW[:, b, :, u * SLOTS:(u + 1) * SLOTS],
                                              OH[:, b, :, u * SLOTS:(u + 1) * SLOTS],
                                              combr[:, bass.ds(e * TT, TT)].unsqueeze(2).to_broadcast([P, TT, SLOTS]),
                                              ALU.mult)
                    ins.then_inc(ohw_ready, 1)
            pool.wait_ge(x2_ok, KT)
            g.iota(delta, [[-1, T]], base=T - P, channel_multiplier=1, allow_small_or_imprecise_dtypes=True)
            g.iota(OTK[:, 0, :].bitcast(I32), [[-1, T]], base=2 * T - P, channel_multiplier=1).then_inc(delta_ok, 1)
            pool.wait_ge(lnm_ok, 1)
            for h in range(2 * HG):
                if h >= HG:
                    pool.wait_ge(biased, 2 * NU + 24 + h - HG + 1)
                link(g.tensor_scalar(RG[:, h % HG, :], delta, -float(2.0 ** (-8.0 * (h + 1) / 16)), None, ALU.mult))
                g.tensor_tensor(RG[:, h % HG, :], RG[:, h % HG, :], lnm, ALU.add).then_inc(bias_ok, 1)
            for t in range(TT):
                pool.wait_ge(ev[0], (PE_XT + 2 * t) // 2 + 1)
                pool.wait_ge(ev[1], (PE_XT + 2 * t) // 2 + 1)
                pool.wait_ge(adt_ok, 1)
                g.tensor_tensor(xg_tok[:, t, :, :], xs_tok[:, t, :, :],
                                dt_t[:, t, :].unsqueeze(2).to_broadcast([P, SSM_H, SSM_P]), ALU.mult).then_inc(xg_ok, 1)
                g.tensor_tensor(y_tokT[:, t, :, :], xs_tok[:, t, :, :],
                                rows[:, R_DSKIP:R_DSKIP + 16].unsqueeze(2).to_broadcast([P, SSM_H, SSM_P]),
                                ALU.mult).then_inc(skip_ok, 1)
            pool.wait_ge(xg_ok, TT)
            pool.wait_ge(sp2, 3)
            for c in range(TT):
                if c < TT - 1:
                    if c > 0:
                        pool.wait_ge(st_full, c)
                    g.tensor_tensor(xgd, xg_tok[:, c, :, :],
                                    dte_t[:, c, :].unsqueeze(2).to_broadcast([P, SSM_H, SSM_P]),
                                    ALU.mult).then_inc(xgd_ok, 1)
                pool.wait_ge(cb_ok, c + 1)
                for q in range(4):
                    pool.wait_ge(ee_ok, 4 * c + q + 1)
                    g.tensor_tensor(decay[:, 4 * q:4 * q + 4, :], decay[:, 4 * q:4 * q + 4, :],
                                    cbm[:, q // 2, :].unsqueeze(1).to_broadcast([P, 4, P]), ALU.mult).then_inc(mm_ok, 1)
            pool.wait_ge(ev[0], PE_ZA // 2)
            pool.wait_ge(ev[1], PE_ZA // 2)
            for i in range(16):
                e = PE_ZA + i
                tile = RB[:, i, :] if i < KT else RG[:, i - KT, :]
                pool.wait_ge(ev[e % 2], e // 2 + 1)
                g.tensor_tensor(tile, tile, zbuf(i), ALU.mult).then_inc(mixp, 1)


def _tiles(w):
    m = w.shape[1] // P
    return w.reshape(KT, P, m, P).transpose(2, 1, 0, 3).reshape(m, P, D)


def _cols(v):
    return v.reshape(-1, P).T


def kernel(**inputs):
    import concourse.bacc as bacc
    from concourse.bass_utils import run_bass_kernel_spmd as run

    a = {k: np.ascontiguousarray(v) for k, v in inputs.items()}
    w_in = a["w_in"][0]
    swap = np.r_[16:32, 0:16]
    kr = 384 + np.arange(32)
    kr_cols = np.r_[kr, kr[swap], kr, kr[swap]]
    s1 = _tiles(np.concatenate([w_in[:, 0:384], w_in[:, kr_cols], w_in[:, 416:1952]], 1))
    ada = _tiles(a["w_ada"][0])
    uq = a["w_uq"][0]
    head = np.arange(8)[:, None] * 96
    nope = (head + np.arange(64)).reshape(4, P)
    rope_a = (head + 64 + np.arange(32)).reshape(2, P)
    rope_b = (head + 64 + swap).reshape(2, P)
    uq_cols = np.concatenate([nope, rope_a[0:1], rope_b[0:1], rope_a[1:2], rope_b[1:2]]).reshape(-1)
    uq_t = uq[:, uq_cols].reshape(2, P, 2, 4, P).transpose(2, 1, 3, 0, 4).reshape(2, P, D)
    ukv = np.concatenate([a["w_uk"][0], a["w_uv"][0]], 1)[None]
    ga, gb = _tiles(w_in[:, 1952:2976]), _tiles(w_in[:, 2976:4000])
    oab = _tiles(np.concatenate([a["w_oa"][0], a["w_ob"][0]], 0))
    first = [ada[0:16]]
    for i in range(16):
        first += [s1[i:i + 1], ada[16 + 2 * i:18 + 2 * i]]
    first += [uq_t, ukv]
    for i in range(KT):
        first += [ga[i:i + 1], gb[i:i + 1], oab[i:i + 1]]
    first += [_tiles(a["w_out"][0])]
    pre = np.concatenate(first, 0)
    gu = np.concatenate([a["w_gate"][0], a["w_up"][0]], 2).reshape(N_EXP, 4, 2, P, T).transpose(0, 1, 3, 2, 4)
    moe = np.concatenate([gu.reshape(N_EXP, 4, P, D), a["w_down"][0].reshape(N_EXP, 2, P, D)], 1)
    moe = moe.reshape(-1, P, D)
    w2 = a["w_in_2"][0]
    out2 = a["w_out_2"][0]
    pair = np.stack([_tiles(out2[0:D]), _tiles(out2[D:2 * D])], 1).reshape(-1, P, D)
    post = np.concatenate([_tiles(w2[:, 0:3072]), _tiles(w2[:, 5120:6656]), _tiles(w2[:, 3072:5120]), pair], 0)
    w_rt = np.concatenate([a["w_rg"][0], a["w_re"][0]], 1).reshape(KT, P, 36).transpose(1, 0, 2)
    w_dt = w2[:, 6656:6672].reshape(KT, P, 16).transpose(1, 0, 2)
    inv = (10000.0 ** (-np.arange(16, dtype=np.float32) / np.float32(16))).astype(np.float32)
    parts = {"c": _cols(a["c"][0]), "b_ada": _cols(a["b_ada"][0]), "g_mix": _cols(a["g_mix"][0]),
             "g_ffn": _cols(a["g_ffn"][0]), "g_final": _cols(a["g_final"]), "g_q": _cols(a["g_q"][0]),
             "g_kv": _cols(a["g_kv"][0]),
             "conv_w": a["conv_w_2"][0].reshape(4, 12, P).transpose(2, 1, 0).reshape(P, 48),
             "conv_b": _cols(a["conv_b_2"][0]), "att_g": _cols(a["att_norm_g_2"][0]),
             "ssm_g": _cols(a["ssm_norm_g_2"][0]), "ln_g": _cols(a["ln_g_2"][0]), "ln_b": _cols(a["ln_b_2"][0]),
             "inv": np.tile(inv, 8)[:, None], "sign": np.tile(np.repeat(np.float32([-1, 1]), 16), 4)[:, None]}
    vec = np.concatenate([parts[n] for n, _ in V_NAMES], 1)
    rows = np.concatenate([a["b_rg"][0], a["b_re"][0], a["dt_bias_2"][0], a["a_log_2"][0], a["d_skip_2"][0]])
    rel = a["rel_bias"][0][:, ::-1]
    arrays = {"xT": a["x"][0].T, "vec": vec, "rows": rows, "pos": a["positions"][0], "rel": rel, "w_rt": w_rt,
              "w_dt": w_dt, "w_pre": pre, "w_moe": moe, "w_post": post}
    nc = bacc.Bacc("TRN2", target_bir_lowering=False, num_devices=1)
    args = []
    for name in arrays:
        arrays[name] = np.ascontiguousarray(arrays[name])
        args.append(nc.dram_tensor(f"in_{name}", arrays[name].shape, mybir.dt.from_np(arrays[name].dtype),
                                   kind="ExternalInput").ap())
    args.append(nc.dram_tensor("outT", (D, T), F32, kind="ExternalOutput").ap())
    build(nc, *args)
    r = run(nc, [{f"in_{n}": v for n, v in arrays.items()}], core_ids=[0])
    return np.ascontiguousarray(r.results[0]["outT"].T)[None]
```

```python
from contextlib import ExitStack

import numpy as np

import concourse.bass as bass
from concourse import mybir

F32 = mybir.dt.float32
F32R = mybir.dt.float32r
I32 = mybir.dt.int32
ALU = mybir.AluOpType
ACT = mybir.ActivationFunctionType
AX_X = mybir.AxisListType.X

P = 128
T = 512
TT = T // P
D = 1024
KT = D // P
RING = 8
HG = 8
EPS1, EPS2 = 1e-6, 1e-5
NEG = -1e30
MLA_SCALE = 96 ** -0.5
N_EXP, SLOTS = 32, 64
MAXPASS = T // SLOTS
MAX_QUADS = 12
ALPHA = 2.0 ** 0.25
SSM_H, SSM_P = 16, 64

N_PRE = 16 + 48 + 3 + 24 + 8
N_ADA = 48
PAIR_TILES = 12
N_POST = 8 * 3 + 12 + 8 + 8 + 16

V_NAMES = [("c", 8), ("b_ada", 48), ("g_mix", 8), ("g_ffn", 8), ("g_final", 8), ("g_q", 2), ("g_kv", 1),
           ("conv_w", 48), ("conv_b", 12), ("att_g", 8), ("ssm_g", 8), ("ln_g", 8), ("ln_b", 8),
           ("inv", 1), ("sign", 1)]
V_AT, _n = {}, 0
for _name, _k in V_NAMES:
    V_AT[_name] = _n
    _n += _k
NV = _n
R_BR, R_DTB, R_ALOG, R_DSKIP, NR = 0, 36, 52, 68, 84
TWO_PI = 2 * np.pi
C1 = 6.28125
C2 = float(np.float32(np.float32((TWO_PI - C1) * 2 ** 22).astype(np.int64) // 4096 * 4096) / 2 ** 22)
C3 = float(TWO_PI - C1 - C2)
ROUND = 12582912.0


def build(nc, xT_d, vec_d, rows_d, pos_d, rel_d, wr_d, wdt_d, pre_d, moe_d, post_d, out_d):
    ctx = ExitStack()
    with ctx:
        def sb(name, shape, dt=F32):
            return ctx.enter_context(nc.sbuf_tensor(name, shape, dt))

        def sem(name):
            return ctx.enter_context(nc.semaphore(name))

        def region(name, shape):
            with nc.sbuf_tensor(name, shape, F32) as f:
                pass
            return f, ctx.enter_context(nc.sbuf_tensor(name + "_r", shape, F32R))

        ring, ring_r = region("ring", [P, PAIR_TILES, D])
        RA = sb("RA", [P, KT, T])
        RB, RBr = region("RB", [P, KT, T])
        RC, RCr = region("RC", [P, KT, T])
        RD, RDr = region("RD", [P, KT, T])
        RE, REr = region("RE", [P, KT, T])
        RF, RFr = region("RF", [P, KT, T])
        RG, RGr = region("RG", [P, KT, T])
        RH, RHr = region("RH", [P, KT, T])
        SB = sb("SB", [P, 2, T])
        PB = sb("PB", [P, 2, T])
        PTB = sb("PTB", [P, 2, T])
        OTK = sb("OTK", [P, 2, T])
        SQ = sb("SQ", [P, 2, T])
        RINV = sb("RINV", [P, T])
        MASK = sb("MASK", [P, T])
        ident = sb("ident", [P, P])
        ones = sb("ones", [P, P])
        upper = sb("upper", [P, P])
        flip = sb("flip", [P, P])
        vec = sb("vec", [P, NV])
        rows = sb("rows", [P, NR])
        small = sb("small", [P, 256])
        w_r = sb("w_r", [P, KT, 36])
        wdt = sb("wdt", [P, KT, 16])
        iota64 = sb("iota64", [P, SLOTS])
        nqi = sb("nqi", [1, 1], I32)
        units = sb("units", [1, 2, SLOTS], I32)
        sel = sb("sel", [P, 8])
        ps = [ctx.enter_context(nc.psum_tensor(f"ps{i}", [P, T], F32)) for i in range(8)]
        ext_d = nc.dram_tensor("ext_scratch", [HG, 640], F32, kind="Internal").ap()

        cact = small[:, 0:8]
        mod = small[:, 8:56]
        A1 = small[:, 56:64]
        A2 = small[:, 64:72]
        gt1h = small[:, 72:80]
        rowsum = small[:, 80:96]
        rsinv = small[:, 96:112]
        eps1 = small[:, 112:113]
        eps2 = small[:, 113:114]
        cnt = small[:, 114:118]
        aneg = small[:, 120:136]


        def slot_weight(b):
            return small[:, 144 + b:145 + b]

        def prod(m):
            return RF[:, 4 + m % 2 * 2:6 + m % 2 * 2, :].rearrange("p a b -> p (a b)")

        def ada_sum(m):
            return RH[:, 7, m % 2 * P:(m % 2 + 1) * P]

        def nmax(n):
            return small[:, 140 + n % 4:141 + n % 4]

        def zbuf(i):
            return (SB, PB)[i % 4 // 2][:, i % 2, :]

        ext_row = PTB[0:HG, :, :].rearrange("p a b -> p (a b)")[:, 0:640]
        cosT, sinT = PB[:, 0, :], PB[:, 1, :]
        qlT, kvT, krT = RH[:, 0:2, :], RH[:, 2, :], RH[:, 3, :]
        qnT, kvnT = RH[:, 4:6, :], RH[:, 6, :]
        qbT, kbT = RC[:, 0:4, :], RC[:, 4:8, :]
        vb, va = RF[:, 0:4, :], RF[:, 4:8, :]
        oaT, obT = RH[:, 0:4, :], RH[:, 4:8, :]
        RCf = RC[:, :, :].rearrange("p a b -> p (a b)")
        REf = RE[:, :, :].rearrange("p a b -> p (a b)")
        RFf = RF[:, :, :].rearrange("p a b -> p (a b)")
        RDf = RD[:, :, :].rearrange("p a b -> p (a b)")
        RHf = RH[:, :, :].rearrange("p a b -> p (a b)")
        RGf = RG[:, :, :].rearrange("p a b -> p (a b)")
        h2_hi, h2_lo = (r.rearrange("p (t a) c -> p t (a c)", t=TT) for r in (RCr, RGr))
        h2_raw = RGf.rearrange("p (t d) -> p t d", t=TT)
        posm = RFf[:, 0:(MAXPASS * N_EXP + 1) * TT]
        combr = RFf[:, 1040:1040 + N_EXP * TT]
        Zh, Zl = (RBr[:, 4 * i:4 * i + 4, :].rearrange("p (a b) c -> p a (b c)", a=2) for i in range(2))
        OHr = REr[:, 0:2, :].rearrange("p a (t s) -> p a t s", t=TT)
        OH = OHr.bitcast(F32)
        Xs = RFf[:, 2048:4096].rearrange("p (a d) -> p a d", a=2)
        OHW = REf[:, 1024:2048].rearrange("p (a t s) -> p a t s", a=2, t=TT)
        St = REr[:, 4:6, :]
        hid = REf[:, 3072:3584].rearrange("p (a f) -> p a f", a=2)
        hidT = REf[:, 3584:4096].rearrange("p (a f s) -> p a f s", a=2, f=2)
        Xg = RHf[:, 0:2048].rearrange("p (a k s) -> p a k s", a=2, k=KT)
        sg = RHf[:, 2048:2560].rearrange("p (a x) -> p a x", a=2)
        ranked = OTK[:, 1, 384:512].rearrange("p (a u) -> p a u", a=2)
        chosen = OTK[:, 0, 0:TT * N_EXP].rearrange("p (t e) -> p t e", t=TT)
        xs_tok, xg_tok, y_tokT = (r.rearrange("p (t h c) -> p t h c", t=TT, h=SSM_H) for r in (RCf, RHf, RDf))
        decay = REf[:, 0:2048].rearrange("p (h l) -> p h l", h=SSM_H)
        xgd = REf[:, 2048:3072].rearrange("p (h c) -> p h c", h=SSM_H)
        y_off = REf[:, 3072:4096].rearrange("p (h c) -> p h c", h=SSM_H)
        convbuf = [REf[:, 0:T + 3], REf[:, 1024:1024 + T + 3]]
        b_tok = RFf[:, 2048:3072].rearrange("p (g t n) -> p g t n", g=2, t=TT)
        state = RFf[:, 3072:4096].rearrange("p (g x) -> p g x", g=2)
        dt_t, cs_t, tot_t, adt_t, sd_t, dte_t, dec_t, tmp_t = (
            MASK[:, i * 64:(i + 1) * 64].rearrange("p (t h) -> p t h", t=TT) for i in range(8))
        cbm = OTK[:, 0, 0:256].rearrange("p (g l) -> p g l", g=2)
        delta, lnm = RH[:, 0, :], RH[:, 1, :]
        v2 = REf.rearrange("p (t d) -> p t d", t=TT)

        w_in = [sem(f"w_in{n}") for n in range(RING)]
        w_moe = [sem(f"w_moe{n}") for n in range(PAIR_TILES)]
        w_in2 = [sem(f"w_in2_{n}") for n in range(RING)]
        w_hi = sem("w_hi")
        w_split = sem("w_split")
        half_used = sem("half_used")
        prod_ok = sem("prod_ok")
        prod_dve = sem("prod_dve")
        red_ok = sem("red_ok")
        ada_done = sem("ada_done")
        x_hi = sem("x_hi")
        x_lo = sem("x_lo")
        h_lo = sem("h_lo")
        oab_hi = sem("oab_hi")
        oab_lo = sem("oab_lo")
        moe_used = sem("moe_used")
        dn_half = sem("dn_half")
        ht_done = sem("ht_done")
        ht_ev = sem("ht_ev")
        cnt_full = sem("cnt_full")
        flag_ok = sem("flag_ok")
        rank_full = sem("rank_full")
        rank_ok = sem("rank_ok")
        list_full = sem("list_full")
        x_in = sem("x_in")
        c_in = sem("c_in")
        wr_in = sem("wr_in")
        wdt_in = sem("wdt_in")
        rev_in = sem("rev_in")
        ext_out = sem("ext_out")
        bias_in = sem("bias_in")
        consts = sem("consts")
        cact_ok = sem("cact_ok")
        sq_ready = sem("sq_ready")
        sq_used = sem("sq_used")
        rinv_ok = sem("rinv_ok")
        rinv_used = sem("rinv_used")
        h_ok = sem("h_ok")
        acc = sem("acc")
        ev = [sem("ev0"), sem("ev1")]
        lat_n = sem("lat_n")
        lat_ok = sem("lat_ok")
        s_full = sem("s_full")
        biased = sem("biased")
        p_ready = sem("p_ready")
        pt_full = sem("pt_full")
        pt_ready = [sem("pt_ready0"), sem("pt_ready1")]
        pv_done = sem("pv_done")
        o_ready = sem("o_ready")
        bias_ok = sem("bias_ok")
        g_used = sem("g_used")
        g_tanh = sem("g_tanh")
        g_done = sem("g_done")
        x1_ok = sem("x1_ok")
        lg_raw = sem("lg_raw")
        lg_sb = sem("lg_sb")
        lg_full = sem("lg_full")
        mask_ok = sem("mask_ok")
        pos_full = sem("pos_full")
        route_ok = sem("route_ok")
        list_ok = sem("list_ok")
        oh_ready = sem("oh_ready")
        ohw_ready = sem("ohw_ready")
        pool_w = sem("pool_w")
        got = sem("got")
        st_t = sem("st_t")
        xs_ev = sem("xs_ev")
        xt_done = sem("xt_done")
        x_ev = sem("x_ev")
        sg_done = sem("sg_done")
        hid_done = sem("hid_done")
        z_hi = sem("z_hi")
        z_ev = sem("z_ev")
        st_ev = sem("st_ev")
        y_full = sem("y_full")
        y_ev = sem("y_ev")
        x2_ok = sem("x2_ok")
        lnm_ok = sem("lnm_ok")
        dt_full = sem("dt_full")
        mod_ok = sem("mod_ok")
        rope_ok = sem("rope_ok")
        ang_ok = sem("ang_ok")
        pos_in = sem("pos_in")
        zero_ok = sem("zero_ok")
        y0_ok = sem("y0_ok")
        ext_ok = sem("ext_ok")
        h2t_ok = sem("h2t_ok")
        sp1 = sem("sp1")
        sp2 = sem("sp2")
        xg_ok = sem("xg_ok")
        yd_full = sem("yd_full")
        yo_full = sem("yo_full")
        st_full = sem("st_full")
        mixp = sem("mixp")
        adt_ok = sem("adt_ok")
        conv_ok = sem("conv_ok")
        xbc_ok = sem("xbc_ok")
        cs_full = sem("cs_full")
        cs_ok = sem("cs_ok")
        cb_full = sem("cb_full")
        cb_ok = sem("cb_ok")
        csb_full = sem("csb_full")
        dd_ok = sem("dd_ok")
        ee_ok = sem("ee_ok")
        mm_ok = sem("mm_ok")
        xgd_ok = sem("xgd_ok")
        state_ok = sem("state_ok")
        y_tok = sem("y_tok")
        mixn = sem("mixn")
        r_ok = sem("r_ok")
        mod_h = sem("mod_h")
        sel_ok = sem("sel_ok")
        flip_full = sem("flip_full")
        flip_ev = sem("flip_ev")
        delta_ok = sem("delta_ok")
        skip_ok = sem("skip_ok")
        cen_ok = sem("cen_ok")
        mu_full = sem("mu_full")
        fin_ok = sem("fin_ok")
        out_done = sem("out_done")
        dve_c, act_c, pool_c = sem("dve_chain"), sem("act_chain"), sem("pool_chain")

        def V(name, i=0, n=1):
            return vec[:, V_AT[name] + i:V_AT[name] + i + n]

        def slot(n):
            return ring[:, n % RING, :]

        def part(m):
            return ring_r[:, RING + m % 2, :]

        def remainder(m):
            return ring_r[:, RING + 2 + m % 2, :]

        M_S1, M_G, M_O, M_Q2, M_XBC, M_Z, M_OUT = 0, 12, 36, 44, 60, 72, 88

        def arrival(m):
            if m < M_Q2:
                n = 16 + 3 * m if m < M_G else 67 + m - M_G
                return w_in[n % RING], 16 * (n // RING + 1), slot(n)
            n = m - M_Q2 if m < M_XBC else 24 + m - M_XBC
            return w_in2[(N_PRE + n) % RING], 16 * (n // RING + 1), slot(N_PRE + n)

        def used(m):
            for first, e in ((M_Z, PE_ZA), (M_XBC, PE_XBC), (M_Q2, PE_Q2), (M_O, PE_O)):
                if first <= m < M_OUT:
                    return acc, e + m - first + 1
            if m >= M_OUT:
                i = (m - M_OUT) // 2
                return (acc, PE_OUT + i + 1) if m % 2 else (half_used, i + 1)
            return (acc, PE_S1 + m + 1) if m < M_G else (g_used, m - M_G + 1)

        def ada_tile(m):
            return m if m < 16 else 17 + (m - 16) // 2 * 3 + (m - 16) % 2

        ADA_DVE = range(1, 16, 3)

        def product(m):
            if m in ADA_DVE:
                return prod_dve, m // 3 + 1
            return prod_ok, m + 1 - len([d for d in ADA_DVE if d < m])

        def freed_pre(n):
            if n < 16:
                return product(n)
            if n < 64:
                i, r = (n - 16) // 3, (n - 16) % 3
                if r:
                    return product(15 + 2 * i + r)
                return (w_split, i + 1) if i < 12 else (acc, PE_S1 + i + 1)
            if n < 67:
                return acc, PE_U + (4, 8, 16)[n - 64]
            return w_split, n - 67 + M_G + 1

        def freed_post(n):
            if 16 <= n < 24:
                return acc, PE_Q2 + n + 1
            return w_split, (n + M_Q2 if n < 16 else n - 24 + M_XBC) + 1

        def moe_slot(j):
            return (N_PRE + j) % RING if j < RING else j

        PE_S1 = 0
        PE_U = PE_S1 + 16
        PE_OT = PE_U + 16
        PE_O = PE_OT + 8
        PE_H = PE_O + 8
        PE_Q2 = PE_H + 8
        PE_OT2 = PE_Q2 + 24
        PE_XBC = PE_OT2 + 8
        PE_XT = PE_XBC + 12
        PE_BT = PE_XT + 8
        PE_YT = PE_BT + 2
        PE_ZA = PE_YT + 8
        PE_ZS = PE_ZA + 8
        PE_OUT = PE_ZS + 8
        assert all(e % 2 == 0 for e in (PE_U, PE_OT, PE_O, PE_H, PE_Q2, PE_OT2, PE_XBC, PE_XT, PE_BT, PE_YT, PE_ZA))

        def bank(e):
            return ps[6 + e % 2]

        def half(ap, h):
            return ap[(h % 2) * 64:(h % 2) * 64 + 64, h // 2, :]

        bias_hc = RG

        def group_ops(g):
            if g == 0:
                return (lambda h, t: half(qbT, h)[:, t * P:(t + 1) * P], lambda h, w: half(kbT, h)[:, 0:w],
                        lambda h, j: vb[:, j, h * 64:h * 64 + 64], lambda h: bias_hc[:, h, :])
            if g == 1:
                return (lambda h, t: RD[:, h, t * P:(t + 1) * P], lambda h, w: RE[:, h, 0:w],
                        lambda h, j: va[:, j, h * 64:h * 64 + 64], lambda h: MASK[:, :])
            o = (g - 2) * HG
            return (lambda h, t: half(RC, h + o)[:, t * P:(t + 1) * P], lambda h, w: half(RD, h + o)[:, 0:w],
                    lambda h, j: v2[:, j, (h + o) * 64:(h + o) * 64 + 64], lambda h: bias_hc[:, h, :])

        Z_SPLIT = ((), (0, 1), (2, 3, 4), (5, 6, 7))
        OT_DST = [obT, oaT, RB[:, 0:4, :], RB[:, 4:8, :]]
        ORDER = list(range(TT))
        UNITS = [(o, h) for o in range(TT) for h in range(HG)]
        NU = len(UNITS)

        def ot_event(g, o):
            return (PE_OT if g < 2 else PE_OT2) + (g % 2) * TT + o

        ST_H1, ST_Q, ST_KV, ST_H2 = 0, 8, 10, 11
        ST_F, ST_AT, ST_SS, ST_VAR = 19, 27, 35, 43
        assert ST_SS == ST_AT + KT

        block = ctx.enter_context(nc.Block())

        @block.sync
        def _(sp):
            sp.dma_start(vec[:, :], vec_d).then_inc(c_in, 16)
            sp.dma_start(rows[:, :], rows_d.partition_broadcast(P)).then_inc(c_in, 16)
            for n in range(N_PRE):
                if n >= RING:
                    sp.wait_ge(*freed_pre(n - RING))
                sp.dma_start(slot(n), pre_d[n]).then_inc(w_in[n % RING], 16)
                if n in (5, 7):
                    a = (n - 5) * 2
                    sp.dma_start(RA[:, a:a + 4, :],
                                 xT_d[a * P:(a + 4) * P, :].rearrange("(k p) t -> p k t", p=P)).then_inc(x_in, 16)
            sp.wait_ge(list_ok, 1)
            n_quads = sp.value_load(nqi[0:1, 0:1], min_val=1, max_val=MAX_QUADS)
            at = [sp.value_load(units[0:1, 1, u:u + 1], min_val=0, max_val=N_EXP - 1) for u in range(2)]
            for j in range(PAIR_TILES):
                if j < RING:
                    sp.wait_ge(*freed_pre(N_PRE + j - RING))
                elif j == RING:
                    sp.wait_ge(acc, PE_O + KT)
                sp.dma_start(ring[:, moe_slot(j), :], moe_d[bass.ds(at[j % 2] * 6 + j // 2, 1)].squeeze(0)).then_inc(
                    w_moe[j], 16)
            with sp.Fori(1, n_quads * 2) as p:
                at = [sp.value_load(units[0:1, 1, bass.ds(p * 2 + u, 1)], min_val=0, max_val=N_EXP - 1)
                      for u in range(2)]
                for j in range(PAIR_TILES):
                    sp.wait_ge(moe_used, PAIR_TILES + 1 + j + p * PAIR_TILES)
                    sp.dma_start(ring[:, moe_slot(j), :],
                                 moe_d[bass.ds(at[j % 2] * 6 + j // 2, 1)].squeeze(0)).then_inc(w_moe[j], 16)
            for n in range(N_POST):
                if n < RING:
                    sp.wait_ge(moe_used, PAIR_TILES + 1 + n + n_quads * (2 * PAIR_TILES))
                else:
                    sp.wait_ge(*freed_post(n - RING))
                sp.dma_start(slot(N_PRE + n), post_d[n]).then_inc(w_in2[(N_PRE + n) % RING], 16)
            for k in range(KT):
                sp.wait_ge(fin_ok, k + 1)
                sp.dma_start(out_d[k * P:(k + 1) * P, :], RC[:, k, :]).then_inc(out_done, 16)
            sp.wait_ge(out_done, 16 * KT)

        @block.tensor
        def _(pe):
            mm = nc.tensor.matmul
            e_state = [0]

            def free_bank(e):
                assert e == e_state[0], (e, e_state[0])
                e_state[0] += 1
                if e >= 2:
                    pe.wait_ge(ev[e % 2], e // 2)

            def arrive(n):
                pe.wait_ge(w_in[n % RING], 16 * (n // RING + 1))

            def arrive2(n):
                s = (N_PRE + n) % RING
                pe.wait_ge(w_in2[s], 16 * (n // RING + 1))

            def column(e, w, x, free=None):
                free_bank(e)
                k_n = free or KT
                for k in range(k_n):
                    last = mm(bank(e)[:, :], w[:, k * P:(k + 1) * P], x(k), start=(k == 0), stop=(k == k_n - 1))
                last.then_inc(acc, 1)

            def split_tile(out, m, x, first=True, last=True, ready=None, n_k=KT):
                xh, xl = x
                pe.wait_ge(w_split, m + 1)
                for k in range(n_k):
                    if ready:
                        pe.wait_ge(ready[0], ready[1] + k + 1)
                    w = slice(k * P, (k + 1) * P)
                    mm(out, part(m)[:, w], xh(k), start=first and k == 0, stop=False)
                    mm(out, part(m)[:, w], xl(k), start=False, stop=False)
                    ins = mm(out, remainder(m)[:, w], xh(k), start=False, stop=last and k == n_k - 1)
                return ins

            def split_column(e, m, x, ready=None):
                free_bank(e)
                split_tile(bank(e)[:, :], m, x, ready=ready).then_inc(acc, 1)

            def two(hi, lo):
                return (lambda k: hi[:, k, :]), (lambda k: lo[:, k, :])

            def column_tok(e, w, x):
                free_bank(e)
                for t in range(TT):
                    for k in range(KT):
                        last = mm(bank(e)[:, t * P:(t + 1) * P], x(k)[:, t * P:(t + 1) * P],
                                  w[:, k * P:(k + 1) * P], start=(k == 0), stop=(k == KT - 1))
                last.then_inc(acc, 1)

            def stats(at, n, b, ks=None):
                for k in ks or range(n):
                    pe.wait_ge(sq_ready, at + k + 1)
                    mm(ps[b][:, :], ones[:, :], SQ[:, (at + k) % 2, :], start=(k == 0),
                       stop=(k == n - 1)).then_inc(sq_used, 1)

            def ada(m, b, base):
                pe.wait_ge(red_ok, m + 1)
                mm(ps[b][:, m - base:m - base + 1], ada_sum(m), ones[:, 0:1], start=True, stop=True).then_inc(ada_done, 1)

            def hT(k):
                return RB[:, k, :]

            def attend(g):
                ql, kr, vv, _ = group_ops(g)

                def scores(u):
                    o, h = UNITS[u]
                    t = ORDER[o]
                    n = g * NU + u
                    if n >= 2:
                        pe.wait_ge(biased, n - 1)
                    w = (t + 1) * P
                    mm(ps[n % 2][:, 0:w], ql(h, t), kr(h, w), start=True, stop=True).then_inc(s_full, 1)

                def turn(u):
                    o, h = UNITS[u]
                    t = ORDER[o]
                    n = g * NU + u
                    pe.wait_ge(p_ready, n + 1)
                    if n >= 2:
                        pe.wait_ge(pt_ready[n % 2], n // 2)
                    for j in range(t + 1):
                        last = nc.tensor.transpose(ps[2 + n % 2][:, j * P:(j + 1) * P],
                                                   PB[:, n % 2, j * P:(j + 1) * P], ident[:, :])
                    last.then_inc(pt_full, 1)

                def values(u):
                    o, h = UNITS[u]
                    t = ORDER[o]
                    n = g * NU + u
                    i = g * TT + o
                    pe.wait_ge(pt_ready[n % 2], n // 2 + 1)
                    if h == 0 and i >= 2:
                        pe.wait_ge(o_ready, i - 1)
                    for j in range(t + 1):
                        last = mm(ps[4 + i % 2][:, h * 64:h * 64 + 64], PTB[:, n % 2, j * P:(j + 1) * P], vv(h, j),
                                  start=(j == 0), stop=(j == t))
                    last.then_inc(pv_done, 1)

                def outputs(o):
                    i = g * TT + o
                    e = ot_event(g, o)
                    free_bank(e)
                    pe.wait_ge(o_ready, i + 1)
                    for c in range(4):
                        last = nc.tensor.transpose(bank(e)[:, c * P:(c + 1) * P], OTK[:, i % 2, c * P:(c + 1) * P],
                                                   ident[:, :])
                    last.then_inc(acc, 1)

                scores(0)
                scores(1)
                for u in range(NU + 1):
                    if u == HG and g != 1:
                        for _ in range(4):
                            mm(ps[6][:, :], ident[:, :], MASK[:, :], start=True, stop=True)
                    if u < NU:
                        turn(u)
                    if u + 2 < NU:
                        scores(u + 2)
                    if u >= 1:
                        values(u - 1)
                    if u >= 4 and (u - 4) % HG == 0 and u >= HG:
                        outputs((u - 4) // HG - 1)
                outputs(TT - 1)

            pe.wait_ge(consts, 1)
            for k in range(KT):
                ada(k, 0, 0)
            for k in range(KT):
                stats(ST_H1, KT, 2, ks=[k])
                ada(KT + k, 0, 0)
            for i in range(16):
                if i < 12:
                    split_column(PE_S1 + i, M_S1 + i, two(RDr, REr), ready=(h_lo, 0) if i == 0 else None)
                else:
                    arrive(16 + 3 * i)
                    column_tok(PE_S1 + i, slot(16 + 3 * i), hT)
                ada(16 + 2 * i, 1, 16)
                ada(17 + 2 * i, 1, 16)
                if i == 7:
                    stats(ST_Q, 2, 2)
                if i == 9:
                    stats(ST_KV, 1, 2)
            n = 64
            pe.wait_ge(lat_n, 3)
            for c in range(8):
                if c % 4 == 0:
                    arrive(n + c // 4)
                w = slot(n + c // 4)[:, (c % 4) * 256:(c % 4) * 256 + 256]
                column(PE_U + c, w, lambda k: qnT[:, k, :], free=2)
            arrive(n + 2)
            for c in range(4):
                column(PE_U + 8 + c, slot(n + 2)[:, c * P:(c + 1) * P], lambda k: kvnT, free=1)
            for t in range(TT):
                e = PE_U + 12 + t
                free_bank(e)
                mm(bank(e)[:, :], kvnT[:, t * P:(t + 1) * P], slot(n + 2)[:, 512:1024], start=True,
                   stop=True).then_inc(acc, 1)
            pe.wait_ge(ev[0], PE_OT // 2)
            pe.wait_ge(ev[1], PE_OT // 2)
            pe.wait_ge(bias_in, 16)
            for h in range(HG):
                if h >= 2:
                    pe.wait_ge(flip_ev, h)
                mm(ps[4 + h % 2][:, :], flip[:, :], RG[:, h, :], start=True, stop=True).then_inc(flip_full, 1)
            pe.wait_ge(flip_ev, HG + 1)
            pe.wait_ge(mod_ok, 2)
            attend(0)
            pe.wait_ge(lat_ok, 1)
            attend(1)
            pe.wait_ge(ev[0], (PE_O) // 2)
            pe.wait_ge(ev[1], (PE_O) // 2)
            pe.wait_ge(o_ready, 2 * TT)
            for i in range(KT):
                m = M_G + 3 * i
                b = 4 * ((i + 1) % 2)
                if i >= 2:
                    pe.wait_ge(g_done, i - 1)
                for s in range(2):
                    split_tile(ps[b + s][:, :], m + s, two(RGr, RCr),
                               ready=(x_lo, 0) if i == s == 0 else None).then_inc(g_used, 1)
                pe.wait_ge(w_split, m + 3)
                for s in range(2):
                    for k in range(4 * s, 4 * s + 4):
                        if i == 0:
                            pe.wait_ge(oab_lo, k + 1)
                        w = slice(k * P, (k + 1) * P)
                        out = ps[b + 2 + s][:, :]
                        mm(out, part(m + 2)[:, w], REr[:, k, :], start=(k % 4 == 0), stop=False)
                        mm(out, part(m + 2)[:, w], RFr[:, k, :], start=False, stop=False)
                        last = mm(out, remainder(m + 2)[:, w], REr[:, k, :], start=False, stop=(k % 4 == 3))
                last.then_inc(g_used, 1)
            pe.wait_ge(g_done, KT - 1)
            for i in range(KT):
                split_column(PE_O + i, M_O + i, two(RDr, RHr), ready=(g_done, 0) if i == 0 else None)
                if i >= 2:
                    stats(ST_H2, KT, 2, ks=[i - 2])
            stats(ST_H2, KT, 2, ks=[KT - 2, KT - 1])
            pe.wait_ge(wr_in, 16)
            for k in range(KT):
                pe.wait_ge(h_ok, KT + k + 1)
                last = mm(ps[0][0:36, :], w_r[:, k, :], hT(k), start=(k == 0), stop=(k == KT - 1))
            last.then_inc(lg_raw, 1)
            for i in range(KT):
                if i == 2:
                    pe.wait_ge(lg_sb, 1)
                    for t in range(TT):
                        last = nc.tensor.transpose(ps[1][:, t * 36:t * 36 + 36], PTB[0:36, 0, t * P:(t + 1) * P],
                                                   ident[0:36, 0:36])
                    last.then_inc(lg_full, 1)
                e = PE_H + i
                free_bank(e)
                t, hf = i // 2, i % 2
                for c in range(4):
                    last = nc.tensor.transpose(bank(e)[:, c * P:(c + 1) * P], hT(hf * 4 + c)[:, t * P:(t + 1) * P],
                                               ident[:, :])
                last.then_inc(acc, 1)
            pe.wait_ge(mask_ok, 1)
            for t in range(TT):
                for s in range(t + 1):
                    last = mm(ps[3][:, t * 32:t * 32 + 32], ones[:, :] if s < t else upper[:, :],
                              chosen[:, s, :], start=(s == 0), stop=(s == t))
            last.then_inc(pos_full, 1)
            for r in range(4):
                for s in range(TT):
                    last = mm(ps[4][32 * r:32 * r + 32, 0:1], chosen[:, s, :], ones[:, 0:1], start=(s == 0),
                              stop=(s == TT - 1))
            last.then_inc(cnt_full, 1)
            pe.wait_ge(flag_ok, 1)
            mm(ps[5][:, 0:1], upper[:, :], sel[:, 6:7], start=True, stop=True)
            mm(ps[5][:, 1:2], ones[:, :], sel[:, 6:7], start=True, stop=False)
            mm(ps[5][:, 1:2], upper[:, :], sel[:, 7:8], start=False, stop=True)
            mm(ps[5][:, 2:3], ones[:, :], sel[:, 6:7], start=True, stop=False)
            mm(ps[5][:, 2:3], ones[:, :], sel[:, 7:8], start=False, stop=True).then_inc(rank_full, 1)
            pe.wait_ge(rank_ok, 1)
            for i in range(2):
                for hf in range(2):
                    last = mm(ps[5][0:1, 64 + i * SLOTS:64 + (i + 1) * SLOTS], sel[:, 2 * i + hf:2 * i + hf + 1],
                              ranked[:, hf, :], start=(hf == 0), stop=(hf == 1))
            last.then_inc(list_full, 1)
            pe.wait_ge(ev[0], PE_Q2 // 2)
            pe.wait_ge(ev[1], PE_Q2 // 2)
            pe.wait_ge(route_ok, 1)
            pe.wait_ge(h2t_ok, KT)
            pe.wait_ge(list_ok, 1)
            n_quads = pe.value_load(nqi[0:1, 0:1], min_val=1, max_val=MAX_QUADS)
            pe.sem_inc(got, 2)
            pe.sem_inc(st_t, 2)
            pe.sem_inc(y_full, 1)
            pe.sem_inc(ht_done, 2)
            pe.sem_inc(moe_used, 2 * PAIR_TILES)

            def gather(b, q2):
                pe.wait_ge(oh_ready, b + 1 + q2)
                pe.wait_ge(x_ev, b + 1 + q2)
                for hf in range(2):
                    for t in range(TT):
                        for h2 in (h2_hi, h2_lo):
                            last = mm(ps[hf][:, :], OHr[:, b % 2, t, :], h2[:, t, hf * T:(hf + 1) * T],
                                      start=(t == 0 and h2 is h2_hi), stop=(t == TT - 1 and h2 is h2_lo))
                last.then_inc(got, 1)

            def turn_gathered(b, q2):
                pe.wait_ge(xs_ev, b + 1 + q2)
                for k in range(KT):
                    last = nc.tensor.transpose(ps[k // 4][:, (k % 4) * P:(k % 4 + 1) * P],
                                               Xs[:, b % 2, k * P:(k + 1) * P], ident[:, :])
                last.then_inc(xt_done, 1)

            gather(0, 0)
            turn_gathered(0, 0)
            with pe.Fori(0, n_quads) as q:
                def arrive_pair(b, j):
                    pe.wait_ge(w_moe[j], 16 * (1 + b) + q * 32)

                def gate_up(b):
                    pe.wait_ge(x_ev, b + 2 + q * 2)
                    pe.wait_ge(ht_ev, b + 1 + q * 2)
                    for s in range(4):
                        for u in range(2):
                            arrive_pair(b, 2 * s + u)
                        for k in range(2):
                            kk = 2 * s + k
                            for u in range(2):
                                last = mm(ps[2 + b][u * SLOTS:(u + 1) * SLOTS, :],
                                          Xg[:, b, kk, u * SLOTS:(u + 1) * SLOTS],
                                          ring[:, moe_slot(2 * s + u), k * T:(k + 1) * T],
                                          start=(kk == 0), stop=(kk == KT - 1))
                        last.then_inc(moe_used, 2)

                def down(b):
                    pe.wait_ge(hid_done, b + 1 + q * 2)
                    for f in range(2):
                        last = nc.tensor.transpose(ps[2 + b][:, f * P:(f + 1) * P], hid[:, b, f * P:(f + 1) * P],
                                                   ident[:, :])
                    pe.wait_ge(ohw_ready, b + 2 + q * 2)
                    mm(ps[2 + b][:, 256:257], OHW[:, b, 0, :], ones[:, 0:1], start=True, stop=True).then_inc(ht_done, 1)
                    turn_gathered(b + 1, q * 2)
                    pe.wait_ge(ht_ev, b + 3 + q * 2)
                    for j in range(8, 12):
                        arrive_pair(b, j)
                    for hf in range(2):
                        pe.wait_ge(z_ev, 2 * b + hf + 1 + q * 4)
                        for f in range(2):
                            for u in range(2):
                                last = mm(ps[4 + hf][u * SLOTS:(u + 1) * SLOTS, :],
                                          hidT[:, b, f, u * SLOTS:(u + 1) * SLOTS],
                                          ring[:, moe_slot(8 + 2 * f + u), hf * T:(hf + 1) * T],
                                          start=(f == 0), stop=(f == 1))
                        if hf == 0:
                            last.then_inc(dn_half, 1)
                    last.then_inc(moe_used, 4)

                def turn_slots(b):
                    pe.wait_ge(y_ev, b + 1 + q * KT)
                    for t in range(TT):
                        last = nc.tensor.transpose(ps[6 + b][:, t * P:(t + 1) * P], OH[:, b, t, :], ident[:, :])
                    last.then_inc(st_t, 1)

                gate_up(0)
                gather(1, q * 2)
                turn_slots(0)
                turn_slots(1)
                down(0)
                gate_up(1)
                gather(2, q * 2)
                down(1)
                pe.wait_ge(st_ev, 2 + q * 2)
                for n in range(KT):
                    if n % 4 == 0:
                        pe.wait_ge(z_ev, 5 + n // 4 + q * 4)
                    if n >= 2:
                        pe.wait_ge(y_ev, n + 1 + q * KT)
                    for b in range(2):
                        for Z in (Zh, Zl):
                            last = mm(ps[6 + n % 2][:, :], Z[:, b, n * P:(n + 1) * P], St[:, b, :],
                                      start=(b == 0 and Z is Zh), stop=(b == 1 and Z is Zl))
                    last.then_inc(y_full, 1)
            stats(ST_F, KT, 2)
            pe.wait_ge(x2_ok, KT)
            xT = lambda k: RA[:, k, :]
            for i in range(24):
                e = PE_Q2 + i
                if i < 16:
                    split_column(e, M_Q2 + i, two(RBr, RFr), ready=(x_lo, 8) if i == 0 else None)
                else:
                    arrive2(i)
                    column_tok(e, slot(N_PRE + i), xT)
            pe.wait_ge(ev[0], PE_OT2 // 2)
            pe.wait_ge(ev[1], PE_OT2 // 2)
            for g in (2, 3):
                attend(g)
            for i in range(12):
                split_column(PE_XBC + i, M_XBC + i, two(RCr, RDr), ready=(x_lo, 16) if i == 0 else None)
            pe.wait_ge(wdt_in, 16)
            for t in range(TT):
                for k in range(KT):
                    last = mm(ps[0][:, t * 16:t * 16 + 16], xT(k)[:, t * P:(t + 1) * P], wdt[:, k, :],
                              start=(k == 0), stop=(k == KT - 1))
            last.then_inc(dt_full, 1)
            pe.wait_ge(xbc_ok, 8)
            for i in range(8):
                e = PE_XT + i
                free_bank(e)
                t, hf = i // 2, i % 2
                for c in range(4):
                    last = nc.tensor.transpose(bank(e)[:, c * P:(c + 1) * P],
                                               RG[:, hf * 4 + c, t * P:(t + 1) * P], ident[:, :])
                last.then_inc(acc, 1)
            pe.wait_ge(xbc_ok, 12)
            for g in range(2):
                e = PE_BT + g
                free_bank(e)
                for t in range(TT):
                    last = nc.tensor.transpose(bank(e)[:, t * P:(t + 1) * P], RF[:, g, t * P:(t + 1) * P], ident[:, :])
                last.then_inc(acc, 1)
            pe.wait_ge(adt_ok, 1)
            for c in range(TT):
                mm(ps[1][:, c * 16:c * 16 + 16], upper[:, :], adt_t[:, c, :], start=True, stop=True)
            for c in range(TT):
                last = mm(ps[1][:, 64 + c * 16:80 + c * 16], ones[:, :], adt_t[:, c, :], start=True, stop=True)
            last.then_inc(cs_full, 1)
            pe.wait_ge(ev[0], PE_YT // 2)
            pe.wait_ge(ev[1], PE_YT // 2)
            pe.wait_ge(cs_ok, 1)
            for c in range(TT):
                if c >= 1:
                    pe.wait_ge(y_tok, c)
                for g in range(2):
                    last = mm(ps[0][:, g * P:(g + 1) * P], RF[:, g, c * P:(c + 1) * P], RF[:, 2 + g, c * P:(c + 1) * P],
                              start=True, stop=True)
                last.then_inc(cb_full, 1)
                for q in range(4):
                    if 4 * c + q >= 2:
                        pe.wait_ge(dd_ok, 4 * c + q - 1)
                    for h in range(4):
                        last = mm(ps[2 + q % 2][:, h * P:(h + 1) * P],
                                  adt_t[:, c, 4 * q + h:4 * q + h + 1].to_broadcast([P, P]), upper[:, :],
                                  start=True, stop=True)
                    last.then_inc(csb_full, 1)
                if c == 0:
                    pe.wait_ge(xg_ok, TT)
                for h in range(SSM_H):
                    if h % 4 == 0:
                        pe.wait_ge(mm_ok, 4 * c + h // 4 + 1)
                    last = mm(ps[4 + h // 8][:, (h % 8) * 64:(h % 8) * 64 + 64], decay[:, h, :], xg_tok[:, c, h, :],
                              start=True, stop=True)
                last.then_inc(yd_full, 1)
                if c > 0:
                    pe.wait_ge(state_ok, c)
                    pe.wait_ge(cb_ok, c + 1)
                    for g in range(2):
                        last = mm(ps[g][:, :], RF[:, 2 + g, c * P:(c + 1) * P], state[:, g, :], start=True, stop=True)
                    last.then_inc(yo_full, 1)
                if c < TT - 1:
                    pe.wait_ge(xgd_ok, c + 1)
                    for g in range(2):
                        last = mm(ps[6 + g][:, :], b_tok[:, g, c, :], REf[:, 2048 + g * T:2048 + (g + 1) * T], start=True, stop=True)
                    last.then_inc(st_full, 1)
            for i in range(8):
                e = PE_YT + i
                t, hf = i // 2, i % 2
                free_bank(e)
                pe.wait_ge(y_tok, TT)
                for c in range(4):
                    last = nc.tensor.transpose(bank(e)[:, c * P:(c + 1) * P],
                                               RDf[:, t * D + (hf * 4 + c) * P:t * D + (hf * 4 + c + 1) * P], ident[:, :])
                last.then_inc(acc, 1)
            def mix_stats(i):
                stats(*((ST_AT, KT, 2) if i < KT else (ST_SS, KT, 3)), ks=[i % KT])

            for i in range(16):
                split_column(PE_ZA + i, M_Z + i, two(RCr, RGr), ready=(x_lo, 24) if i == 0 else None)
                if i >= 2:
                    mix_stats(i - 2)
            mix_stats(14)
            mix_stats(15)
            def mean(k):
                pe.wait_ge(r_ok, k + 1)
                return mm(ps[4][:, :], ones[:, :], RA[:, k, :], start=(k == 0), stop=(k == KT - 1))

            for i in range(KT):
                e = PE_OUT + i
                free_bank(e)
                for s, x in ((0, two(RDr, REr)), (1, two(RFr, RCr))):
                    last = split_tile(bank(e)[:, :], M_OUT + 2 * i + s, x, first=(s == 0), last=(s == 1),
                                      ready=(x_lo, 32 + KT * s) if i == 0 else None)
                    last.then_inc(*((acc, 1) if s else (half_used, 1)))
                if i:
                    mean(i - 1)
            mean(KT - 1).then_inc(mu_full, 1)
            stats(ST_VAR, KT, 5)

        def tok_dst(view, t, hf):
            return view[:, t, hf * T:(hf + 1) * T]

        def quad(ap):
            return ap.rearrange("p (a b) -> p a b", a=4)

        def s1_dst(i):
            b = bank(PE_S1 + i)
            if i < 2:
                return [(qlT[:, i, :], b[:, :])], 1.0
            if i == 2:
                return [(kvT, b[:, :])], 1.0
            if i == 3:
                return [(krT, b[:, :])], 1.0
            if i < 8:
                return [(qbT[:, i - 4, :], b[:, :])], 0.125
            if i < 12:
                return [(kbT[:, i - 8, :], b[:, :])], 1.0
            return [(vb[:, :, (i - 12) * P:(i - 11) * P], quad(b[:, :]))], 1.0

        def u_dst(c):
            b = bank(PE_U + c)
            if c < 4:
                return [(RD[0:64, 2 * c, :], b[0:64, :]), (RD[64:128, 2 * c + 1, :], b[64:128, :])], MLA_SCALE
            if c < 8:
                return [((OTK if c % 2 == 0 else PTB)[:, (c - 4) // 2, :], b[:, :])], MLA_SCALE
            if c < 12:
                j = c - 8
                return [(RE[0:64, 2 * j, :], b[0:64, :]), (RE[64:128, 2 * j + 1, :], b[64:128, :])], 1.0
            return [(va[:, c - 12, :], b[:, :])], 1.0

        def q2_dst(i):
            b = bank(PE_Q2 + i)
            if i < 8:
                return [(RC[:, i, :], b[:, :])], 0.125
            if i < 16:
                return [(RD[:, i - 8, :], b[:, :])], 1.0
            return [(v2[:, :, (i - 16) * P:(i - 15) * P], quad(b[:, :]))], 1.0

        def ot_dst(g, o):
            t = ORDER[o]
            return [(OT_DST[g][:, :, t * P:(t + 1) * P], quad(bank(ot_event(g, o))[:, :]))], 1.0

        def multiply_ada(queue, engine, m):
            n = ada_tile(m)
            queue.wait_ge(w_in[n % RING], 16 * (n // RING + 1))
            if m >= 2:
                queue.wait_ge(red_ok, m - 1)
            engine.tensor_tensor(prod(m).rearrange("p (k n) -> p k n", k=KT),
                                 slot(n).rearrange("p (k n) -> p k n", k=KT),
                                 cact.unsqueeze(2).to_broadcast([P, KT, P]), ALU.mult).then_inc(product(m)[0], 1)

        @block.scalar
        def _(act):
            A = nc.scalar.activation
            links = [0]

            def link(ins):
                links[0] += 1
                ins.then_inc(act_c, 1)
                act.wait_ge(act_c, links[0])

            def evict(e, what):
                pairs, scale = what
                act.wait_ge(acc, e + 1)
                for dst, src in pairs:
                    ins = A(dst, src, ACT.Copy, scale=scale)
                ins.then_inc(ev[e % 2], 1)

            def norm(idx, at, n, b, src, ready, eps):
                for k in range(n):
                    ready(k)
                    if at + k >= 2:
                        act.wait_ge(sq_used, at + k - 1)
                    A(SQ[:, (at + k) % 2, :], src(k), ACT.Square).then_inc(sq_ready, 1)
                root(idx, at, n, b, eps)

            def root(idx, at, n, b, eps):
                act.wait_ge(sq_used, at + n)
                if idx > 0:
                    act.wait_ge(rinv_used, idx)
                link(A(RINV[:, :], ps[b][:, :], ACT.Ln, scale=1.0 / (n * P), bias=eps))
                A(RINV[:, :], RINV[:, :], ACT.Exp, scale=-0.5).then_inc(rinv_ok, 1)

            def hi(m):
                s, count, tile = arrival(m)
                act.wait_ge(s, count)
                if m >= 2:
                    act.wait_ge(*used(m - 2))
                A(part(m), tile, ACT.Copy).then_inc(w_hi, 1)

            def attend(g):
                def evict_pt(u):
                    n = g * NU + u
                    if n % 2 == 0:
                        return
                    w = (ORDER[UNITS[u][0]] + 1) * P
                    act.wait_ge(pt_full, n + 1)
                    if n >= 2:
                        act.wait_ge(pv_done, n - 1)
                    A(PTB[:, 1, 0:w], ps[3][:, 0:w], ACT.Copy).then_inc(pt_ready[1], 1)

                for u in range(NU):
                    o, h = UNITS[u]
                    t = ORDER[o]
                    n, i = g * NU + u, g * TT + o
                    w = (t + 1) * P
                    act.wait_ge(biased, n + 1)
                    if n >= 2:
                        act.wait_ge(pt_full, n - 1)
                    if h == 0 and i >= 2:
                        act.wait_ge(o_ready, i - 1)
                    A(PB[:, n % 2, 0:w], SB[:, n % 2, 0:w], ACT.Exp, scale=-1.0, bias=nmax(n),
                      accum_out=rowsum[:, (i % 2) * HG + h:(i % 2) * HG + h + 1]).then_inc(p_ready, 1)
                    if u >= 1:
                        evict_pt(u - 1)
                    if u % HG == 5 and u > HG:
                        o_o = u // HG - 1
                        if ot_event(g, o_o) % 2:
                            evict(ot_event(g, o_o), ot_dst(g, o_o))
                evict_pt(NU - 1)
                if ot_event(g, TT - 1) % 2:
                    evict(ot_event(g, TT - 1), ot_dst(g, TT - 1))

            act.dma_start(OTK[:, 0, :].bitcast(I32), pos_d.partition_broadcast(P)).then_inc(pos_in, 16)
            act.dma_start(ext_row[:, 255:640], rel_d[:, 0:385]).then_inc(rev_in, 16)
            act.dma_start(w_r[:, :, :], wr_d).then_inc(wr_in, 16)
            act.dma_start(wdt[:, :, :], wdt_d).then_inc(wdt_in, 16)
            act.wait_ge(c_in, 32)
            A(cact, V("c", 0, 8), ACT.Silu).then_inc(cact_ok, 1)
            act.wait_ge(x_in, 32)
            act.wait_ge(consts, 1)
            norm(0, ST_H1, KT, 2, lambda k: RA[:, k, :], lambda k: None, eps1)
            act.wait_ge(ext_ok, 1)
            act.dma_start(ext_d, ext_row[:, :]).then_inc(ext_out, 16)
            act.wait_ge(ext_out, 16)
            act.dma_start(RG[:, :, :], bass.AP(ext_d.tensor, 0, [[1, P], [640, HG], [1, T]])).then_inc(bias_in, 16)
            hi(0)
            hi(1)
            for k in range(KT + 1):
                if k < KT:
                    act.wait_ge(mod_h, k + 1)
                    A(RB[:, k, :], RB[:, k, :], ACT.Identity, bias=mod[:, k:k + 1]).then_inc(h_ok, 1)
                if k:
                    act.wait_ge(h_ok, k)
                    A(RDr[:, k - 1, :], RB[:, k - 1, :], ACT.Copy).then_inc(x_hi, 1)
            for i in range(16):
                if i + 2 < M_G:
                    hi(i + 2)
                if i == 14:
                    act.wait_ge(ang_ok, 2)
                    A(sinT, sinT, ACT.Sin)
                    A(cosT, cosT, ACT.Sin).then_inc(rope_ok, 1)
                if i % 2:
                    evict(PE_S1 + i, s1_dst(i))
                if i == 7:
                    act.wait_ge(ev[0], 1)
                    norm(1, ST_Q, 2, 2, lambda k: qlT[:, k, :], lambda k: None, eps1)
                if i == 9:
                    act.wait_ge(ev[0], 2)
                    norm(2, ST_KV, 1, 2, lambda k: kvT, lambda k: None, eps1)
            for c in range(16):
                if c % 2:
                    evict(PE_U + c, u_dst(c))
            hi(M_G)
            hi(M_G + 1)
            act.wait_ge(lat_ok, 1)
            attend(0)
            attend(1)
            act.wait_ge(pt_full, 2 * NU)
            act.wait_ge(s_full, 2 * NU)
            for p in range(2):
                act.wait_ge(ev[p], PE_O // 2)
            for k in range(KT):
                A(REr[:, k, :], RH[:, k, :], ACT.Copy).then_inc(oab_hi, 1)
            for i in range(KT):
                if i >= 2:
                    act.wait_ge(g_done, i - 1)
                b = 4 * ((i + 1) % 2)
                act.wait_ge(g_used, 3 * i + 1)
                hi(M_G + 3 * i + 2)
                A(SB[:, i % 2, :], ps[b][:, :], ACT.Tanh, scale=0.5)
                hi(M_G + 3 * i + 3)
                act.wait_ge(g_used, 3 * i + 2)
                A(PB[:, i % 2, :], ps[b + 1][:, :], ACT.Tanh, scale=0.5).then_inc(g_tanh, 1)
                hi(M_G + 3 * i + 4)

            def x1_ready(k):
                if k + 2 < KT:
                    hi(M_O + k + 2)
                act.wait_ge(x1_ok, k + 1)

            norm(3, ST_H2, KT, 2, lambda k: RA[:, k, :], x1_ready, eps1)
            for k in range(KT):
                act.wait_ge(mod_h, KT + k + 1)
                A(RB[:, k, :], RB[:, k, :], ACT.Identity, bias=mod[:, 24 + k:25 + k]).then_inc(h_ok, 1)
            for i in range(1, KT, 2):
                e = PE_H + i
                act.wait_ge(acc, e + 1)
                A(h2_hi[:, i // 2, T:D], bank(e)[:, :], ACT.Copy)
                A(h2_raw[:, i // 2, T:D], bank(e)[:, :], ACT.Copy).then_inc(ev[1], 1)
            act.wait_ge(sp1, 1)
            A(SB[:, 0, 32:52], SB[:, 0, 0:20], ACT.Exp).then_inc(sp2, 1)
            act.wait_ge(list_ok, 1)
            n_quads = act.value_load(nqi[0:1, 0:1], min_val=1, max_val=MAX_QUADS)
            act.sem_inc(x_ev, 1)
            act.sem_inc(z_ev, 2)
            act.sem_inc(ht_ev, 2)

            def gathered(b, q2):
                act.wait_ge(got, b + 3 + q2)
                for hf in range(2):
                    ins = A(Xs[:, b % 2, hf * T:(hf + 1) * T], ps[hf][:, :], ACT.Copy)
                ins.then_inc(xs_ev, 1)

            def turned_gathered(b, q2, q24):
                act.wait_ge(xt_done, b + 1 + q2)
                act.wait_ge(moe_used, PAIR_TILES * b + 8 + q24)
                A(Xg[:, b % 2, 0:4, :], quad(ps[0][:, :]), ACT.Copy)
                A(Xg[:, b % 2, 4:8, :], quad(ps[1][:, :]), ACT.Copy).then_inc(x_ev, 1)

            gathered(0, 0)
            turned_gathered(0, 0, 0)
            with act.Fori(0, n_quads) as q:
                def gate(b):
                    act.wait_ge(moe_used, PAIR_TILES * (b + 2) + 8 + q * (2 * PAIR_TILES))
                    A(sg[:, b, :], ps[2 + b][:, 0:256], ACT.Silu).then_inc(sg_done, 1)

                def turned_hidden(b):
                    act.wait_ge(ht_done, b + 3 + q * 2)
                    act.wait_ge(moe_used, PAIR_TILES * b + 12 + q * (2 * PAIR_TILES))
                    A(hidT[:, b, :, :], ps[2 + b][:, 0:256].rearrange("p (f s) -> p f s", f=2),
                      ACT.Copy)
                    A(slot_weight(b), ps[2 + b][:, 256:257], ACT.Copy).then_inc(ht_ev, 1)
                    act.wait_ge(ht_ev, b + 3 + q * 2)

                def downs(b):
                    act.wait_ge(y_full, 1 + q * KT)
                    act.wait_ge(dn_half, b + 1 + q * 2)
                    A(Zh[:, b, 0:T], ps[4][:, :], ACT.Copy, scale=slot_weight(b)).then_inc(z_hi, 1)
                    act.wait_ge(moe_used, PAIR_TILES * (b + 3) + q * (2 * PAIR_TILES))
                    A(Zh[:, b, T:D], ps[5][:, :], ACT.Copy, scale=slot_weight(b)).then_inc(z_hi, 1)

                def turned(b):
                    act.wait_ge(st_t, 3 + b + q * 2)
                    A(St[:, b, :], ps[6 + b][:, :], ACT.Copy).then_inc(st_ev, 1)

                gate(0)
                gathered(1, q * 2)
                turned(0)
                turned(1)
                turned_hidden(0)
                turned_gathered(1, q * 2, q * (2 * PAIR_TILES))
                downs(0)
                gate(1)
                gathered(2, q * 2)
                turned_hidden(1)
                turned_gathered(2, q * 2, q * (2 * PAIR_TILES))
                downs(1)
            hi(M_Q2)
            hi(M_Q2 + 1)
            norm(4, ST_F, KT, 2, lambda k: RA[:, k, :], lambda k: act.wait_ge(x1_ok, KT + k + 1), eps1)
            for k in range(KT):
                act.wait_ge(x2_ok, k + 1)
                A(RBr[:, k, :], RA[:, k, :], ACT.Copy).then_inc(x_hi, 1)
            for i in range(24):
                if i < 14:
                    hi(M_Q2 + i + 2)
                if i in (20, 21):
                    hi(M_XBC + i - 20)
                if i % 2:
                    evict(PE_Q2 + i, q2_dst(i))
            attend(2)
            attend(3)
            act.wait_ge(s_full, 4 * NU)
            for k in range(KT):
                A(RCr[:, k, :], RA[:, k, :], ACT.Copy).then_inc(x_hi, 1)
            act.wait_ge(pv_done, 4 * NU)
            for i in range(13):
                if i < 12:
                    hi(M_XBC + i + 2)
                    if i >= 2:
                        act.wait_ge(conv_ok, i - 1)
                    act.wait_ge(acc, PE_XBC + i + 1)
                    ins = A(convbuf[i % 2][:, 3:T + 3], bank(PE_XBC + i)[:, :], ACT.Copy)
                    ins.then_inc(ev[i % 2], 1)
                if i >= 1:
                    act.wait_ge(conv_ok, i)
                    tile = RG[:, i - 1, :] if i - 1 < 8 else RF[:, i - 9, :]
                    A(tile, tile, ACT.Silu).then_inc(xbc_ok, 1)
            act.wait_ge(sp1, 2)
            link(A(tmp_t[:, :, :], tmp_t[:, :, :], ACT.Exp))
            A(aneg, rows[:, R_ALOG:R_ALOG + 16], ACT.Exp)
            A(tmp_t[:, :, :], tmp_t[:, :, :], ACT.Ln, bias=ones[:, 0:1]).then_inc(sp2, 1)
            for i in range(8):
                if i % 2:
                    e = PE_XT + i
                    evict(e, ([(RCf[:, (i // 2) * D + T:(i // 2) * D + D], bank(e)[:, :])], 1.0))
            evict(PE_BT + 1, ([(b_tok[:, 1, :, :], quad(bank(PE_BT + 1)[:, :]))], 1.0))
            act.wait_ge(cs_ok, 1)
            A(sd_t[:, :, :], cs_t[:, :, :], ACT.Exp)
            A(dec_t[:, :, :], tot_t[:, :, :], ACT.Exp)
            A(dte_t[:, :, :], tmp_t[:, :, :], ACT.Exp).then_inc(sp2, 1)
            for c in range(TT):
                for q in range(4):
                    act.wait_ge(dd_ok, 4 * c + q + 1)
                    A(decay[:, 4 * q:4 * q + 4, :], decay[:, 4 * q:4 * q + 4, :], ACT.Exp).then_inc(ee_ok, 1)
                for k in Z_SPLIT[c]:
                    act.wait_ge(skip_ok, TT)
                    A(RCr[:, k, :], RA[:, k, :], ACT.Copy).then_inc(x_hi, 1)
            for i in range(8):
                if i % 2:
                    e = PE_YT + i
                    evict(e, ([(RH[:, 4:8, (i // 2) * P:(i // 2 + 1) * P], quad(bank(e)[:, :]))], 1.0))
            def mix_parts(dst, src, first):
                for k in range(KT):
                    act.wait_ge(mixn, first + k + 1)
                    A(dst[:, k, :], src[:, k, :], ACT.Copy).then_inc(x_hi, 1)

            for i in range(16):
                e = PE_ZA + i
                hi(M_Z + i + 2)
                if i >= 4:
                    act.wait_ge(mixp, i - 3)
                act.wait_ge(acc, e + 1)
                A(zbuf(i), bank(e)[:, :], ACT.Silu).then_inc(ev[e % 2], 1)
                if i == 12:
                    root(5, ST_AT, KT, 2, eps2)
                if i == 14:
                    mix_parts(RDr, RB, 0)
            root(6, ST_SS, KT, 3, eps2)
            mix_parts(RFr, RH, KT)
            for m in range(M_OUT + 2, M_OUT + 2 * KT):
                hi(m)
            norm(7, ST_VAR, KT, 5, lambda k: RC[:, k, :], lambda k: act.wait_ge(cen_ok, k + 1), eps2)

        @block.vector
        def _(dve):
            v = nc.vector
            links = [0]

            def link(ins):
                links[0] += 1
                ins.then_inc(dve_c, 1)
                dve.wait_ge(dve_c, links[0])

            def evict(e, what):
                pairs, scale = what
                dve.wait_ge(acc, e + 1)
                for dst, src in pairs:
                    ins = v.tensor_scalar(dst, src, scale, None, ALU.mult) if scale != 1.0 else v.tensor_copy(dst, src)
                ins.then_inc(ev[e % 2], 1)

            def lo(m):
                dve.wait_ge(w_hi, m + 1)
                v.tensor_tensor(remainder(m), arrival(m)[2], part(m).bitcast(F32), ALU.subtract).then_inc(w_split, 1)

            def reduce_ada(m):
                dve.wait_ge(*product(m))
                if m >= 2:
                    dve.wait_ge(ada_done, m - 1)
                v.tensor_reduce(ada_sum(m), prod(m).rearrange("p (k n) -> p n k", k=KT), AX_X, ALU.add).then_inc(red_ok, 1)

            def attend(g):
                def evict_pt(u):
                    n = g * NU + u
                    if n % 2:
                        return
                    w = (ORDER[UNITS[u][0]] + 1) * P
                    dve.wait_ge(pt_full, n + 1)
                    if n >= 2:
                        dve.wait_ge(pv_done, n - 1)
                    v.tensor_copy(PTB[:, 0, 0:w], ps[2][:, 0:w]).then_inc(pt_ready[0], 1)

                def normalise(o):
                    i = g * TT + o
                    dve.wait_ge(pv_done, HG * (i + 1))
                    r = rsinv[:, 0:HG]
                    link(v.reciprocal(r, rowsum[:, (i % 2) * HG:(i % 2) * HG + HG]))
                    if i >= 2:
                        gg, tt = (i - 2) // TT, (i - 2) % TT
                        dve.wait_ge(acc, ot_event(gg, tt) + 1)
                    v.tensor_tensor(OTK[:, i % 2, :].rearrange("p (h c) -> p h c", h=HG),
                                    ps[4 + i % 2][:, :].rearrange("p (h c) -> p h c", h=HG),
                                    r.unsqueeze(2).to_broadcast([P, HG, 64]), ALU.mult).then_inc(o_ready, 1)

                bias = group_ops(g)[3]
                for u in range(NU):
                    o, h = UNITS[u]
                    t = ORDER[o]
                    n = g * NU + u
                    w = (t + 1) * P
                    if g == 0 and u == 0:
                        dve.wait_ge(bias_ok, 1)
                    if g >= 2 and o == 0:
                        dve.wait_ge(bias_ok, 1 + (g - 2) * HG + h + 1)
                    dve.wait_ge(s_full, n + 1)
                    if n >= 2:
                        dve.wait_ge(p_ready, n - 1)
                    v.tensor_tensor_reduce(SB[:, n % 2, 0:w], ps[n % 2][:, 0:w], bias(h)[:, T - w:T], -1.0, 3e38,
                                           ALU.add, ALU.min, nmax(n)).then_inc(biased, 1)
                    if u >= 1:
                        evict_pt(u - 1)
                    if u % HG == 2 and u > HG:
                        normalise(u // HG - 1)
                    if u % HG == 5 and u > HG:
                        o_o = u // HG - 1
                        if ot_event(g, o_o) % 2 == 0:
                            evict(ot_event(g, o_o), ot_dst(g, o_o))
                evict_pt(NU - 1)
                normalise(TT - 1)
                if ot_event(g, TT - 1) % 2 == 0:
                    evict(ot_event(g, TT - 1), ot_dst(g, TT - 1))

            def angles(quarter, dst):
                posf, ang, turns, red = OTK[:, 1, :], SB[:, 0, :], SB[:, 1, :], PB[:, 0, :]
                if quarter == 0.0:
                    dve.wait_ge(pos_in, 16)
                    link(v.tensor_copy(posf, OTK[:, 0, :].bitcast(I32)))
                    link(v.tensor_scalar(ang, posf, V("inv"), None, ALU.mult))
                link(v.tensor_scalar(turns, ang, float(1 / TWO_PI), quarter, ALU.mult, ALU.add))
                link(v.tensor_scalar(turns, turns, ROUND, None, ALU.add))
                link(v.tensor_scalar(turns, turns, ROUND, None, ALU.subtract))
                link(v.scalar_tensor_tensor(red, turns, -C1, ang, ALU.mult, ALU.add))
                link(v.scalar_tensor_tensor(red, turns, -C2, red, ALU.mult, ALU.add))
                link(v.scalar_tensor_tensor(red, turns, -C3, red, ALU.mult, ALU.add))
                link(v.tensor_scalar(red, red, quarter * TWO_PI, 3.1415925, ALU.add, ALU.min))
                link(v.tensor_scalar(dst, red, -3.1415925, None, ALU.max))
                dve.sem_inc(ang_ok, 1)

            dve.wait_ge(c_in, 32)
            dve.wait_ge(cact_ok, 1)
            for m in range(17):
                if m in ADA_DVE:
                    multiply_ada(dve, v, m)
                if m:
                    reduce_ada(m - 1)
            dve.wait_ge(ada_done, 16)
            link(v.tensor_tensor(mod[:, 0:16], ps[0][:, 0:16], V("b_ada", 0, 16), ALU.add))
            link(v.scalar_tensor_tensor(A1, mod[:, 8:16], 1.0, V("g_mix", 0, 8), ALU.add, ALU.mult))
            dve.wait_ge(rinv_ok, 1)
            for k in range(KT + 3):
                if k < KT:
                    v.scalar_tensor_tensor(RB[:, k, :], RA[:, k, :], A1[:, k:k + 1], RINV[:, :], ALU.mult,
                                           ALU.mult).then_inc(mod_h, 1)
                if k == 2:
                    lo(0)
                if k >= 3:
                    dve.wait_ge(x_hi, k - 2)
                    v.tensor_tensor(REr[:, k - 3, :], RB[:, k - 3, :], RDr[:, k - 3, :].bitcast(F32),
                                    ALU.subtract).then_inc(h_lo, 1)
            dve.wait_ge(mod_h, KT)
            dve.sem_inc(rinv_used, 1)
            lo(1)
            for i in range(16):
                reduce_ada(16 + 2 * i)
                reduce_ada(17 + 2 * i)
                if i + 2 < M_G:
                    lo(i + 2)
                if i in (12, 13):
                    angles(0.25 * (i - 12), (sinT, cosT)[i - 12])
                if i % 2 == 0:
                    evict(PE_S1 + i, s1_dst(i))
                if i == 8:
                    dve.wait_ge(rinv_ok, 2)
                    dve.wait_ge(ev[1], 1)
                    for k in range(2):
                        v.scalar_tensor_tensor(qnT[:, k, :], qlT[:, k, :], V("g_q", k), RINV[:, :], ALU.mult,
                                               ALU.mult).then_inc(lat_n, 1)
                    dve.wait_ge(lat_n, 2)
                    dve.sem_inc(rinv_used, 1)
                if i == 10:
                    dve.wait_ge(rinv_ok, 3)
                    v.scalar_tensor_tensor(kvnT, kvT, V("g_kv"), RINV[:, :], ALU.mult, ALU.mult).then_inc(lat_n, 1)
                    dve.wait_ge(lat_n, 3)
                    dve.sem_inc(rinv_used, 1)
            dve.wait_ge(ada_done, 48)
            v.tensor_tensor(mod[:, 16:48], ps[1][:, 0:32], V("b_ada", 16, 32), ALU.add).then_inc(mod_ok, 2)
            dve.wait_ge(mod_ok, 2)
            link(v.scalar_tensor_tensor(A2, mod[:, 32:40], 1.0, V("g_ffn", 0, 8), ALU.add, ALU.mult))
            link(v.tensor_scalar(gt1h, mod[:, 16:24], 0.5, None, ALU.mult))
            dve.wait_ge(rope_ok, 1)
            dve.wait_ge(ev[1], 2)
            link(v.tensor_scalar(sinT, sinT, V("sign"), None, ALU.mult))
            dve.wait_ge(acc, PE_S1 + M_G)
            link(v.tensor_tensor(SB[0:32, 0, :], krT[0:32, :], cosT[0:32, :], ALU.mult))
            link(v.tensor_tensor(SB[0:32, 1, :], krT[32:64, :], sinT[32:64, :], ALU.mult))
            for h in range(8):
                r = 64 if h % 2 == 0 else 32
                ins = v.tensor_tensor(RE[r:r + 32, h, :], SB[0:32, 0, :], SB[0:32, 1, :], ALU.add)
            link(ins)
            for c in range(16):
                if c % 2 == 0:
                    evict(PE_U + c, u_dst(c))
                if c in (6, 8):
                    r = (c - 6) // 2
                    dve.wait_ge(ev[0], (PE_U + 4 + 2 * r) // 2 + 1)
                    dve.wait_ge(ev[1], (PE_U + 5 + 2 * r) // 2 + 1)
                    link(v.tensor_tensor(SB[:, 0, :], OTK[:, r, :], cosT, ALU.mult))
                    link(v.tensor_tensor(SB[:, 1, :], PTB[:, r, :], sinT, ALU.mult))
                    for h in range(4):
                        hh, o = 4 * r + h, 64 if h % 2 == 0 else 32
                        ins = v.tensor_tensor(RD[o:o + 32, hh, :], SB[32 * h:32 * h + 32, 0, :],
                                              SB[32 * h:32 * h + 32, 1, :], ALU.add)
                    link(ins)
            for h in range(HG):
                dve.wait_ge(flip_full, h + 1)
                v.tensor_copy(RG[:, h, :], ps[4 + h % 2][:, :]).then_inc(flip_ev, 1)
            lo(M_G)
            lo(M_G + 1)
            dve.wait_ge(zero_ok, 1)
            dve.sem_inc(lat_ok, 1)
            attend(0)
            attend(1)
            for k in range(KT):
                dve.wait_ge(oab_hi, k + 1)
                if k == 0:
                    dve.wait_ge(pv_done, 2 * NU)
                v.tensor_tensor(RFr[:, k, :], RH[:, k, :], REr[:, k, :].bitcast(F32), ALU.subtract).then_inc(oab_lo, 1)
            for i in range(KT):
                b = 4 * ((i + 1) % 2)
                for s in range(3):
                    lo(M_G + 3 * i + s + 2)
                dve.wait_ge(g_tanh, i + 1)
                dve.wait_ge(g_used, 3 * i + 3)
                link(v.scalar_tensor_tensor(SB[:, i % 2, :], SB[:, i % 2, :], 1.0, ps[b + 2][:, :], ALU.add, ALU.mult))
                link(v.scalar_tensor_tensor(PB[:, i % 2, :], PB[:, i % 2, :], 1.0, ps[b + 3][:, :], ALU.add, ALU.mult))
                link(v.tensor_tensor(SB[:, i % 2, :], SB[:, i % 2, :], PB[:, i % 2, :], ALU.add))
                if i == 0:
                    dve.wait_ge(oab_lo, KT)
                link(v.tensor_copy(RDr[:, i, :], SB[:, i % 2, :]))
                v.tensor_tensor(RHr[:, i, :], SB[:, i % 2, :], RDr[:, i, :].bitcast(F32),
                                ALU.subtract).then_inc(g_done, 1)
            for i in range(KT):
                e = PE_O + i
                if i + 2 < KT:
                    lo(M_O + i + 2)
                dve.wait_ge(acc, e + 1)
                v.scalar_tensor_tensor(RA[:, i, :], bank(e)[:, :], gt1h[:, i:i + 1], RA[:, i, :], ALU.mult,
                                       ALU.add).then_inc(x1_ok, 1)
                dve.wait_ge(x1_ok, i + 1)
                dve.sem_inc(ev[e % 2], 1)
            dve.wait_ge(rinv_ok, 4)
            dve.wait_ge(g_used, 24)
            for k in range(KT):
                v.scalar_tensor_tensor(RB[:, k, :], RA[:, k, :], A2[:, k:k + 1], RINV[:, :], ALU.mult,
                                       ALU.mult).then_inc(mod_h, 1)
            dve.wait_ge(mod_h, 2 * KT)
            dve.sem_inc(rinv_used, 1)
            def lane(a, n):
                return SB[:, 0, a:a + n]

            L = OTK[:, 1, 0:144].rearrange("p (t n) -> p t n", t=TT)
            dve.wait_ge(lg_raw, 1)
            v.tensor_copy(PTB[0:36, 0, :], ps[0][0:36, :]).then_inc(lg_sb, 1)
            dve.wait_ge(lg_full, 1)
            link(v.tensor_tensor(L, ps[1][:, 0:144].rearrange("p (t n) -> p t n", t=TT),
                                 rows[:, 0:36].unsqueeze(1).to_broadcast([P, TT, 36]), ALU.add))
            for i in range(8):
                if i % 2 == 0:
                    e = PE_H + i
                    evict(e, ([(h2_hi[:, i // 2, 0:T], bank(e)[:, :]), (h2_raw[:, i // 2, 0:T], bank(e)[:, :])], 1.0))
            R = SB[:, 1, :]

            def r3(a, n):
                return R[:, a:a + TT * n].rearrange("p (t n) -> p t n", t=TT)

            def first_max(src, n, top, oh):
                link(v.tensor_reduce(top, src, AX_X, ALU.max))
                c = r3(256, n)
                link(v.tensor_tensor(c, src, top.unsqueeze(2).to_broadcast([P, TT, n]), ALU.is_equal))
                link(v.scalar_tensor_tensor(c, c, -64.0, iota64[:, 0:n].unsqueeze(1).to_broadcast([P, TT, n]),
                                            ALU.mult, ALU.add))
                link(v.tensor_reduce(R[:, 384:388], c, AX_X, ALU.min))
                link(v.tensor_tensor(oh, c, R[:, 384:388].unsqueeze(2).to_broadcast([P, TT, n]), ALU.is_equal))

            gmax, top1, top2 = lane(60, 4), lane(64, 4), lane(68, 4)
            goh = r3(400, 4)
            first_max(L[:, :, 0:4], 4, gmax, goh)
            link(v.tensor_scalar(goh, goh, 1e30, -1e30, ALU.mult, ALU.add))
            el = r3(0, 32)
            for t in range(TT):
                ins = v.tensor_tensor(el[:, t, :].rearrange("p (g e) -> p g e", g=4),
                                      L[:, t, 4:36].rearrange("p (g e) -> p g e", g=4),
                                      goh[:, t, :].unsqueeze(2).to_broadcast([P, 4, 8]), ALU.add)
            link(ins)
            oh1, oh2 = r3(128, 32), OTK[:, 1, 256:384].rearrange("p (t n) -> p t n", t=TT)
            first_max(el, 32, top1, oh1)
            link(v.scalar_tensor_tensor(el, oh1, -3e30, el, ALU.mult, ALU.add))
            first_max(el, 32, top2, oh2)
            link(v.tensor_tensor(lane(0, 16).rearrange("p (t n) -> p t n", t=TT), L[:, :, 0:4],
                                 gmax.unsqueeze(2).to_broadcast([P, TT, 4]), ALU.subtract))
            v.tensor_tensor(lane(16, 4), top2, top1, ALU.subtract).then_inc(sp1, 1)
            link(v.tensor_tensor(chosen, oh1, oh2, ALU.add))
            dve.sem_inc(mask_ok, 1)
            dve.wait_ge(sp2, 1)
            gsum, w1, w2 = lane(72, 4), lane(76, 4), lane(80, 4)
            link(v.tensor_reduce(gsum, lane(32, 16).rearrange("p (t n) -> p t n", t=TT), AX_X, ALU.add))
            link(v.tensor_scalar(w1, lane(48, 4), 1.0, None, ALU.add))
            link(v.tensor_tensor(w1, w1, gsum, ALU.mult))
            link(v.reciprocal(w1, w1))
            link(v.tensor_tensor(w2, w1, lane(48, 4), ALU.mult))
            link(v.tensor_tensor(oh1, oh1, w1.unsqueeze(2).to_broadcast([P, TT, 32]), ALU.mult))
            link(v.tensor_tensor(oh2, oh2, w2.unsqueeze(2).to_broadcast([P, TT, 32]), ALU.mult))
            dve.wait_ge(pv_done, 2 * NU)

            def et(ap, p=0):
                return ap[:, p * P:(p + 1) * P].rearrange("p (e t) -> p t e", t=TT)

            link(v.tensor_tensor(et(combr), oh1, oh2, ALU.add))
            dve.wait_ge(pos_full, 1)
            link(v.tensor_tensor(el, ps[3][:, 0:128].rearrange("p (t n) -> p t n", t=TT), chosen, ALU.mult))
            for p in range(MAXPASS):
                ins = v.tensor_scalar(et(posm, p), el, -1.0 - p * SLOTS, None, ALU.add)
            v.memset(posm[:, MAXPASS * P:(MAXPASS * N_EXP + 1) * TT], -1.0)
            link(ins)
            dve.sem_inc(route_ok, 1)
            dve.wait_ge(cnt_full, 1)
            dve.wait_ge(sel_ok, 1)
            link(v.tensor_scalar(sel[:, 6:8], sel[:, 4:6], ps[4][:, 0:1], None, ALU.is_lt))
            dve.sem_inc(flag_ok, 1)
            dve.wait_ge(rank_full, 1)
            link(v.tensor_tensor(cnt[:, 0:2], ps[5][:, 0:2], sel[:, 6:8], ALU.mult))
            link(v.tensor_scalar(cnt[:, 0:2], cnt[:, 0:2], 1.0, None, ALU.subtract))
            for hf in range(2):
                ins = v.tensor_scalar(ranked[:, hf, :], iota64[:, :], cnt[:, hf:hf + 1], None, ALU.is_equal)
            link(ins)
            link(v.tensor_scalar(cnt[:, 2:3], ps[5][:, 2:3], 0.25, 0.75 - 0.5 + 0.125, ALU.mult, ALU.add))
            dve.sem_inc(rank_ok, 1)
            link(v.tensor_copy(nqi[0:1, 0:1], cnt[0:1, 2:3]))
            dve.wait_ge(list_full, 1)
            link(v.tensor_scalar(units[0:1, 0, :], ps[5][0:1, 64:128], float(MAXPASS * N_EXP), None, ALU.add))
            link(v.tensor_copy(units[0:1, 1, :], ps[5][0:1, 128:192]))
            dve.sem_inc(list_ok, 1)
            n_quads = dve.value_load(nqi[0:1, 0:1], min_val=1, max_val=MAX_QUADS)
            dve.wait_ge(y0_ok, 1)
            dve.sem_inc(y_ev, 2)

            def one_hot(b, q2):
                dve.wait_ge(st_t, b + 1 + q2)
                if b:
                    dve.wait_ge(ohw_ready, b + q2)
                for u in range(2):
                    at = units[0:1, 0, bass.ds(q2 * 2 + 2 * b + u, 1)] if b else units[0:1, 0, u:u + 1]
                    block_no = dve.value_load(at, min_val=0, max_val=MAXPASS * N_EXP)
                    ins = v.tensor_tensor(OHr[:, b % 2, :, u * SLOTS:(u + 1) * SLOTS],
                                          iota64[:, :].unsqueeze(1).to_broadcast([P, TT, SLOTS]),
                                          posm[:, bass.ds(block_no * TT, TT)].unsqueeze(2).to_broadcast([P, TT, SLOTS]),
                                          ALU.is_equal)
                ins.then_inc(oh_ready, 1)

            one_hot(0, 0)
            with dve.Fori(0, n_quads) as q:
                def hidden(b):
                    dve.wait_ge(sg_done, b + 1 + q * 2)
                    dve.wait_ge(ht_done, b + 1 + q * 2)
                    v.tensor_tensor(hid[:, b, :], sg[:, b, :], ps[2 + b][:, 256:512], ALU.mult).then_inc(hid_done, 1)

                def downs_rest(b):
                    for hf in range(2):
                        dve.wait_ge(z_hi, 2 * b + hf + 1 + q * 4)
                        half_d = slice(hf * T, (hf + 1) * T)
                        v.scalar_tensor_tensor(Zl[:, b, half_d], ps[4 + hf][:, :], slot_weight(b),
                                               Zh[:, b, half_d].bitcast(F32), ALU.mult, ALU.subtract).then_inc(z_ev, 1)

                one_hot(1, q * 2)
                hidden(0)
                one_hot(2, q * 2)
                downs_rest(0)
                hidden(1)
                downs_rest(1)
                for n in range(KT):
                    dve.wait_ge(y_full, n + 2 + q * KT)
                    v.tensor_tensor(RD[:, n, :], RD[:, n, :], ps[6 + n % 2][:, :], ALU.add).then_inc(y_ev, 1)
                dve.wait_ge(y_ev, KT + 2 + q * KT)
            lo(M_Q2)
            for k in range(KT):
                v.scalar_tensor_tensor(RA[:, k, :], RD[:, k, :], mod[:, 40 + k:41 + k], RA[:, k, :], ALU.mult,
                                       ALU.add).then_inc(x1_ok, 1)
            dve.wait_ge(x1_ok, 2 * KT)
            dve.wait_ge(rinv_ok, 5)
            for k in range(KT):
                v.scalar_tensor_tensor(RA[:, k, :], RA[:, k, :], V("g_final", k), RINV[:, :], ALU.mult,
                                       ALU.mult).then_inc(x2_ok, 1)
            dve.wait_ge(x2_ok, KT)
            dve.sem_inc(rinv_used, 1)
            lo(M_Q2 + 1)
            di = OTK[:, 0, :].bitcast(I32)
            dj = OTK[:, 1, :].bitcast(I32)
            df = RH[:, 2, :]

            def multiples(m, mask):
                link(v.tensor_scalar(dj, di, mask, None, ALU.bitwise_and))
                link(v.tensor_copy(df, dj))
                link(v.tensor_scalar(RH[:, 3 + m, :], df, 0.0, None, ALU.is_equal))

            def reached():
                link(v.tensor_scalar(lnm, delta, 128.0, None, ALU.is_le))
                link(v.tensor_tensor(lnm, lnm, RH[:, 3, :], ALU.add))
                link(v.tensor_tensor(lnm, lnm, RH[:, 4, :], ALU.add))
                link(v.tensor_scalar(df, delta, 0.0, None, ALU.is_ge))
                link(v.tensor_tensor(df, df, lnm, ALU.mult))

            def logarithm():
                link(v.tensor_scalar(lnm, df, 0.0, NEG, ALU.is_equal, ALU.mult))
                link(v.tensor_scalar(RH[:, 3, :], df, 2.0, float(np.log(2.0)), ALU.is_equal, ALU.mult))
                link(v.tensor_scalar(RH[:, 4, :], df, 3.0, float(np.log(3.0)), ALU.is_equal, ALU.mult))
                link(v.tensor_tensor(lnm, lnm, RH[:, 3, :], ALU.add))
                link(v.tensor_tensor(lnm, lnm, RH[:, 4, :], ALU.add))
                dve.sem_inc(lnm_ok, 1)

            for i in range(24):
                if i < 14:
                    lo(M_Q2 + i + 2)
                if i == 2:
                    dve.wait_ge(delta_ok, 1)
                    multiples(0, 3)
                if i == 3:
                    multiples(1, 15)
                if i == 4:
                    reached()
                if i == 5:
                    logarithm()
                if i in (20, 21):
                    lo(M_XBC + i - 20)
                if i % 2 == 0:
                    evict(PE_Q2 + i, q2_dst(i))
            attend(2)
            attend(3)
            dve.wait_ge(pv_done, 4 * NU)
            link(v.memset(convbuf[0][:, 0:3], 0.0))
            link(v.memset(convbuf[1][:, 0:3], 0.0))
            for i in range(12):
                buf = convbuf[i % 2]
                lo(M_XBC + i + 2)
                tile = RG[:, i, :] if i < 8 else RF[:, i - 8, :]
                dve.wait_ge(ev[i % 2], PE_XBC // 2 + i // 2 + 1)
                link(v.tensor_scalar(tile, buf[:, 0:T], V("conv_w", 4 * i), V("conv_b", i), ALU.mult, ALU.add))
                for w in range(1, 4):
                    ins = v.scalar_tensor_tensor(tile, buf[:, w:w + T], V("conv_w", 4 * i + w), tile, ALU.mult, ALU.add)
                    if w < 3:
                        link(ins)
                ins.then_inc(conv_ok, 1)
            dve.wait_ge(dt_full, 1)
            link(v.tensor_tensor(dt_t, ps[0][:, 0:64].rearrange("p (t h) -> p t h", t=TT),
                                 rows[:, R_DTB:R_DTB + 16].unsqueeze(1).to_broadcast([P, TT, 16]), ALU.add))
            link(v.scalar_tensor_tensor(tmp_t, dt_t, -1.0, dt_t, ALU.mult, ALU.min))
            link(v.tensor_scalar(dt_t, dt_t, 0.0, None, ALU.max))
            dve.sem_inc(sp1, 1)
            dve.wait_ge(sp2, 2)
            link(v.tensor_tensor(dt_t, dt_t, tmp_t, ALU.add))
            link(v.scalar_tensor_tensor(adt_t, dt_t, -1.0, aneg.unsqueeze(1).to_broadcast([P, TT, 16]), ALU.mult,
                                        ALU.mult))
            dve.sem_inc(adt_ok, 1)
            for i in range(8):
                if i % 2 == 0:
                    e = PE_XT + i
                    evict(e, ([(RCf[:, (i // 2) * D:(i // 2) * D + T], bank(e)[:, :])], 1.0))
            evict(PE_BT, ([(b_tok[:, 0, :, :], quad(bank(PE_BT)[:, :]))], 1.0))
            dve.wait_ge(cs_full, 1)
            link(v.tensor_copy(cs_t, ps[1][:, 0:64].rearrange("p (t h) -> p t h", t=TT)))
            link(v.tensor_copy(tot_t, ps[1][:, 64:128].rearrange("p (t h) -> p t h", t=TT)))
            link(v.tensor_tensor(tmp_t, tot_t, cs_t, ALU.subtract))
            dve.sem_inc(cs_ok, 1)
            dve.wait_ge(sp2, 3)

            def heads(ap, o=0, n=8):
                return ap[:, o:o + n].unsqueeze(2).to_broadcast([P, n, 64])

            def h8(ap):
                return ap.rearrange("p (h c) -> p h c", h=8)

            for c in range(TT):
                dve.wait_ge(cb_full, c + 1)
                if c > 0:
                    dve.wait_ge(mm_ok, 4 * c)
                v.tensor_tensor(cbm, ps[0][:, 0:256].rearrange("p (g l) -> p g l", g=2),
                                upper[:, :].unsqueeze(1).to_broadcast([P, 2, P]), ALU.mult).then_inc(cb_ok, 1)
                if c > 0:
                    dve.wait_ge(yd_full, c)
                for q in range(4):
                    dve.wait_ge(csb_full, 4 * c + q + 1)
                    for h in range(4):
                        ins = v.tensor_scalar(decay[:, 4 * q + h, :], ps[2 + q % 2][:, h * P:(h + 1) * P],
                                              cs_t[:, c, 4 * q + h:4 * q + h + 1], 0.0, ALU.subtract, ALU.min)
                    ins.then_inc(dd_ok, 1)
                dve.wait_ge(skip_ok, c + 1)
                dve.wait_ge(yd_full, c + 1)
                for g in range(2):
                    yt = y_tokT[:, c, 8 * g:8 * g + 8, :]
                    ins = v.tensor_tensor(yt, yt, h8(ps[4 + g][:, :]), ALU.add)
                link(ins)
                if c > 0:
                    dve.wait_ge(yo_full, c)
                    for g in range(2):
                        ins = v.tensor_tensor(y_off[:, 8 * g:8 * g + 8, :], h8(ps[g][:, :]),
                                              heads(sd_t[:, c, :], 8 * g), ALU.mult)
                    link(ins)
                    link(v.tensor_tensor(y_tokT[:, c, :, :], y_tokT[:, c, :, :], y_off, ALU.add))
                dve.sem_inc(y_tok, 1)
                if c < TT - 1:
                    dve.wait_ge(st_full, c + 1)
                    for g in range(2):
                        sv = h8(state[:, g, :])
                        if c == 0:
                            ins = v.tensor_copy(sv, h8(ps[6 + g][:, :]))
                        else:
                            link(v.tensor_tensor(sv, sv, heads(dec_t[:, c, :], 8 * g), ALU.mult))
                            ins = v.tensor_tensor(sv, sv, h8(ps[6 + g][:, :]), ALU.add)
                    link(ins)
                    dve.sem_inc(state_ok, 1)
            for i in range(8):
                if i % 2 == 0:
                    e = PE_YT + i
                    evict(e, ([(RH[:, 0:4, (i // 2) * P:(i // 2 + 1) * P], quad(bank(e)[:, :]))], 1.0))
            def mix_square(i):
                at = ST_AT + i
                dve.wait_ge(mixp, i + 1)
                dve.wait_ge(sq_used, at - 1)
                tile = RB[:, i, :] if i < KT else RH[:, i - KT, :]
                v.tensor_tensor(SQ[:, at % 2, :], tile, tile, ALU.mult).then_inc(sq_ready, 1)

            def mix_norm(idx, reg, gain):
                dve.wait_ge(rinv_ok, idx)
                for k in range(KT):
                    v.scalar_tensor_tensor(reg[:, k, :], reg[:, k, :], V(gain, k), RINV[:, :], ALU.mult,
                                           ALU.mult).then_inc(mixn, 1)
                dve.wait_ge(mixn, KT * (idx - 5))
                dve.sem_inc(rinv_used, 1)

            for i in range(16):
                lo(M_Z + i + 2)
                if i:
                    mix_square(i - 1)
                if i == 13:
                    mix_norm(6, RB, "att_g")
            mix_square(15)
            mix_norm(7, RH, "ssm_g")
            for i in range(KT):
                e = PE_OUT + i
                if i + 1 < KT:
                    lo(M_OUT + 2 * i + 2)
                    lo(M_OUT + 2 * i + 3)
                dve.wait_ge(acc, e + 1)
                v.scalar_tensor_tensor(RA[:, i, :], RA[:, i, :], ALPHA, bank(e)[:, :], ALU.mult,
                                       ALU.add).then_inc(r_ok, 1)
                dve.wait_ge(r_ok, i + 1)
                dve.sem_inc(ev[e % 2], 1)
            dve.wait_ge(mu_full, 1)
            for k in range(KT):
                v.scalar_tensor_tensor(RC[:, k, :], ps[4][:, :], -1.0 / D, RA[:, k, :], ALU.mult,
                                       ALU.add).then_inc(cen_ok, 1)
            dve.wait_ge(cen_ok, KT)
            dve.wait_ge(rinv_ok, 8)
            for k in range(KT):
                link(v.scalar_tensor_tensor(RC[:, k, :], RC[:, k, :], V("ln_g", k), RINV[:, :], ALU.mult, ALU.mult))
                v.tensor_scalar(RC[:, k, :], RC[:, k, :], V("ln_b", k), None, ALU.add).then_inc(fin_ok, 1)

        @block.gpsimd
        def _(pool):
            g = nc.gpsimd
            links = [0]

            def link(ins):
                links[0] += 1
                ins.then_inc(pool_c, 1)
                pool.wait_ge(pool_c, links[0])

            link(g.memset(ones[:, :], 1.0))
            link(g.memset(ident[:, :], 0.0))
            g.memset(eps1, EPS1)
            g.memset(eps2, EPS2)
            link(g.affine_select(out=ident[:, :], in_=ident[:, :], compare_op=ALU.not_equal, fill=1.0, base=0,
                                 pattern=[[-1, P]], channel_multiplier=1))
            link(g.affine_select(out=upper[:, :], in_=ones[:, :], compare_op=ALU.is_ge, fill=0.0, base=0,
                                 pattern=[[1, P]], channel_multiplier=-1))
            g.memset(flip[:, :], 0.0).then_inc(flip_ev, 1)
            pool.wait_ge(flip_ev, 1)
            link(g.affine_select(out=flip[:, :], in_=flip[:, :], compare_op=ALU.not_equal, fill=1.0, base=1 - P,
                                 pattern=[[1, P]], channel_multiplier=1))
            pool.sem_inc(consts, 1)
            g.iota(iota64[:, :], [[1, SLOTS]], base=0, channel_multiplier=0, allow_small_or_imprecise_dtypes=True)
            for hf in range(2):
                link(g.iota(sel[:, hf:hf + 1], [[0, 1]], base=hf * P - MAXPASS * N_EXP, channel_multiplier=1,
                            allow_small_or_imprecise_dtypes=True))
                for r in range(4):
                    link(g.iota(sel[32 * r:32 * r + 32, 2 + hf:3 + hf], [[0, 1]], base=0, channel_multiplier=1,
                                allow_small_or_imprecise_dtypes=True))
                    link(g.memset(sel[32 * r:32 * r + 32, 4 + hf:5 + hf], float((4 * hf + r) * SLOTS)))
            pool.sem_inc(sel_ok, 1)
            pool.wait_ge(rev_in, 16)
            g.tensor_copy(ext_row[:, 0:255], ext_row[:, 255:256].to_broadcast([HG, 255])).then_inc(ext_ok, 1)
            link(g.memset(MASK[:, :], 0.0))
            g.memset(MASK[0:64, 448:512], NEG)
            pool.wait_ge(cact_ok, 1)
            for m in range(N_ADA):
                if m not in ADA_DVE:
                    multiply_ada(pool, g, m)
            pool.wait_ge(prod_ok, N_ADA - len(ADA_DVE))
            pool.wait_ge(acc, PE_S1 + M_G)
            g.memset(RD[96:128, 0:8:2, :], 0.0)
            g.memset(RD[0:32, 1:8:2, :], 0.0)
            g.memset(RE[96:128, 0:8:2, :], 0.0)
            link(g.memset(RE[0:32, 1:8:2, :], 0.0))
            pool.sem_inc(zero_ok, 1)
            pool.wait_ge(flip_ev, HG + 1)
            g.memset(RG[0:64, :, 448:512], NEG).then_inc(bias_ok, 1)
            pool.wait_ge(biased, NU)
            pool.wait_ge(s_full, NU)
            for k in range(KT):
                link(g.tensor_copy(RGr[:, k, :], RB[:, k, :]))
                g.tensor_tensor(RCr[:, k, :], RB[:, k, :], RGr[:, k, :].bitcast(F32), ALU.subtract).then_inc(x_lo, 1)
            pool.wait_ge(acc, PE_O + KT)
            link(g.memset(RD[:, :, :], 0.0))
            pool.sem_inc(y0_ok, 1)
            for i in range(KT):
                pool.wait_ge(ev[i % 2], (PE_H + i) // 2 + 1)
                at = slice(i % 2 * T, i % 2 * T + T)
                g.tensor_tensor(h2_lo[:, i // 2, at], h2_raw[:, i // 2, at], h2_hi[:, i // 2, at].bitcast(F32),
                                ALU.subtract).then_inc(h2t_ok, 1)
            pool.wait_ge(route_ok, 1)
            pool.wait_ge(list_ok, 1)
            n_quads = pool.value_load(nqi[0:1, 0:1], min_val=1, max_val=MAX_QUADS)
            pool.sem_inc(ohw_ready, 1)
            with pool.Fori(0, n_quads) as q:
                for b in range(2):
                    pool.wait_ge(ht_done, b + 1 + q * 2)
                    pool.wait_ge(oh_ready, b + 1 + q * 2)
                    for u in range(2):
                        e = pool.value_load(units[0:1, 1, bass.ds(q * 4 + 2 * b + u, 1)], min_val=0, max_val=N_EXP - 1)
                        ins = g.tensor_tensor(OHW[:, b, :, u * SLOTS:(u + 1) * SLOTS],
                                              OH[:, b, :, u * SLOTS:(u + 1) * SLOTS],
                                              combr[:, bass.ds(e * TT, TT)].unsqueeze(2).to_broadcast([P, TT, SLOTS]),
                                              ALU.mult)
                    ins.then_inc(pool_w, 1)
                    for t in range(1, TT):
                        pool.wait_ge(pool_w, TT * b + t + q * (2 * TT))
                        g.tensor_tensor(OHW[:, b, 0, :], OHW[:, b, 0, :], OHW[:, b, t, :],
                                        ALU.add).then_inc(pool_w if t < TT - 1 else ohw_ready, 1)
                    pool.wait_ge(ohw_ready, b + 2 + q * 2)
                    pool.sem_inc(pool_w, 1)
            def remainders(dst, hi_r, src, first, ks):
                for k in ks:
                    pool.wait_ge(x_hi, first + k + 1)
                    g.tensor_tensor(dst[:, k, :], src[:, k, :], hi_r[:, k, :].bitcast(F32), ALU.subtract).then_inc(x_lo, 1)

            remainders(RFr, RBr, RA, 8, range(KT))
            g.iota(delta, [[-1, T]], base=T - P, channel_multiplier=1, allow_small_or_imprecise_dtypes=True)
            g.iota(OTK[:, 0, :].bitcast(I32), [[-1, T]], base=2 * T - P, channel_multiplier=1).then_inc(delta_ok, 1)
            pool.wait_ge(lnm_ok, 1)
            for h in range(2 * HG):
                if h >= HG:
                    pool.wait_ge(biased, 2 * NU + 24 + h - HG + 1)
                link(g.tensor_scalar(RG[:, h % HG, :], delta, -float(2.0 ** (-8.0 * (h + 1) / 16)), None, ALU.mult))
                g.tensor_tensor(RG[:, h % HG, :], RG[:, h % HG, :], lnm, ALU.add).then_inc(bias_ok, 1)
            pool.wait_ge(s_full, 4 * NU)
            remainders(RDr, RCr, RA, 16, range(KT))
            for t in range(TT):
                pool.wait_ge(ev[0], (PE_XT + 2 * t) // 2 + 1)
                pool.wait_ge(ev[1], (PE_XT + 2 * t) // 2 + 1)
                pool.wait_ge(adt_ok, 1)
                g.tensor_tensor(xg_tok[:, t, :, :], xs_tok[:, t, :, :],
                                dt_t[:, t, :].unsqueeze(2).to_broadcast([P, SSM_H, SSM_P]), ALU.mult).then_inc(xg_ok, 1)
                g.tensor_tensor(y_tokT[:, t, :, :], xs_tok[:, t, :, :],
                                rows[:, R_DSKIP:R_DSKIP + 16].unsqueeze(2).to_broadcast([P, SSM_H, SSM_P]),
                                ALU.mult).then_inc(skip_ok, 1)
            pool.wait_ge(xg_ok, TT)
            pool.wait_ge(sp2, 3)
            for c in range(TT):
                if c < TT - 1:
                    if c > 0:
                        pool.wait_ge(st_full, c)
                    g.tensor_tensor(xgd, xg_tok[:, c, :, :],
                                    dte_t[:, c, :].unsqueeze(2).to_broadcast([P, SSM_H, SSM_P]),
                                    ALU.mult).then_inc(xgd_ok, 1)
                pool.wait_ge(cb_ok, c + 1)
                for q in range(4):
                    pool.wait_ge(ee_ok, 4 * c + q + 1)
                    g.tensor_tensor(decay[:, 4 * q:4 * q + 4, :], decay[:, 4 * q:4 * q + 4, :],
                                    cbm[:, q // 2, :].unsqueeze(1).to_broadcast([P, 4, P]), ALU.mult).then_inc(mm_ok, 1)
                remainders(RGr, RCr, RA, 24, Z_SPLIT[c])
            pool.wait_ge(ev[0], PE_ZA // 2)
            pool.wait_ge(ev[1], PE_ZA // 2)
            for i in range(16):
                e = PE_ZA + i
                tile = RB[:, i, :] if i < KT else RH[:, i - KT, :]
                pool.wait_ge(ev[e % 2], e // 2 + 1)
                g.tensor_tensor(tile, tile, zbuf(i), ALU.mult).then_inc(mixp, 1)
            remainders(REr, RDr, RB, 32, range(KT))
            remainders(RCr, RFr, RH, 40, range(KT))


def _tiles(w):
    m = w.shape[1] // P
    return w.reshape(KT, P, m, P).transpose(2, 1, 0, 3).reshape(m, P, D)


def _cols(v):
    return v.reshape(-1, P).T


def kernel(**inputs):
    import concourse.bacc as bacc
    from concourse.bass_utils import run_bass_kernel_spmd as run

    a = {k: np.ascontiguousarray(v) for k, v in inputs.items()}
    w_in = a["w_in"][0]
    swap = np.r_[16:32, 0:16]
    kr = 384 + np.arange(32)
    kr_cols = np.r_[kr, kr[swap], kr, kr[swap]]
    s1 = _tiles(np.concatenate([w_in[:, 0:384], w_in[:, kr_cols], w_in[:, 416:1952]], 1))
    ada = _tiles(a["w_ada"][0])
    uq = a["w_uq"][0]
    head = np.arange(8)[:, None] * 96
    nope = (head + np.arange(64)).reshape(4, P)
    rope_a = (head + 64 + np.arange(32)).reshape(2, P)
    rope_b = (head + 64 + swap).reshape(2, P)
    uq_cols = np.concatenate([nope, rope_a[0:1], rope_b[0:1], rope_a[1:2], rope_b[1:2]]).reshape(-1)
    uq_t = uq[:, uq_cols].reshape(2, P, 2, 4, P).transpose(2, 1, 3, 0, 4).reshape(2, P, D)
    ukv = np.concatenate([a["w_uk"][0], a["w_uv"][0]], 1)[None]
    ga, gb = _tiles(w_in[:, 1952:2976]), _tiles(w_in[:, 2976:4000])
    oab = _tiles(np.concatenate([a["w_oa"][0], a["w_ob"][0]], 0))
    first = [ada[0:16]]
    for i in range(16):
        first += [s1[i:i + 1], ada[16 + 2 * i:18 + 2 * i]]
    first += [uq_t, ukv]
    for i in range(KT):
        first += [ga[i:i + 1], gb[i:i + 1], oab[i:i + 1]]
    first += [_tiles(a["w_out"][0])]
    pre = np.concatenate(first, 0)
    gu = np.concatenate([a["w_gate"][0], a["w_up"][0]], 2).reshape(N_EXP, 4, 2, P, T).transpose(0, 1, 3, 2, 4)
    moe = np.concatenate([gu.reshape(N_EXP, 4, P, D), a["w_down"][0].reshape(N_EXP, 2, P, D)], 1)
    moe = moe.reshape(-1, P, D)
    w2 = a["w_in_2"][0]
    out2 = a["w_out_2"][0]
    pair = np.stack([_tiles(out2[0:D]), _tiles(out2[D:2 * D])], 1).reshape(-1, P, D)
    post = np.concatenate([_tiles(w2[:, 0:3072]), _tiles(w2[:, 5120:6656]), _tiles(w2[:, 3072:5120]), pair], 0)
    w_rt = np.concatenate([a["w_rg"][0], a["w_re"][0]], 1).reshape(KT, P, 36).transpose(1, 0, 2)
    w_dt = w2[:, 6656:6672].reshape(KT, P, 16).transpose(1, 0, 2)
    inv = (10000.0 ** (-np.arange(16, dtype=np.float32) / np.float32(16))).astype(np.float32)
    parts = {"c": _cols(a["c"][0]), "b_ada": _cols(a["b_ada"][0]), "g_mix": _cols(a["g_mix"][0]),
             "g_ffn": _cols(a["g_ffn"][0]), "g_final": _cols(a["g_final"]), "g_q": _cols(a["g_q"][0]),
             "g_kv": _cols(a["g_kv"][0]),
             "conv_w": a["conv_w_2"][0].reshape(4, 12, P).transpose(2, 1, 0).reshape(P, 48),
             "conv_b": _cols(a["conv_b_2"][0]), "att_g": _cols(a["att_norm_g_2"][0]),
             "ssm_g": _cols(a["ssm_norm_g_2"][0]), "ln_g": _cols(a["ln_g_2"][0]), "ln_b": _cols(a["ln_b_2"][0]),
             "inv": np.tile(inv, 8)[:, None], "sign": np.tile(np.repeat(np.float32([-1, 1]), 16), 4)[:, None]}
    vec = np.concatenate([parts[n] for n, _ in V_NAMES], 1)
    rows = np.concatenate([a["b_rg"][0], a["b_re"][0], a["dt_bias_2"][0], a["a_log_2"][0], a["d_skip_2"][0]])
    rel = a["rel_bias"][0][:, ::-1]
    arrays = {"xT": a["x"][0].T, "vec": vec, "rows": rows, "pos": a["positions"][0], "rel": rel, "w_rt": w_rt,
              "w_dt": w_dt, "w_pre": pre, "w_moe": moe, "w_post": post}
    nc = bacc.Bacc("TRN2", target_bir_lowering=False, num_devices=1)
    args = []
    for name in arrays:
        arrays[name] = np.ascontiguousarray(arrays[name])
        args.append(nc.dram_tensor(f"in_{name}", arrays[name].shape, mybir.dt.from_np(arrays[name].dtype),
                                   kind="ExternalInput").ap())
    args.append(nc.dram_tensor("outT", (D, T), F32, kind="ExternalOutput").ap())
    build(nc, *args)
    r = run(nc, [{f"in_{n}": v for n, v in arrays.items()}], core_ids=[0])
    return np.ascontiguousarray(r.results[0]["outT"].T)[None]
```
